# Optimizing a Trainium2 kernel written in Bass

```python
import math
import jax, jax.numpy as jnp
from jax import lax
import numpy as np

D_MODEL = 1024
BATCH = 1
SEQ = 1024
DEPTH = 1
DEC_BATCH = 1
DEC_SEQ = 256
PAST_LEN = 128

N_ATT_HEADS = 4
ATT_HEAD_DIM = 64
ATT_V_DIM = 2 * ATT_HEAD_DIM
ROT_DIM = ATT_HEAD_DIM // 4
ROPE_THETA = 500000.0
Q_BLOCK = 128
ATT_QK_W = N_ATT_HEADS * 2 * ATT_HEAD_DIM
ATT_V_W = N_ATT_HEADS * ATT_V_DIM
HY_WIDTH = 512
FILTER_EMB = 33
FILTER_HIDDEN = 64
DECAY_TARGET = 1e-2
FAST_DECAY_PCT = 0.3
SLOW_DECAY_PCT = 1.5
N_BRANCH = 2
IN_W = 2 * ATT_QK_W + ATT_V_W + 3 * HY_WIDTH + N_BRANCH * D_MODEL
N_MEM = 256
X_HEADS = 4
X_HEAD_DIM = D_MODEL // X_HEADS
N_EXPERTS = 16
EC_CAPACITY_FACTOR = 2
EXPERT_FF = 1024
EPS = 1e-6

kernel_name = "hybrid_diffattn_hyena_ec_encoder"

F32 = jnp.float32

def rmsnorm(x, g):
    xf = x.astype(F32)
    y = xf * lax.rsqrt(jnp.mean(xf * xf, axis=-1, keepdims=True) + EPS)
    return (y * g.astype(F32)).astype(x.dtype)

def rope_partial(t, pos):
    inv = ROPE_THETA ** (-jnp.arange(0, ROT_DIM, 2, dtype=F32) / ROT_DIM)
    ang = pos[:, None] * inv[None, :]
    cos = jnp.cos(ang)[:, None, None, :]
    sin = jnp.sin(ang)[:, None, None, :]
    tr = t[..., :ROT_DIM].astype(F32)
    t1, t2 = tr[..., :ROT_DIM // 2], tr[..., ROT_DIM // 2:]
    rot = jnp.concatenate([t1 * cos - t2 * sin, t1 * sin + t2 * cos], axis=-1)
    return jnp.concatenate([rot.astype(t.dtype), t[..., ROT_DIM:]], axis=-1)

def diff_attention(q, k, v, lam):
    B, L, H, _, dh = q.shape
    nb = L // Q_BLOCK
    qb = q.reshape(B, nb, Q_BLOCK, H, 2, dh).transpose(1, 0, 2, 3, 4, 5)
    scale = dh ** -0.5

    def block(qi):
        s = jnp.einsum('bqhcd,bkhcd->bhcqk', qi, k).astype(F32) * scale
        p = jax.nn.softmax(s, axis=-1)
        w = p[:, :, 0] - lam * p[:, :, 1]
        return jnp.einsum('bhqk,bkhe->bqhe', w.astype(v.dtype), v)

    o = lax.map(block, qb)
    return o.transpose(1, 0, 2, 3, 4).reshape(B, L, H, v.shape[-1])

def short_conv(u, w, b):
    up = jnp.pad(u, ((0, 0), (1, 1), (0, 0)))
    return up[:, :-2] * w[0] + up[:, 1:-1] * w[1] + up[:, 2:] * w[2] + b

def hyena_filter(L, w1, b1, w2, b2, w3, freq):
    t = jnp.linspace(0.0, 1.0, L, dtype=F32)[:, None]
    bands = (FILTER_EMB - 1) // 2
    wpos = 2.0 * math.pi * jnp.arange(L, dtype=F32)[:, None] / L
    f = jnp.linspace(1e-4, bands - 1, bands, dtype=F32)[None, :]
    z = jnp.concatenate([t, jnp.cos(f * wpos), -jnp.sin(f * wpos)], axis=-1)
    fr = freq.astype(F32)
    h = jnp.sin(fr * (z @ w1.astype(F32) + b1.astype(F32)))
    h = jnp.sin(fr * (h @ w2.astype(F32) + b2.astype(F32)))
    h = (h @ w3.astype(F32)).reshape(L, 2, HY_WIDTH)
    max_decay = math.log(DECAY_TARGET) / FAST_DECAY_PCT
    min_decay = math.log(DECAY_TARGET) / SLOW_DECAY_PCT
    deltas = jnp.abs(jnp.linspace(min_decay, max_decay, HY_WIDTH, dtype=F32))
    h = h * jnp.exp(-t[:, :, None] * deltas)
    kern = jnp.concatenate([h[:, 0], jnp.zeros((1, HY_WIDTH), F32), h[1:, 1][::-1]], axis=0)
    return kern / jnp.sum(jnp.abs(kern), axis=0, keepdims=True)

def long_conv(z, kern, bias):
    L = z.shape[1]
    zf32 = z.astype(F32)
    zf = jnp.fft.rfft(zf32, n=2 * L, axis=1)
    kf = jnp.fft.rfft(kern, n=2 * L, axis=0)
    y = jnp.fft.irfft(zf * kf[None], n=2 * L, axis=1)[:, :L]
    return (y + zf32 * bias.astype(F32)).astype(z.dtype)

def cross_attention(h, mem, wq, wkv, wo):
    B, L, _ = h.shape
    M = mem.shape[1]
    q = (h @ wq).reshape(B, L, X_HEADS, X_HEAD_DIM)
    kv = (mem @ wkv).reshape(B, M, 2, X_HEADS, X_HEAD_DIM)
    s = jnp.einsum('bqhd,bkhd->bhqk', q, kv[:, :, 0]).astype(F32) * (X_HEAD_DIM ** -0.5)
    p = jax.nn.softmax(s, axis=-1)
    o = jnp.einsum('bhqk,bkhd->bqhd', p.astype(h.dtype), kv[:, :, 1]).reshape(B, L, D_MODEL)
    return o @ wo

def expert_choice_ffn(h, w_router, w_gate, w_up, w_down):
    B, L, D = h.shape
    T = B * L
    xt = h.reshape(T, D)
    cap = EC_CAPACITY_FACTOR * T // N_EXPERTS
    aff = jax.nn.softmax((xt @ w_router).astype(F32), axis=-1)
    g, idx = lax.top_k(aff.T, cap)
    xe = xt[idx]
    he = jax.nn.silu(jnp.einsum('ecd,edf->ecf', xe, w_gate)) * jnp.einsum('ecd,edf->ecf', xe, w_up)
    ye = jnp.einsum('ecf,efd->ecd', he, w_down) * g[..., None].astype(h.dtype)
    y = jnp.zeros((T, D), h.dtype).at[idx.reshape(-1)].add(ye.reshape(-1, D))
    return y.reshape(B, L, D)

def encoder_layer(x, mem, P, l):
    B, L, _ = x.shape
    pos = jnp.arange(L, dtype=F32)
    u = rmsnorm(x, P['norm_mix'][l])
    proj = u @ P['w_in'][l]
    o1 = ATT_QK_W
    o2 = o1 + ATT_QK_W
    o3 = o2 + ATT_V_W
    o4 = o3 + 3 * HY_WIDTH
    q, k, v, hy, gates = jnp.split(proj, [o1, o2, o3, o4], axis=-1)
    q = rope_partial(q.reshape(B, L, N_ATT_HEADS, 2, ATT_HEAD_DIM), pos)
    k = rope_partial(k.reshape(B, L, N_ATT_HEADS, 2, ATT_HEAD_DIM), pos)
    v = v.reshape(B, L, N_ATT_HEADS, ATT_V_DIM)
    lam_init = 0.8 - 0.6 * math.exp(-0.3 * l)
    lam = (jnp.exp(jnp.sum(P['lambda_q1'][l].astype(F32) * P['lambda_k1'][l].astype(F32)))
           - jnp.exp(jnp.sum(P['lambda_q2'][l].astype(F32) * P['lambda_k2'][l].astype(F32)))
           + lam_init)
    a = diff_attention(q, k, v, lam)
    a = rmsnorm(a, P['subln'][l]) * (1.0 - lam_init)
    a = a.reshape(B, L, ATT_V_W) @ P['w_br_attn'][l]
    hy = short_conv(hy, P['hy_conv_w'][l], P['hy_conv_b'][l])
    x0, x1, hv = jnp.split(hy, 3, axis=-1)
    kern = hyena_filter(L, P['filt_w1'][l], P['filt_b1'][l], P['filt_w2'][l],
                        P['filt_b2'][l], P['filt_w3'][l], P['filt_freq'][l])
    hz = long_conv(hv * x1, kern, P['filt_bias'][l]) * x0
    hz = hz @ P['w_br_hyena'][l]
    g = jax.nn.sigmoid(gates.astype(F32)).astype(x.dtype).reshape(B, L, N_BRANCH, D_MODEL)
    x = x + (g[:, :, 0] * a + g[:, :, 1] * hz) @ P['w_out'][l]
    x = x + cross_attention(rmsnorm(x, P['norm_x'][l]), rmsnorm(mem, P['norm_mem'][l]),
                            P['w_xq'][l], P['w_xkv'][l], P['w_xo'][l])
    x = x + expert_choice_ffn(rmsnorm(x, P['norm_ffn'][l]), P['w_router'][l],
                              P['w_exp_gate'][l], P['w_exp_up'][l], P['w_exp_down'][l])
    return x

def run_trunk(x, mem, P, norm_final):
    for l in range(DEPTH):
        x = encoder_layer(x, mem, P, l)
    return rmsnorm(x, norm_final)

def setup_inputs(seed: int = 0) -> dict:
    key = jax.random.key(seed)
    ks = iter(jax.random.split(key, 40))

    def nrm(shape, scale):
        return jax.random.normal(next(ks), shape, F32) * scale

    def gain(shape):
        return 1.0 + nrm(shape, 0.02)

    Dl = DEPTH
    D = D_MODEL
    return {
        'x_prompt': nrm((BATCH, SEQ, D), 1.0),
        'x_sample': nrm((DEC_BATCH, DEC_SEQ, D), 1.0),
        'mem_prompt': nrm((BATCH, N_MEM, D), 1.0),
        'mem_sample': nrm((DEC_BATCH, N_MEM, D), 1.0),
        'norm_mix': gain((Dl, D)),
        'w_in': nrm((Dl, D, IN_W), D ** -0.5),
        'lambda_q1': nrm((Dl, ATT_HEAD_DIM), 0.1),
        'lambda_k1': nrm((Dl, ATT_HEAD_DIM), 0.1),
        'lambda_q2': nrm((Dl, ATT_HEAD_DIM), 0.1),
        'lambda_k2': nrm((Dl, ATT_HEAD_DIM), 0.1),
        'subln': gain((Dl, ATT_V_DIM)),
        'w_br_attn': nrm((Dl, ATT_V_W, D), ATT_V_W ** -0.5),
        'hy_conv_w': nrm((Dl, 3, 3 * HY_WIDTH), 3 ** -0.5),
        'hy_conv_b': nrm((Dl, 3 * HY_WIDTH), 0.02),
        'filt_w1': nrm((Dl, FILTER_EMB, FILTER_HIDDEN), FILTER_EMB ** -0.5),
        'filt_b1': nrm((Dl, FILTER_HIDDEN), 0.1),
        'filt_w2': nrm((Dl, FILTER_HIDDEN, FILTER_HIDDEN), FILTER_HIDDEN ** -0.5),
        'filt_b2': nrm((Dl, FILTER_HIDDEN), 0.1),
        'filt_w3': nrm((Dl, FILTER_HIDDEN, 2 * HY_WIDTH), FILTER_HIDDEN ** -0.5),
        'filt_freq': gain((Dl, FILTER_HIDDEN)),
        'filt_bias': nrm((Dl, HY_WIDTH), 1.0),
        'w_br_hyena': nrm((Dl, HY_WIDTH, D), HY_WIDTH ** -0.5),
        'w_out': nrm((Dl, D, D), D ** -0.5),
        'norm_x': gain((Dl, D)),
        'norm_mem': gain((Dl, D)),
        'w_xq': nrm((Dl, D, D), D ** -0.5),
        'w_xkv': nrm((Dl, D, 2 * D), D ** -0.5),
        'w_xo': nrm((Dl, D, D), D ** -0.5),
        'norm_ffn': gain((Dl, D)),
        'w_router': nrm((Dl, D, N_EXPERTS), D ** -0.5),
        'w_exp_gate': nrm((Dl, N_EXPERTS, D, EXPERT_FF), D ** -0.5),
        'w_exp_up': nrm((Dl, N_EXPERTS, D, EXPERT_FF), D ** -0.5),
        'w_exp_down': nrm((Dl, N_EXPERTS, EXPERT_FF, D), EXPERT_FF ** -0.5),
        'norm_final': gain((D,)),
    }

def reference(x_prompt, x_sample, mem_prompt, mem_sample, norm_mix, w_in, lambda_q1, lambda_k1,
              lambda_q2, lambda_k2, subln, w_br_attn, hy_conv_w, hy_conv_b, filt_w1, filt_b1,
              filt_w2, filt_b2, filt_w3, filt_freq, filt_bias, w_br_hyena, w_out, norm_x, norm_mem,
              w_xq, w_xkv, w_xo, norm_ffn, w_router, w_exp_gate, w_exp_up, w_exp_down, norm_final):
    P = dict(norm_mix=norm_mix, w_in=w_in, lambda_q1=lambda_q1, lambda_k1=lambda_k1,
             lambda_q2=lambda_q2, lambda_k2=lambda_k2, subln=subln, w_br_attn=w_br_attn,
             hy_conv_w=hy_conv_w, hy_conv_b=hy_conv_b, filt_w1=filt_w1, filt_b1=filt_b1,
             filt_w2=filt_w2, filt_b2=filt_b2, filt_w3=filt_w3, filt_freq=filt_freq,
             filt_bias=filt_bias, w_br_hyena=w_br_hyena, w_out=w_out, norm_x=norm_x,
             norm_mem=norm_mem, w_xq=w_xq, w_xkv=w_xkv, w_xo=w_xo, norm_ffn=norm_ffn,
             w_router=w_router, w_exp_gate=w_exp_gate, w_exp_up=w_exp_up, w_exp_down=w_exp_down)
    y_prompt = run_trunk(x_prompt, mem_prompt, P, norm_final)
    y_sample = run_trunk(x_sample, mem_sample, P, norm_final)
    return (y_prompt, y_sample)


_drawn_inputs = setup_inputs


def setup_inputs(seed=0):
    import zlib

    import numpy as np

    out = dict(_drawn_inputs(seed))
    spreads = {}
    factors = {'lambda_q1': 3.806,
     'lambda_k2': 8.0,
     'subln': 4.708,
     'hy_conv_b': 2.698,
     'filt_b1': 7.639,
     'filt_b2': 5.995,
     'filt_freq': 8.0,
     'norm_x': 8.0,
     'norm_mem': 8.0,
     'norm_ffn': 3.974,
     'norm_final': 2.837}
    for name, (base, spread) in spreads.items():
        noise = np.random.default_rng([zlib.crc32(name.encode()), seed]).standard_normal(out[name].shape)
        drawn = base * np.exp(spread * noise) if base else spread * noise
        out[name] = __import__('jax').numpy.asarray(drawn.astype(out[name].dtype))
    for name, factor in factors.items():
        out[name] = (out[name] * factor).astype(out[name].dtype)
    return out
```

```python
from contextlib import ExitStack

import numpy as np

import concourse.bass as bass
from concourse import mybir

F32 = mybir.dt.float32
U32 = mybir.dt.uint32
BF16 = mybir.dt.bfloat16
ACT = mybir.ActivationFunctionType
ALU = mybir.AluOpType
AX = mybir.AxisListType

P = 128
D = 1024
KD = D // P
LP, LS = 1024, 256
T = LP + LS
NTP, NTS = LP // P, LS // P
NT = NTP + NTS
CHUNKS = [(0, 512), (512, 512), (1024, 256)]
HEADS, DH, DV = 4, 64, 128
ROT = DH // 4
HY = 512
HG = HY // P
EMB, FH = 33, 64
COL_K, COL_V, COL_HY = 512, 1024, 1536
COL_GA, COL_GB = 3072, 4096
NMEM = 256
XH, XD = 4, 256
NE, FF = 16, 1024
CP, CS = 2 * LP // NE, 2 * LS // NE
CE = CP + CS
EPS = 1e-6
LAM_INIT = 0.2
PI_LOW = 3.1415925
INV_2PI = float(np.float32(1 / (2 * np.pi)))
TWO_PI_A = 6.28125
TWO_PI_B = float(2 * np.pi - 6.28125)
ROUND = 12582912.0

V_MIX, V_X, V_MEM, V_FFN = 0, 8, 16, 24
V_CW, V_CB, V_FB, V_SUB, V_FREQ, V_B1, V_B2 = 32, 68, 80, 84, 85, 86, 87
NV = 88


def shape_tables():
    f = np.float32

    def order(n):
        return np.concatenate([np.arange(0, n, 2), np.arange(1, n, 2)])

    feats, decays = [], []
    bands = (EMB - 1) // 2
    lo, hi = np.log(1e-2) / 1.5, np.log(1e-2) / 0.3
    deltas = np.abs(np.linspace(lo, hi, HY).astype(f))
    for n in (LP, LS):
        t = np.linspace(0.0, 1.0, n).astype(f)
        w = (f(2.0 * np.pi) * np.arange(n).astype(f) / f(n)).astype(f)
        fr = np.linspace(1e-4, bands - 1, bands).astype(f)
        a = (fr[None, :] * w[:, None]).astype(f)
        z = np.concatenate([t[:, None], np.cos(a), -np.sin(a)], axis=1).astype(f)
        feats.append(z[order(n)])
        decays.append(np.exp(-t[:, None] * deltas[None, :]).astype(f)[order(n)])
    feat = np.ascontiguousarray(np.concatenate(feats).T)
    decay = np.ascontiguousarray(np.concatenate(decays).reshape(NT, P, HY).transpose(1, 0, 2))

    def transforms(n):
        k = 2 * np.arange(n // 2) + 1
        even, odd = np.arange(0, n, 2), np.arange(1, n, 2)
        return np.stack([
            g(np.pi * ((t[:, None] * k[None, :]) % (4 * n)) / (2 * n))
            for g, t in ((np.cos, even), (np.cos, odd), (np.sin, even), (np.sin, odd))
        ])

    def rows(m):
        kinds, n, w = m.shape
        return np.ascontiguousarray(m.reshape(kinds, n // P, P, w).transpose(2, 0, 1, 3).astype(f))

    tp, ts = transforms(LP), transforms(LS)
    back = [0, 2, 1, 3]
    inv = ROT // 2
    freq = (f(500000.0) ** (-np.arange(0, ROT, 2).astype(f) / f(ROT))).astype(f)
    ang = (np.arange(LP).astype(f)[None, :] * freq[:, None]).astype(f)
    cos, sin = np.ones((P, LP), f), np.zeros((P, LP), f)
    perm = np.zeros((P, P), f)
    for c in range(2):
        a = DH * c
        cos[a:a + inv], cos[a + inv:a + ROT] = np.cos(ang), np.cos(ang)
        sin[a:a + inv], sin[a + inv:a + ROT] = np.sin(ang), np.sin(ang)
        for d in range(inv):
            perm[a + inv + d, a + d] = -1.0
            perm[a + d, a + inv + d] = 1.0
    return {
        "feat": feat, "decay": decay,
        "fwd_p": rows(tp), "fwd_s": rows(ts),
        "inv_p": rows(tp.transpose(0, 2, 1)[back] / LP), "inv_s": rows(ts.transpose(0, 2, 1)[back] / LS),
        "rope_cos": cos, "rope_sin": sin, "perm": perm, "ident": np.eye(P, dtype=f),
    }


class Count:

    def __init__(self, eng, sem):
        self.eng, self.sem, self.base, self.n = eng, sem, 0, 0

    def inc(self, ins):
        ins.then_inc(self.sem, 1)
        self.n += 1

    def value(self):
        return self.base + self.n

    def wait(self):
        self.eng.wait_ge(self.sem, self.base + self.n)

    def enter(self, i, per):
        self.start, self.per = self.base + self.n, per
        self.base, self.n = i * per + (self.start - per), 0

    def leave(self, passes):
        assert self.n == self.per, (self.n, self.per)
        self.base, self.n = 0, self.start + passes * self.per


SEMS = """dve_step vec_zero vec_in vec_tr vec_ready const_in feat_in decay_in fwd_in inv_in
mlp_mm  arg_ready sin_ready h_mm h_dve tap_abs sums_ready h_pool norm_mm invn_ready
dft_mm dft_act dft_dve x_in_0 x_in_1 x_in_2 norm_act root_rec xn_ready xn_tr ut_ready
hy_in_0 hy_in_1 hy_in_2 hy_mm raw_ready pad_zero  conv_done z_ready z_tr zt_ready
inv_mm  inv_used hz_ready wv_in v_mm v_ready lam_in  lam_sum lam_exp lam_ready
wq_in wk_in rope_in qk_mm raw_qk pm_mm  q_roped k_roped k_zero
s_mm  smax_ready exp_ready  w_ready w_tr wt_ready pv_mm o_ready
 sub_sum sub_root sub_ready sub_tr at_ready
mg_in_0 mg_in_1 mg_mm mg_sig  m_ready wo_in xr_in wo_mm x1_ready
mem_in_0 mem_in_1 wxv_in vm_mm vm_ready xb_in_0 xb_in_1 xb_mm q_ready xk_ready
xs_mm  xmax_ready xexp_ready  xp_ready xp_tr pt_ready xo_mm ot_ready
wx_in_0 wx_in_1 xo2_mm x2_ready acc_out hn_out_0 hn_out_1 wr_in rt_mm  rt_low rt_exp aff_ready aff_tr
 slots_ready idx_tr idx_ready eg0 eu0 eg1 eu1 ed0 ed1 col_ready gather_p gather_s xe_tr xet_ready
gu_mm silu_ready he_ready scol_ready dn_mm y_out scatter_p scatter_s gain_in
fin_act fin_rec fin_ready fin_out""".split() + [f"fin_in_{t}" for t in range(NT // 2)]


def encoder_kernel(nc, a, out_p, out_s):
    def rows_of(p, s, t, n):
        return (p if t < n else s)[(t % n) * P:(t % n + 1) * P, :]

    x_rows = [rows_of(a["x_prompt"][0], a["x_sample"][0], t, NTP) for t in range(NT)]
    out_rows = [rows_of(out_p[0], out_s[0], t, NTP) for t in range(NT)]
    mem_rows = [rows_of(a["mem_prompt"][0], a["mem_sample"][0], t, 2) for t in range(4)]
    w_in = a["w_in"][0]
    acc = nc.dram_tensor("residual_rows", [T, D], F32, kind="Internal").ap()
    hn = nc.dram_tensor("normed_rows", [T, D], F32, kind="Internal").ap()
    acc_quarters = acc.rearrange("t (j n) -> (t j) n", j=4)

    with ExitStack() as ctx:
        sem = {n: ctx.enter_context(nc.semaphore(n)) for n in SEMS}
        arena = ctx.enter_context(nc.sbuf_tensor("arena", [P, 204 * 256], F32))
        PS = ctx.enter_context(nc.psum_tensor("banks", [P, 8, 512], F32))

        def at(kb, *dims):
            n = int(np.prod(dims))
            v = arena[:, int(kb * 256):int(kb * 256) + n]
            if len(dims) == 2:
                v = v.rearrange("p (a b) -> p a b", a=dims[0])
            if len(dims) == 3:
                v = v.rearrange("p (a b c) -> p a b c", a=dims[0], b=dims[1])
            return v

        def small(name, shape, dt=F32):
            return ctx.enter_context(nc.sbuf_tensor(name, shape, dt))

        vec, ident, perm = small("vec", [P, NV]), small("ident_sb", [P, P]), small("perm_sb", [P, P])
        ones, eps = small("ones", [P, 2]), small("eps", [P, 1])
        stat = small("stat", [P, 3, 16])
        invn = small("invn", [P, 2, HG])
        att = small("att", [P, 2, 4, 4])
        lam = small("lam", [P, 4])
        sub = small("sub", [P, 3, NT * HEADS])
        rw = small("rw", [P, KD, NE])
        idx_p, idx_s, idx_q = small("idx_p", [P, NE], U32), small("idx_s", [CS, NE], U32), small("idx_q", [P, NE], U32)
        gates = small("gates", [P, 2, NE])
        now_p, now_s = small("now_p", [P, 1], U32), small("now_s", [CS, 1], U32)
        turn = small("turn", [P, 1])
        out_p_idx, out_q_idx = small("out_p_idx", [P, 1], U32), small("out_q_idx", [P, 1], U32)

        UT = at(0, KD, T)
        SF, DF = at(0, NT, HY), at(20, NT, HY)
        DEC = at(60, NT, HY)
        KS = at(80, 5, 4, HY)
        TAP = at(80, 2, 2, HY)
        FWD, FWDS = at(120, 4, 4, 512), at(152, 4, P)
        FEAT, W3F, H1, H2 = at(154, T), at(159, 2 * HY), at(163, T), at(168, T)
        ARG, RND, W1F, W2F, VROW = at(173, T), at(178, T), at(183, P), at(183.5, P), at(184, P)
        HACC, HAB = at(186, 2, HY), at(192, 4, HY).rearrange("p (r s) c -> p r s c", r=2)
        XS = [at(182 + 4 * i, D) for i in range(3)]
        XN = [at(194 + 4 * i, D) for i in range(2)]
        SQJ = at(202, D // 2).bitcast(BF16)
        Z = at(40, HG, T)
        ZT = at(60, NT, HY)
        RAW, CX, CH = [at(166, LP + LS + 4), at(171.25, LP + LS + 4)], at(176.5, T), at(182, T)
        RAW0, CX0 = at(68, LP + LS + 4), at(73.25, T)
        HYW = [at(154 + 4 * i, KD, P) for i in range(3)] + [at(60, KD, P), at(64, KD, P)]
        TEF, TE, AB, TT = at(60, 2, HY), at(188, 2, HY), at(192, 4, HY), at(200, 2, HY)
        INV, INVS = at(154, 4, 4, 512), at(186, 4, P)
        V, AO, AT = at(80, NT, HY), at(60, NT, HY), at(100, HEADS, T)
        WV, COS, SIN = at(120, KD, HY), at(136, LP), at(140, LP)
        PP = [[at(120 + 8 * i + 4 * c, LP) for c in range(2)] for i in range(2)]
        WT = [at(144 + 4 * i, KD, P) for i in range(2)]
        WQ, WK = at(154, KD, P), at(158, KD, P)
        QRAW, KRAW, QT, K0, K1, RT = (at(162 + 5 * i, T) for i in range(6))
        LAMV = at(152, 4, DH)
        SQ = at(120, NT, HY)
        MT = at(60, KD, T)
        MGW = [(at(120 + 12 * b, KD, P), at(124 + 12 * b, KD, P), at(128 + 12 * b, HG, P), at(130 + 12 * b, HG, P))
               for b in range(2)]
        SG, TM = at(144, 2, 2, HY), at(152, 2, 2, HY)
        WO = at(160, KD, D)
        X = at(0, NT, D)
        U2T = at(100, KD, T)
        MEMT, MS = at(40, KD, 2 * NMEM), [at(56, D), at(96, D)]
        WXV, VM = at(60, KD, D), at(172, 4, D)
        XQW, XKW = [at(156 + 8 * b, KD, P) for b in range(2)], [at(160 + 8 * b, KD, P) for b in range(2)]
        QX, KX = at(60, KD, T), at(140, KD, 2 * NMEM)
        XP, PT = [at(156 + 4 * i, XH, NMEM) for i in range(2)], [at(164 + 4 * i, 2 * XH, P) for i in range(2)]
        OT = at(100, KD, T)
        WXO = [at(40, KD, 512), at(140, KD, 512)]
        HT = at(60, KD, T)
        LG, AF = at(156, NT, NE), at(157, T)[0:NE]
        VAL, IDX = at(162, CE)[0:NE], at(163, CE)[0:NE].bitcast(U32)
        SLOT_I, SLOT_V = at(164, P + CS + P)[0:NE], at(166, P + CS + P)[0:NE]
        RM = at(168, 2, 16)
        WG, WU, WD = [at(0, KD, 512), at(32, KD, 512)], [at(16, KD, 512), at(48, KD, 512)], [at(64, KD, 512), at(80, KD, 512)]
        XE, XES = at(100, D), at(104, D)[0:CS]
        XET, HE = at(112, KD, CE), at(117, KD, CE)
        SL = at(122, 2, CE)
        YP, YS = at(124, D), at(128, 256)
        GROW = at(130, D)
        FIN = [at(4 * t, D) for t in range(NT)]

        def blocked(dram, c0, n):
            return dram[:, bass.ds(c0, n)].rearrange("(k p) c -> p k c", p=P)

        def bank4(b):
            return PS[:, b, :].rearrange("p (a c) -> p a c", a=4)

        def wide(v, n):
            return v.unsqueeze(2).to_broadcast([v.shape[0], v.shape[1], n])

        def taps_at(r):
            before = 2 * r + (r > 0) + (r > NTP)
            return before + 2, before + 2 + (r in (0, NTP))

        def taps_summed(r):
            return 2 * (r + 1) - 1 - (r >= NTP)

        def dft_read(q):
            return (4 * q if q < 5 else 20 + 20 * (q - 5)) + 4

        DFT_ALL = 20 + 5 * 20
        N_X, N_MEM, N_FFN = NT, 2 * NT, 2 * NT + 4
        NORMED = N_FFN + NT
        tiles = [slice(t * P, (t + 1) * P) for t in range(NT)]

        def keys(i):
            return (0, LP) if i < NTP else (LP, LS)

        def w_blocks(i):
            return (2 * i if i < NTP else 2 * NTP + (i - NTP)), (2 if i < NTP else 1)

        W_HEAD = 2 * NTP + NTS
        block = ctx.enter_context(nc.Block())

        @block.sync
        def _(sp):
            sp.wait_ge(sem["vec_zero"], 1)
            n_vec = 0
            for row, v, r in ((V_MIX, a["norm_mix"], 8), (V_X, a["norm_x"], 8), (V_MEM, a["norm_mem"], 8),
                              (V_FFN, a["norm_ffn"], 8), (V_CB, a["hy_conv_b"], 12), (V_FB, a["filt_bias"], 4),
                              (V_SUB, a["subln"], 1)):
                sp.dma_start(VROW[row:row + r, :], v[0].rearrange("(r c) -> r c", c=P)).then_inc(sem["vec_in"], 16)
            sp.dma_start(VROW[V_CW:V_CW + 36, :], a["hy_conv_w"][0].rearrange("k (r c) -> (k r) c", c=P)).then_inc(sem["vec_in"], 16)
            for row, v in ((V_FREQ, a["filt_freq"]), (V_B1, a["filt_b1"]), (V_B2, a["filt_b2"])):
                sp.dma_start(VROW[row:row + 1, 0:FH], v).then_inc(sem["vec_in"], 16)
            sp.dma_start(ident[:, :], a["ident"]).then_inc(sem["const_in"], 16)
            sp.dma_start(perm[:, :], a["perm"]).then_inc(sem["const_in"], 16)
            sp.dma_start(FEAT[0:EMB, :], a["feat"]).then_inc(sem["feat_in"], 16)
            sp.dma_start(W1F[0:EMB, 0:FH], a["filt_w1"][0]).then_inc(sem["feat_in"], 16)
            sp.dma_start(W2F[0:FH, 0:FH], a["filt_w2"][0]).then_inc(sem["feat_in"], 16)
            sp.dma_start(W3F[0:FH, :], a["filt_w3"][0]).then_inc(sem["feat_in"], 16)
            sp.dma_start(DEC, a["decay"]).then_inc(sem["decay_in"], 16)
            sp.dma_start(FWD, a["fwd_p"]).then_inc(sem["fwd_in"], 16)
            sp.dma_start(FWDS, a["fwd_s"].rearrange("p a b c -> p (a b) c")).then_inc(sem["fwd_in"], 16)
            sp.dma_start(rw[:, :, :], blocked(a["w_router"][0], 0, NE)).then_inc(sem["wr_in"], 16)
            sp.wait_ge(sem["norm_mm"], 1)
            for t in range(NT):
                if t >= 3:
                    sp.wait_ge(sem["xn_ready"], t - 2)
                sp.dma_start(XS[t % 3], x_rows[t]).then_inc(sem[f"x_in_{t % 3}"], 16)
            sp.wait_ge(sem["h_mm"], NT)
            for b in range(2 * HG):
                if b >= 3:
                    sp.wait_ge(sem["hy_mm"], 3 * (b - 2))
                c0 = COL_HY + HY * (1 + b % 2) + P * (b // 2)
                sp.dma_start(HYW[b % 3], blocked(w_in, c0, P)).then_inc(sem[f"hy_in_{b % 3}"], 16)
            sp.wait_ge(sem["z_ready"], HG)
            sp.dma_start(INV, a["inv_p"]).then_inc(sem["inv_in"], 16)
            sp.dma_start(INVS, a["inv_s"].rearrange("p a b c -> p (a b) c")).then_inc(sem["inv_in"], 16)
            sp.wait_ge(sem["dft_mm"], 40)
            for g in range(HG):
                if g == 2:
                    sp.dma_start(WV, blocked(w_in, COL_V, HY)).then_inc(sem["wv_in"], 16)
                    sp.dma_start(COS, a["rope_cos"]).then_inc(sem["rope_in"], 16)
                    sp.dma_start(SIN, a["rope_sin"]).then_inc(sem["rope_in"], 16)
                if g >= 2:
                    sp.wait_ge(sem["hy_mm"], 3 * (2 * HG + g - 1))
                sp.dma_start(HYW[3 + g % 2], blocked(w_in, COL_HY + P * g, P)).then_inc(sem[f"hy_in_{g % 2}"], 16)
            sp.wait_ge(sem["inv_mm"], 3 * HG)
            sp.dma_start(WQ, blocked(w_in, 0, P)).then_inc(sem["wq_in"], 16)
            sp.dma_start(WK, blocked(w_in, COL_K, P)).then_inc(sem["wk_in"], 16)
            with sp.Fori(1, HEADS) as h:
                sp.wait_ge(sem["qk_mm"], h * 6)
                sp.dma_start(WQ, blocked(w_in, h * P, P)).then_inc(sem["wq_in"], 16)
                sp.dma_start(WK, blocked(w_in, h * P + COL_K, P)).then_inc(sem["wk_in"], 16)

            def merge_load(B, b):
                ga, gb, wa, wh = MGW[b]
                s = sem[f"mg_in_{b}"]
                sp.dma_start(ga, blocked(w_in, B * P + COL_GA, P)).then_inc(s, 16)
                sp.dma_start(gb, blocked(w_in, B * P + COL_GB, P)).then_inc(s, 16)
                sp.dma_start(wa, blocked(a["w_br_attn"][0], B * P, P)).then_inc(s, 16)
                sp.dma_start(wh, blocked(a["w_br_hyena"][0], B * P, P)).then_inc(s, 16)

            sp.wait_ge(sem["sub_ready"], 1)
            merge_load(0, 0)
            merge_load(1, 1)
            sp.dma_start(WO, blocked(a["w_out"][0], 0, D)).then_inc(sem["wo_in"], 16)
            with sp.Fori(1, KD // 2) as c:
                for b in range(2):
                    sp.wait_ge(sem["mg_mm"], c * 6 + (3 * b - 3))
                    merge_load(c * 2 + b, b)
            sp.wait_ge(sem["mg_mm"], 3 * KD)
            sp.dma_start(X[:, 0:NTP, :], a["x_prompt"][0].rearrange("(t p) d -> p t d", p=P)).then_inc(sem["xr_in"], 16)
            sp.dma_start(X[:, NTP:NT, :], a["x_sample"][0].rearrange("(t p) d -> p t d", p=P)).then_inc(sem["xr_in"], 16)
            sp.wait_ge(sem["wo_mm"], 2 * NT)
            sp.dma_start(MS[0], mem_rows[0]).then_inc(sem["mem_in_0"], 16)
            sp.dma_start(MS[1], mem_rows[1]).then_inc(sem["mem_in_1"], 16)
            sp.dma_start(WXV, blocked(a["w_xkv"][0], D, D)).then_inc(sem["wxv_in"], 16)

            def xq_load(B, b):
                sp.dma_start(XQW[b], blocked(a["w_xq"][0], B * P, P)).then_inc(sem[f"xb_in_{b}"], 16)
                sp.dma_start(XKW[b], blocked(a["w_xkv"][0], B * P, P)).then_inc(sem[f"xb_in_{b}"], 16)

            xq_load(0, 0)
            xq_load(1, 1)
            for m in (2, 3):
                sp.wait_ge(sem["xn_ready"], N_MEM + m - 1)
                sp.dma_start(MS[m % 2], mem_rows[m]).then_inc(sem[f"mem_in_{m % 2}"], 16)
            with sp.Fori(1, KD // 2) as c:
                for b in range(2):
                    sp.wait_ge(sem["xb_mm"], c * 8 + (4 * b - 4))
                    xq_load(c * 2 + b, b)
            sp.wait_ge(sem["xb_mm"], 4 * KD)
            sp.dma_start(WXO[0], blocked(a["w_xo"][0], 0, 512)).then_inc(sem["wx_in_0"], 16)
            sp.wait_ge(sem["xs_mm"], NT)
            sp.dma_start(WXO[1], blocked(a["w_xo"][0], 512, 512)).then_inc(sem["wx_in_1"], 16)
            for t in range(NT):
                sp.wait_ge(sem["x2_ready"], NT + t + 1)
                sp.dma_start(acc[tiles[t], :], X[:, t, :]).then_inc(sem["acc_out"], 16)
                sp.wait_ge(sem["xn_ready"], N_FFN + t + 1)
                sp.dma_start(hn[tiles[t], :], XN[t % 2]).then_inc(sem[f"hn_out_{t % 2}"], 16)
            sp.wait_ge(sem["acc_out"], 16 * NT)
            sp.wait_ge(sem["rt_mm"], NT)

            def expert_load(e, first):
                halves = (("eg0", WG[0], "w_exp_gate", 0), ("eu0", WU[0], "w_exp_up", 0),
                          ("eg1", WG[1], "w_exp_gate", 512), ("eu1", WU[1], "w_exp_up", 512),
                          ("ed0", WD[0], "w_exp_down", 0), ("ed1", WD[1], "w_exp_down", 512))
                for n, (s, dst, w, c0) in enumerate(halves):
                    if not first and n in (0, 2):
                        sp.wait_ge(sem["gu_mm"], e * 8 + (2 * n - 4))
                    if not first and n == 4:
                        sp.wait_ge(sem["dn_mm"], e * 3)
                    src = a[w][0][bass.ds(e, 1), :, c0:c0 + 512].rearrange("e (k p) c -> p (e k) c", p=P)
                    sp.dma_start(dst, src).then_inc(sem[s], 16)

            expert_load(0, True)
            sp.dma_start(GROW, a["norm_final"].unsqueeze(0).to_broadcast([P, D])).then_inc(sem["gain_in"], 16)
            with sp.Fori(1, NE) as e:
                expert_load(e, False)
            sp.wait_ge(sem["gu_mm"], 8 * NE)
            sp.wait_ge(sem["scatter_p"], 16 * NE)
            sp.wait_ge(sem["scatter_s"], 16 * NE)
            for t in range(0, NT, 2):
                sp.dma_start(at(4 * t, 2, D), acc[t * P:(t + 2) * P, :].rearrange("(t p) d -> p t d", p=P)).then_inc(sem[f"fin_in_{t // 2}"], 16)
            for t in range(NT):
                sp.wait_ge(sem["fin_ready"], t + 1)
                sp.dma_start(out_rows[t], FIN[t]).then_inc(sem["fin_out"], 16)
            sp.wait_ge(sem["fin_out"], 16 * NT)

        @block.gpsimd
        def _(pool):
            taps = Count(pool, sem["h_pool"])
            for r in range(NT):
                pool.wait_ge(sem["h_dve"], taps_at(r)[1])
                taps.inc(pool.tensor_tensor(SF[:, r, :], TAP[:, r % 2, 0, :], TAP[:, r % 2, 1, :], ALU.add))
                taps.inc(pool.tensor_tensor(DF[:, r, :], TAP[:, r % 2, 0, :], TAP[:, r % 2, 1, :], ALU.subtract))

            pool.wait_ge(sem["dft_mm"], 40)
            for n, v in enumerate(("lambda_q1", "lambda_k1", "lambda_q2", "lambda_k2")):
                pool.dma_start(LAMV[:, n, :], a[v].to_broadcast([P, DH])).then_inc(sem["lam_in"], 16)

            def gather(e, first):
                if not first:
                    pool.wait_ge(sem["gather_p"], e * 16)
                    pool.wait_ge(sem["gather_s"], e * 16)
                pool.tensor_copy(now_p[:, :], idx_p[:, bass.ds(e, 1)]).then_inc(sem["col_ready"], 1)
                pool.tensor_copy(now_s[:, :], idx_s[:, bass.ds(e, 1)]).then_inc(sem["col_ready"], 1)
                if not first:
                    pool.wait_ge(sem["xe_tr"], e * 3)
                pool.wait_ge(sem["col_ready"], e * 2 + 2)
                pool.tensor_tensor(turn[:, :], ones[:, 0:1], ones[:, 0:1], ALU.mult)
                pool.indirect_dma_start(XE, None, hn, bass.IndirectOffsetOnAxis(ap=now_p[:, 0:1], axis=0)).then_inc(sem["gather_p"], 16)
                pool.indirect_dma_start(XES, None, hn, bass.IndirectOffsetOnAxis(ap=now_s[:, 0:1], axis=0)).then_inc(sem["gather_s"], 16)

            def scatter(e, first):
                if not first:
                    pool.wait_ge(sem["scatter_p"], e * 16)
                    pool.wait_ge(sem["scatter_s"], e * 16)
                pool.tensor_copy(out_p_idx[:, :], idx_p[:, bass.ds(e, 1)]).then_inc(sem["scol_ready"], 1)
                pool.tensor_copy(out_q_idx[:, :], idx_q[:, bass.ds(e, 1)]).then_inc(sem["scol_ready"], 1)
                pool.wait_ge(sem["scol_ready"], e * 2 + 2)
                pool.wait_ge(sem["y_out"], e * 3 + 3)
                pool.tensor_tensor(turn[:, :], ones[:, 0:1], ones[:, 0:1], ALU.mult)
                pool.indirect_dma_start(acc, bass.IndirectOffsetOnAxis(ap=out_p_idx[:, 0:1], axis=0), YP, None,
                                        compute_op=ALU.add).then_inc(sem["scatter_p"], 16)
                pool.indirect_dma_start(acc_quarters, bass.IndirectOffsetOnAxis(ap=out_q_idx[:, 0:1], axis=0), YS, None,
                                        compute_op=ALU.add).then_inc(sem["scatter_s"], 16)

            pool.wait_ge(sem["idx_ready"], 5)
            pool.wait_ge(sem["hn_out_0"], 16 * NT // 2)
            pool.wait_ge(sem["hn_out_1"], 16 * NT // 2)
            pool.wait_ge(sem["acc_out"], 16 * NT)
            gather(0, True)
            gather(1, False)
            scatter(0, True)
            with pool.Fori(1, NE - 1) as e:
                gather(e + 1, False)
                scatter(e, False)
            scatter(NE - 1, False)

        @block.tensor
        def _(pe):
            def product(out, pairs):
                for n, (l, r) in enumerate(pairs):
                    last = pe.matmul(out, l, r, start=(n == 0), stop=(n == len(pairs) - 1))
                return last

            def wait(name, v):
                pe.wait_ge(sem[name], v)

            wait("vec_in", 16 * 11)
            wait("const_in", 32)
            pe.transpose(PS[:, 0, 0:NV], VROW[0:NV, :], ident[0:NV, 0:NV]).then_inc(sem["vec_tr"], 1)
            wait("feat_in", 64)
            wait("vec_ready", 1)
            for layer, (w, h) in enumerate(((W1F, FEAT), (W2F, H1))):
                if layer:
                    wait("sin_ready", 1)
                for n, (c0, cn) in enumerate(CHUNKS):
                    product(PS[:, n, 0:cn], [(w, h[:, c0:c0 + cn])]).then_inc(sem["mlp_mm"], 1)
            wait("sin_ready", 2)
            for r in range(NT):
                if r >= 4:
                    wait("h_dve", taps_at(r - 4)[0])
                b = 2 * (r % 4)
                product(PS[:, b, :], [(H2[:, tiles[r]], W3F[:, 0:HY])])
                product(PS[:, b + 1, :], [(H2[:, tiles[r]], W3F[:, HY:2 * HY])]).then_inc(sem["h_mm"], 1)
            wait("sums_ready", 1)
            for s in range(2):
                for g in range(HG):
                    last = product(PS[:, 0, 4 * s + g:4 * s + g + 1], [(HACC[:, s, tiles[g]], ones[:, 0:1])])
            last.then_inc(sem["norm_mm"], 1)

            def dft(q, even, odd):
                j = q % 5
                b = 4 * (q % 2)
                if q >= 2:
                    wait("dft_dve", dft_read(q - 2))
                for kind in (0, 2, 1, 3):
                    src = (even, odd)[kind % 2][kind // 2]
                    if j < 4:
                        pairs = [(FWD[:, kind, m, tiles[j]], src[:, 4 * (kind % 2) + m, :]) for m in range(4)]
                    else:
                        pairs = [(FWDS[:, kind, :], src[:, NTP + kind % 2, :])]
                    product(PS[:, b + kind, :], pairs).then_inc(sem["dft_mm"], 1)

            wait("h_pool", 2 * NT)
            wait("fwd_in", 32)
            wait("invn_ready", 1)
            for q in range(5):
                dft(q, (SF, DF), (SF, DF))

            def turn_rows(q):
                wait("xn_ready", q + 1)
                for half in range(2):
                    if q >= 1:
                        wait("ut_ready", 2 * (q - 1) + half + 1)
                    for k in range(4):
                        last = pe.transpose(PS[:, 6 + half, k * P:(k + 1) * P], XN[q % 2][:, tiles[4 * half + k]], ident[:, :])
                    last.then_inc(sem["xn_tr"], 1)

            wait("dft_dve", dft_read(3))
            for t in range(NT):
                turn_rows(t)

            def hyena_project(b, slot, arrived, first_bank):
                wait(f"hy_in_{arrived[0]}", arrived[1])
                for n, (c0, cn) in enumerate(CHUNKS):
                    product(PS[:, first_bank + n, 0:cn], [(HYW[slot][:, k, :], UT[:, k, c0:c0 + cn]) for k in range(KD)]
                            ).then_inc(sem["hy_mm"], 1)

            def turn_z(g):
                wait("z_ready", g + 1)
                for part, (n0, n1) in enumerate(((0, 4), (4, 8), (8, 10))):
                    if part == 2:
                        wait("zt_ready", 3 * g + 1)
                    elif g >= 1:
                        wait("zt_ready", 3 * g if part == 0 else 3 * g - 1)
                    for r in range(n0, n1):
                        base, odd = (256 * (r % 4), r // 4) if r < NTP else (LP, r - NTP)
                        last = pe.transpose(PS[:, 6 + part % 2, (r - n0) * P:(r - n0 + 1) * P],
                                            Z[:, g, base + odd:base + 256:2], ident[:, :])
                    last.then_inc(sem["z_tr"], 1)

            wait("dft_dve", dft_read(4))
            wait("ut_ready", 2 * NT)
            for b in range(2 * HG):
                if b >= 2:
                    wait("raw_ready", b - 1)
                hyena_project(b, b % 3, (b % 3, 16 * (b // 3 + 1)), 3 * (b % 2))
                if b >= 2 and b % 2 == 0:
                    turn_z(b // 2 - 1)
            turn_z(HG - 1)
            wait("zt_ready", 3 * HG)
            wait("raw_ready", 2 * HG)
            for q in range(5, 10):
                dft(q, (ZT, ZT), (ZT, ZT))
            wait("dft_dve", dft_read(8))
            loads = [3, 3]
            for g in range(HG):
                loads[g % 2] += 1
                if g >= 1:
                    wait("raw_ready", 2 * HG + g)
                hyena_project(2 * HG + g, 3 + g % 2, (g % 2, 16 * loads[g % 2]), 0)
                if g == 0:
                    wait("dft_dve", DFT_ALL)
                    wait("inv_in", 32)
                else:
                    wait("inv_used", g)
                for odd in range(2):
                    product(PS[:, 3 + odd, :], [(KS[:, j, 2 * odd + s, tiles[g]], INV[:, 2 * odd + s, j, :])
                                                for s in range(2) for j in range(4)]).then_inc(sem["inv_mm"], 1)
                for odd in range(2):
                    last = product(PS[:, 5, odd * P:(odd + 1) * P],
                                   [(KS[:, 4, 2 * odd + s, tiles[g]], INVS[:, 2 * odd + s, :]) for s in range(2)])
                last.then_inc(sem["inv_mm"], 1)
            wait("wv_in", 16)
            for t in range(NT):
                if t >= 2:
                    wait("v_ready", t - 1)
                product(PS[:, 6 + t % 2, :], [(UT[:, k, tiles[t]], WV[:, k, :]) for k in range(KD)]).then_inc(sem["v_mm"], 1)

            def head(h, first):
                wait("wq_in", h * 16 + 16)
                if first:
                    wait("raw_ready", 3 * HG)
                    wait("inv_used", HG)
                    wait("rope_in", 32)
                else:
                    wait("exp_ready", h * 20)
                for part, w in enumerate((WQ, WK)):
                    if part:
                        wait("wk_in", h * 16 + 16)
                        if not first:
                            wait("wt_ready", h * W_HEAD)
                    for n, (c0, cn) in enumerate(CHUNKS):
                        product(PS[:, 3 * part + n, 0:cn], [(w[:, k, :], UT[:, k, c0:c0 + cn]) for k in range(KD)]
                                ).then_inc(sem["qk_mm"], 1)
                for part, raw in enumerate((QRAW, KRAW)):
                    wait("raw_qk", h * 6 + (3 * part + 3))
                    for n, (c0, cn) in enumerate(CHUNKS):
                        product(PS[:, 3 * part + n, 0:cn], [(perm[:, :], raw[:, c0:c0 + cn])]).then_inc(sem["pm_mm"], 1)
                wait("q_roped", h + 1)
                wait("k_roped", h * 2 + 2)

                def scores(i):
                    k0, kn = keys(i)
                    for c, kk in enumerate((K0, K1)):
                        if i >= 1:
                            wait("exp_ready", h * 20 + (2 * i - 1 + c))
                        for n in range(0, kn, 512):
                            m = min(512, kn - n)
                            last = product(PS[:, 2 * c + n // 512, 0:m], [(QT[:, tiles[i]], kk[:, k0 + n:k0 + n + m])])
                        last.then_inc(sem["s_mm"], 1)

                def values(i):
                    k0, kn = keys(i)
                    before, groups = w_blocks(i)
                    wait("w_ready", h * NT + (i + 1))
                    for g in range(groups):
                        if i >= 1 or g >= 1:
                            prior = before + g if i > NTP or (i == NTP) else before + g - 1
                            if prior > 0:
                                wait("wt_ready", h * W_HEAD + prior)
                        for m in range(4 * g, min(4 * g + 4, kn // P)):
                            last = pe.transpose(PS[:, 4 + g, (m % 4) * P:(m % 4 + 1) * P], PP[i % 2][0][:, tiles[m]], ident[:, :])
                        last.then_inc(sem["w_tr"], 1)
                    if i >= 2:
                        wait("o_ready", h * NT + (i - 1))
                    wait("wt_ready", h * W_HEAD + (before + groups))
                    product(PS[:, 6 + i % 2, 0:P],
                            [(WT[i % 2][:, m, :], V[:, k0 // P + m, bass.ds(h * P, P)]) for m in range(kn // P)]
                            ).then_inc(sem["pv_mm"], 1)

                scores(0)
                for i in range(NT):
                    if i + 1 < NT:
                        scores(i + 1)
                    values(i)

            head(0, True)
            with pe.Fori(1, HEADS) as h:
                wait("o_ready", h * NT)
                head(h, False)
            wait("o_ready", HEADS * NT)
            wait("sub_ready", 1)
            for q in range(3 * HEADS):
                h, n = q // 3, q % 3
                if q >= 8:
                    wait("at_ready", q - 7)
                for t in range(4 * n, min(4 * n + 4, NT)):
                    last = pe.transpose(PS[:, q % 8, (t % 4) * P:(t % 4 + 1) * P], AO[:, t, tiles[h]], ident[:, :])
                last.then_inc(sem["sub_tr"], 1)
            wait("at_ready", 3 * HEADS)

            def merge(B, b, first):
                wait(f"mg_in_{b}", (B - b) * 32 + 64)
                ga, gb, wa, wh = MGW[b]
                for n, (c0, cn) in enumerate(CHUNKS):
                    s = 4 * ((b + n) % 2)
                    if not (first and 3 * b + n < 2):
                        wait("m_ready", B * 3 + (n - 1))
                    product(PS[:, s, 0:cn], [(ga[:, k, :], UT[:, k, c0:c0 + cn]) for k in range(KD)])
                    product(PS[:, s + 1, 0:cn], [(gb[:, k, :], UT[:, k, c0:c0 + cn]) for k in range(KD)])
                    product(PS[:, s + 2, 0:cn], [(wa[:, k, :], AT[:, k, c0:c0 + cn]) for k in range(HG)])
                    product(PS[:, s + 3, 0:cn], [(wh[:, k, :], Z[:, k, c0:c0 + cn]) for k in range(HG)]).then_inc(sem["mg_mm"], 1)

            wait("hz_ready", HG)
            merge(0, 0, True)
            merge(1, 1, True)
            with pe.Fori(1, KD // 2) as c:
                for b in range(2):
                    merge(c * 2 + b, b, False)
            wait("m_ready", 3 * KD)
            wait("wo_in", 16)
            for q in range(2 * NT):
                t, n = q // 2, q % 2
                if q >= 6:
                    wait("x1_ready", q - 5)
                product(PS[:, q % 6, :], [(MT[:, k, tiles[t]], WO[:, k, n * 512:(n + 1) * 512]) for k in range(KD)]
                        ).then_inc(sem["wo_mm"], 1)
            for t in range(NT):
                turn_rows(N_X + t)
            for m in range(4):
                turn_rows(N_MEM + m)
            wait("ut_ready", 2 * N_FFN)
            wait("x1_ready", 2 * NT)
            wait("wxv_in", 16)
            for q in range(8):
                m, n = q // 2, q % 2
                if q >= 6:
                    wait("vm_ready", q - 5)
                product(PS[:, q % 6, :], [(MEMT[:, k, tiles[m]], WXV[:, k, n * 512:(n + 1) * 512]) for k in range(KD)]
                        ).then_inc(sem["vm_mm"], 1)

            def cross_project(B, b, first):
                wait(f"xb_in_{b}", (B - b) * 16 + 32)
                if first:
                    wait("vm_ready", 8)
                else:
                    wait("q_ready", B * 3 - 3)
                    wait("xk_ready", B - 1)
                for n, (c0, cn) in enumerate(CHUNKS):
                    product(PS[:, 4 * b + n, 0:cn], [(XQW[b][:, k, :], U2T[:, k, c0:c0 + cn]) for k in range(KD)]
                            ).then_inc(sem["xb_mm"], 1)
                product(PS[:, 4 * b + 3, :], [(XKW[b][:, k, :], MEMT[:, k, :]) for k in range(KD)]).then_inc(sem["xb_mm"], 1)

            cross_project(0, 0, True)
            cross_project(1, 1, True)
            with pe.Fori(1, KD // 2) as c:
                for b in range(2):
                    cross_project(c * 2 + b, b, False)

            def cross_scores(i):
                m0 = 0 if i < NTP else NMEM
                if i >= 2:
                    wait("xexp_ready", 4 * (i - 1))
                for hx in range(XH):
                    last = product(PS[:, 2 * (i % 2) + hx // 2, (hx % 2) * NMEM:(hx % 2 + 1) * NMEM],
                                   [(QX[:, 2 * hx + j, tiles[i]], KX[:, 2 * hx + j, m0:m0 + NMEM]) for j in range(2)])
                last.then_inc(sem["xs_mm"], 1)

            def cross_turn(i):
                wait("xp_ready", i + 1)
                for half in range(2):
                    if i >= 1:
                        wait("pt_ready", 2 * (i - 1) + half + 1)
                    for o in range(4 * half, 4 * half + 4):
                        last = pe.transpose(PS[:, 4 + half, (o % 4) * P:(o % 4 + 1) * P],
                                            XP[i % 2][:, o // 2, (o % 2) * P:(o % 2 + 1) * P], ident[:, :])
                    last.then_inc(sem["xp_tr"], 1)

            def cross_values(i):
                m0 = 0 if i < NTP else 2
                wait("pt_ready", 2 * i + 2)
                for half in range(2):
                    if i >= 1:
                        wait("ot_ready", 2 * (i - 1) + half + 1)
                    for o in range(4 * half, 4 * half + 4):
                        hx = o // 2
                        last = product(PS[:, 6 + half, (o % 4) * P:(o % 4 + 1) * P],
                                       [(VM[:, m0 + j, tiles[o]], PT[i % 2][:, 2 * hx + j, :]) for j in range(2)])
                    last.then_inc(sem["xo_mm"], 1)

            wait("q_ready", 3 * KD)
            wait("xk_ready", KD)
            cross_scores(0)
            for i in range(NT):
                if i + 1 < NT:
                    cross_scores(i + 1)
                if i >= 1:
                    cross_values(i - 1)
                cross_turn(i)
            cross_values(NT - 1)
            wait("ot_ready", 2 * NT)
            for q in range(2 * NT):
                n, t = q // NT, q % NT
                if q % NT == 0:
                    wait(f"wx_in_{n}", 16)
                if q >= 6:
                    wait("x2_ready", q - 5)
                product(PS[:, q % 6, :], [(OT[:, k, tiles[t]], WXO[n][:, k, :]) for k in range(KD)]).then_inc(sem["xo2_mm"], 1)

            def route(t):
                wait("ut_ready", 2 * (N_FFN + t) + 2)
                product(PS[:, 0, t * NE:(t + 1) * NE], [(HT[:, k, tiles[t]], rw[:, k, :]) for k in range(KD)]).then_inc(sem["rt_mm"], 1)

            wait("x2_ready", 2 * NT)
            wait("wr_in", 16)
            for t in range(NT):
                turn_rows(N_FFN + t)
                if t >= 1:
                    route(t - 1)
            route(NT - 1)
            wait("aff_ready", 1)
            for t in range(NT):
                last = pe.transpose(PS[0:NE, 1 + t // 4, (t % 4) * P:(t % 4 + 1) * P], LG[:, t, :], ident[:, :])
            last.then_inc(sem["aff_tr"], 1)
            wait("slots_ready", 1)
            pe.transpose(PS[:, 4, 0:NE], SLOT_I[:, 0:P], ident[0:NE, 0:NE])
            pe.transpose(PS[0:CS, 4, NE:2 * NE], SLOT_I[:, P:P + CS], ident[0:NE, 0:NE])
            pe.transpose(PS[:, 4, 2 * NE:3 * NE], SLOT_I[:, P + CS:2 * P + CS], ident[0:NE, 0:NE])
            pe.transpose(PS[:, 4, 3 * NE:4 * NE], SLOT_V[:, 0:P], ident[0:NE, 0:NE])
            pe.transpose(PS[:, 4, 4 * NE:5 * NE], SLOT_V[:, P + CS:2 * P + CS], ident[0:NE, 0:NE]).then_inc(sem["idx_tr"], 1)

            def turn_slots(e, first):
                wait("gather_p", e * 16 + 16)
                wait("gather_s", e * 16 + 16)
                if not first:
                    wait("xet_ready", e * 3)
                for half in range(2):
                    for k in range(4 * half, 4 * half + 4):
                        last = pe.transpose(PS[:, 3 + half, (k % 4) * P:(k % 4 + 1) * P], XE[:, tiles[k]], ident[:, :])
                    last.then_inc(sem["xe_tr"], 1)
                for k in range(KD):
                    last = pe.transpose(PS[:, 5, k * CS:(k + 1) * CS], XES[:, tiles[k]], ident[0:CS, 0:CS])
                last.then_inc(sem["xe_tr"], 1)

            def gate_up(e, first):
                wait("xet_ready", e * 3 + 3)
                for f in range(FF // P):
                    if f % 4 == 0:
                        wait(f"eg{f // 4}", e * 16 + 16)
                        wait(f"eu{f // 4}", e * 16 + 16)
                    if not (first and f < 3):
                        wait("he_ready", e * 8 + (f - 2))
                    for part, w in enumerate((WG, WU)):
                        last = product(PS[:, f % 3, part * CE:(part + 1) * CE],
                                       [(w[f // 4][:, k, tiles[f % 4]], XET[:, k, :]) for k in range(KD)])
                    last.then_inc(sem["gu_mm"], 1)

            def down(e, first, last_one):
                wait("he_ready", e * 8 + 8)
                if not first:
                    wait("y_out", e * 3)
                for n in range(2):
                    wait(f"ed{n}", e * 16 + 16)
                    product(PS[:, 6 + n, :], [(HE[:, f, 0:CP], WD[n][:, f, :]) for f in range(FF // P)]).then_inc(sem["dn_mm"], 1)
                if not last_one:
                    wait("xet_ready", e * 3 + 6)
                for f in range(FF // P):
                    for j in range(4):
                        last = pe.matmul(PS[CS * j:CS * (j + 1), 5, 0:256], HE[:, f, CP:CE],
                                         WD[j // 2][:, f, (j % 2) * 256:(j % 2 + 1) * 256],
                                         start=(f == 0), stop=(f == FF // P - 1), tile_position=(0, CS * j))
                last.then_inc(sem["dn_mm"], 1)

            turn_slots(0, True)
            gate_up(0, True)
            turn_slots(1, False)
            down(0, True, False)
            with pe.Fori(1, NE - 1) as e:
                gate_up(e, False)
                wait("y_out", e * 3)
                turn_slots(e + 1, False)
                down(e, False, False)
            gate_up(NE - 1, False)
            down(NE - 1, False, True)

        @block.scalar
        def _(act):
            for layer, h in enumerate((H1, H2)):
                act.wait_ge(sem["arg_ready"], layer + 1)
                act.activation(h, ARG, ACT.Sin).then_inc(sem["sin_ready"], 1)

            for r in range(NT):
                act.wait_ge(sem["h_dve"], taps_at(r)[1])
                if r >= 2:
                    act.wait_ge(sem["dve_step"], 14 + taps_summed(r - 2))
                act.activation(HAB[:, r % 2, :, :], TAP[:, r % 2, :, :], ACT.Abs).then_inc(sem["tap_abs"], 1)

            def spectra(q):
                for n, kind in enumerate((0, 2)):
                    act.wait_ge(sem["dft_mm"], 4 * q + n + 1)
                    if q >= 1:
                        act.wait_ge(sem["dft_dve"], dft_read(q - 1))
                    act.copy((TEF if q < 5 else TE)[:, n, :], PS[:, 4 * (q % 2) + kind, :]).then_inc(sem["dft_act"], 1)

            for q in range(5):
                spectra(q)

            steps = Count(act, sem["norm_act"])

            def normed(q, src):
                col = q % 16
                if q:
                    steps.wait()
                steps.inc(act.activation(SQJ, src, ACT.Square, accum_out=stat[:, 0, col:col + 1]))
                steps.wait()
                steps.inc(act.activation(stat[:, 1, col:col + 1], stat[:, 0, col:col + 1], ACT.Sqrt, scale=1.0 / D, bias=eps[:, 0:1]))

            act.wait_ge(sem["pad_zero"], 7)
            for t in range(NT):
                act.wait_ge(sem[f"x_in_{t % 3}"], 16 * (t // 3 + 1))
                normed(t, XS[t % 3])

            def raw_out(b, raw, first_bank):
                for n, off in enumerate((1, 513, LP + 3)):
                    cn = CHUNKS[n][1]
                    act.wait_ge(sem["hy_mm"], 3 * b + n + 1)
                    last = act.copy(raw[:, off:off + cn], PS[:, first_bank + n, 0:cn])
                last.then_inc(sem["raw_ready"], 1)

            def z_out(g):
                for part, (n0, n1) in enumerate(((0, 4), (4, 8), (8, 10))):
                    act.wait_ge(sem["z_tr"], 3 * g + part + 1)
                    act.copy(ZT[:, n0:n1, tiles[g]], bank4(6 + part % 2)[:, 0:n1 - n0, :]).then_inc(sem["zt_ready"], 1)

            for b in range(2 * HG):
                if b >= 2:
                    act.wait_ge(sem["conv_done"], b - 1)
                raw_out(b, RAW[b % 2], 3 * (b % 2))
                if b >= 2 and b % 2 == 0:
                    z_out(b // 2 - 1)
            z_out(HG - 1)
            for q in range(5, 10):
                spectra(q)
            act.wait_ge(sem["pad_zero"], 11)
            for g in range(HG):
                if g >= 1:
                    act.wait_ge(sem["conv_done"], 2 * HG + g)
                raw_out(2 * HG + g, RAW0, 0)
            act.wait_ge(sem["lam_sum"], 2)
            act.activation(lam[:, 2:4], lam[:, 0:2], ACT.Exp).then_inc(sem["lam_exp"], 1)
            for t in range(NT):
                act.wait_ge(sem["v_mm"], t + 1)
                act.copy(V[:, t, :], PS[:, 6 + t % 2, :]).then_inc(sem["v_ready"], 1)

            def head(h, first):
                for part, raw in enumerate((QRAW, KRAW)):
                    if not first:
                        act.wait_ge(sem["k_roped"], h * 2)
                    for n, (c0, cn) in enumerate(CHUNKS):
                        act.wait_ge(sem["qk_mm"], h * 6 + (3 * part + n + 1))
                        act.copy(raw[:, c0:c0 + cn], PS[:, 3 * part + n, 0:cn]).then_inc(sem["raw_qk"], 1)

                def exps(i):
                    kn = keys(i)[1]
                    before, groups = w_blocks(i - 2) if i >= 2 else (0, 0)
                    for c in range(2):
                        act.wait_ge(sem["smax_ready"], h * 20 + (2 * i + c + 1))
                        if i >= 2:
                            act.wait_ge(sem["w_tr"], h * W_HEAD + (before + groups))
                        elif not first:
                            act.wait_ge(sem["w_tr"], h * W_HEAD)
                        s = PS[:, 2 * c:2 * c + 2, :].rearrange("p b n -> p (b n)")[:, 0:kn]
                        act.activation(PP[i % 2][c][:, 0:kn], s, ACT.Exp, bias=att[:, i % 2, 1, c:c + 1], scale=DH ** -0.5,
                                       accum_out=att[:, i % 2, 2, c:c + 1]).then_inc(sem["exp_ready"], 1)

                def maps(i):
                    before, groups = w_blocks(i)
                    kn = keys(i)[1]
                    for g in range(groups):
                        act.wait_ge(sem["w_tr"], h * W_HEAD + (before + g + 1))
                        if i >= 2:
                            act.wait_ge(sem["pv_mm"], h * NT + (i - 1))
                        elif not first:
                            act.wait_ge(sem["pv_mm"], h * NT)
                        m = min(4, kn // P - 4 * g)
                        act.copy(WT[i % 2][:, 4 * g:4 * g + m, :], bank4(4 + g)[:, 0:m, :]).then_inc(sem["wt_ready"], 1)

                exps(0)
                for i in range(NT):
                    if i + 1 < NT:
                        exps(i + 1)
                    maps(i)

            act.wait_ge(sem["lam_exp"], 1)
            head(0, True)
            with act.Fori(1, HEADS) as h:
                head(h, False)
            act.wait_ge(sem["sub_sum"], 1)
            act.activation(sub[:, 1, :], sub[:, 0, :], ACT.Sqrt, scale=1.0 / DV, bias=eps[:, 0:1]).then_inc(sem["sub_root"], 1)

            def gates_out(B, b, first):
                for n, (c0, cn) in enumerate(CHUNKS):
                    s = (b + n) % 2
                    act.wait_ge(sem["mg_mm"], B * 3 + (n + 1))
                    if not (first and 3 * b + n < 2):
                        act.wait_ge(sem["m_ready"], B * 3 + (n - 1))
                    for part in range(2):
                        act.activation(SG[:, s, part, 0:cn], PS[:, 4 * s + part, 0:cn], ACT.Sigmoid).then_inc(sem["mg_sig"], 1)

            gates_out(0, 0, True)
            gates_out(1, 1, True)
            with act.Fori(1, KD // 2) as c:
                for b in range(2):
                    gates_out(c * 2 + b, b, False)
            for t in range(NT):
                act.wait_ge(sem["x1_ready"], 2 * t + 2)
                normed(N_X + t, X[:, t, :])
            for m in range(4):
                act.wait_ge(sem[f"mem_in_{m % 2}"], 16 * (m // 2 + 1))
                normed(N_MEM + m, MS[m % 2])

            def queries_out(B, b):
                for n, (c0, cn) in enumerate(CHUNKS):
                    act.wait_ge(sem["xb_mm"], B * 4 + (n + 1))
                    act.copy(QX[:, bass.ds(B, 1), c0:c0 + cn].rearrange("p a n -> p (a n)"), PS[:, 4 * b + n, 0:cn]).then_inc(sem["q_ready"], 1)

            queries_out(0, 0)
            queries_out(1, 1)
            with act.Fori(1, KD // 2) as c:
                for b in range(2):
                    queries_out(c * 2 + b, b)

            def cross_exps(i):
                act.wait_ge(sem["xmax_ready"], i + 1)
                if i >= 2:
                    act.wait_ge(sem["xp_tr"], 2 * (i - 1))
                for hx in range(XH):
                    act.activation(XP[i % 2][:, hx, :], PS[:, 2 * (i % 2) + hx // 2, (hx % 2) * NMEM:(hx % 2 + 1) * NMEM],
                                   ACT.Exp, bias=att[:, i % 2, 1, hx:hx + 1], scale=XD ** -0.5,
                                   accum_out=att[:, i % 2, 2, hx:hx + 1]).then_inc(sem["xexp_ready"], 1)

            cross_exps(0)
            for i in range(NT):
                if i + 1 < NT:
                    cross_exps(i + 1)
                for half in range(2):
                    act.wait_ge(sem["xp_tr"], 2 * i + half + 1)
                    if i >= 2:
                        act.wait_ge(sem["xo_mm"], 2 * (i - 1))
                    act.copy(PT[i % 2][:, 4 * half:4 * half + 4, :], bank4(4 + half)).then_inc(sem["pt_ready"], 1)
            for t in range(NT):
                act.wait_ge(sem["x2_ready"], NT + t + 1)
                normed(N_FFN + t, X[:, t, :])
            act.wait_ge(sem["rt_low"], 1)
            act.activation(LG, LG, ACT.Exp).then_inc(sem["rt_exp"], 1)

            def silus(e, first):
                for f in range(FF // P):
                    act.wait_ge(sem["gu_mm"], e * 8 + (f + 1))
                    if not (first and f < 2):
                        act.wait_ge(sem["he_ready"], e * 8 + (f - 1))
                    act.activation(SL[:, f % 2, :], PS[:, f % 3, 0:CE], ACT.Silu).then_inc(sem["silu_ready"], 1)

            silus(0, True)
            with act.Fori(1, NE) as e:
                silus(e, False)
            fin = Count(act, sem["fin_act"])
            for t in range(NT):
                act.wait_ge(sem[f"fin_in_{t // 2}"], 16)
                if t:
                    fin.wait()
                fin.inc(act.activation(SQJ, FIN[t], ACT.Square, accum_out=stat[:, 0, t:t + 1]))
                fin.wait()
                fin.inc(act.activation(stat[:, 1, t:t + 1], stat[:, 0, t:t + 1], ACT.Sqrt, scale=1.0 / D, bias=eps[:, 0:1]))

        @block.vector
        def _(dve):
            dve.memset(VROW, 0.0)
            dve.memset(at(154, 30 * 256), 0.0)
            dve.memset(ones[:, :], 1.0)
            dve.memset(eps[:, :], EPS).then_inc(sem["vec_zero"], 1)
            dve.wait_ge(sem["vec_tr"], 1)
            dve.tensor_copy(vec[:, :], PS[:, 0, 0:NV]).then_inc(sem["vec_ready"], 1)
            dve.wait_ge(sem["vec_ready"], 1)

            c = step = Count(dve, sem["dve_step"])
            for layer, vb in enumerate((V_B1, V_B2)):
                if layer:
                    dve.wait_ge(sem["sin_ready"], 1)
                for n, (c0, cn) in enumerate(CHUNKS):
                    dve.wait_ge(sem["mlp_mm"], 3 * layer + n + 1)
                    c.inc(dve.tensor_scalar(ARG[:, c0:c0 + cn], PS[:, n, 0:cn], vec[:, vb:vb + 1], vec[:, V_FREQ:V_FREQ + 1],
                                            ALU.add, ALU.mult))
                c.wait()
                c.inc(dve.tensor_scalar(RND, ARG, INV_2PI, ROUND, ALU.mult, ALU.add))
                c.wait()
                c.inc(dve.tensor_scalar(RND, RND, ROUND, None, ALU.subtract))
                for part in (TWO_PI_A, TWO_PI_B):
                    c.wait()
                    c.inc(dve.scalar_tensor_tensor(ARG, RND, -part, ARG, ALU.mult, ALU.add))
                c.wait()
                dve.tensor_scalar(ARG, ARG, PI_LOW, -PI_LOW, ALU.min, ALU.max).then_inc(sem["arg_ready"], 1)

            c = Count(dve, sem["h_dve"])
            dve.wait_ge(sem["decay_in"], 16)
            for r in range(NT):
                dve.wait_ge(sem["h_mm"], r + 1)
                if r >= 2:
                    dve.wait_ge(sem["h_pool"], 2 * (r - 1))
                c.wait() if r else None
                for side in range(2):
                    c.inc(dve.tensor_tensor(TAP[:, r % 2, side, :], PS[:, 2 * (r % 4) + side, :], DEC[:, r, :], ALU.mult))
                assert c.value() == taps_at(r)[0]
                c.wait()
                if r in (0, NTP):
                    c.inc(dve.memset(TAP[0:1, r % 2, 1, :], 0.0))
                    c.wait()
                assert c.value() == taps_at(r)[1]
                into = HACC[:, r // NTP, :]
                dve.wait_ge(sem["tap_abs"], r + 1)
                if r in (0, NTP):
                    step.inc(dve.tensor_tensor(into, HAB[:, r % 2, 0, :], HAB[:, r % 2, 1, :], ALU.add))
                else:
                    for side in range(2):
                        step.wait()
                        step.inc(dve.tensor_tensor(into, HAB[:, r % 2, side, :], into, ALU.add))
            step.wait()
            dve.memset(lam[:, :], 0.0).then_inc(sem["sums_ready"], 1)
            dve.wait_ge(sem["norm_mm"], 1)
            dve.reciprocal(invn[:, :, :].rearrange("p a b -> p (a b)"), PS[:, 0, 0:2 * HG]).then_inc(sem["invn_ready"], 1)
            for raw in RAW:
                for c0, c1 in ((0, 1), (LP + 1, LP + 3), (LP + LS + 3, LP + LS + 4)):
                    dve.memset(raw[:, c0:c1], 0.0).then_inc(sem["pad_zero"], 1)
            dve.memset(att[:, :, :, :], 0.0).then_inc(sem["pad_zero"], 1)

            spec = Count(dve, sem["dft_dve"])

            def butterflies(q, to):
                b = 4 * (q % 2)
                dve.wait_ge(sem["dft_act"], 2 * q + 2)
                dve.wait_ge(sem["dft_mm"], 4 * q + 4)
                te = TEF if q < 5 else TE
                spec.inc(dve.tensor_tensor(to[0], te[:, 0, :], PS[:, b + 1, :], ALU.add))
                spec.inc(dve.tensor_tensor(to[1], te[:, 0, :], PS[:, b + 1, :], ALU.subtract))
                spec.inc(dve.tensor_tensor(to[2], PS[:, b + 3, :], te[:, 1, :], ALU.add))
                spec.inc(dve.tensor_tensor(to[3], PS[:, b + 3, :], te[:, 1, :], ALU.subtract))
                assert spec.value() == dft_read(q)

            for q in range(5):
                if q:
                    spec.wait()
                butterflies(q, [KS[:, q, m, :] for m in range(4)])

            def scaled(q, src, stored):
                dve.wait_ge(sem["norm_act"], 2 * q + 2)
                col = slice(q % 16, q % 16 + 1)
                dve.reciprocal(stat[:, 2, col], stat[:, 1, col]).then_inc(sem["root_rec"], 1)
                if q >= 2:
                    dve.wait_ge(sem["xn_tr"], 2 * (q - 1))
                if stored and q >= N_FFN + 2:
                    dve.wait_ge(sem[f"hn_out_{q % 2}"], 16 * ((q - N_FFN) // 2))
                dve.wait_ge(sem["root_rec"], q + 1)
                dve.tensor_scalar(XN[q % 2], src, stat[:, 2, col], None, ALU.mult).then_inc(sem["xn_ready"], 1)

            def rows_in(q, dst, t, gain):
                for half in range(2):
                    dve.wait_ge(sem["xn_tr"], 2 * q + half + 1)
                    g = vec[:, gain + 4 * half:gain + 4 * half + 4]
                    dve.tensor_tensor(dst[:, 4 * half:4 * half + 4, tiles[t]], bank4(6 + half), wide(g, P), ALU.mult).then_inc(sem["ut_ready"], 1)

            def norm_stage(q0, n, src, dst, gain, stored=False):
                scaled(q0, src(0), stored)
                for t in range(n):
                    if t + 1 < n:
                        scaled(q0 + t + 1, src(t + 1), stored)
                    rows_in(q0 + t, dst, t, gain)

            dve.wait_ge(sem["dft_mm"], 20)
            norm_stage(0, NT, lambda t: XS[t % 3], UT, V_MIX)

            conv, done = step, Count(dve, sem["conv_done"])

            def short_conv(b, raw, to, channel_tile):
                dve.wait_ge(sem["raw_ready"], b + 1)
                col = [V_CW + 12 * k + channel_tile for k in range(3)]
                segs = ((1, 0, LP), (LP + 3, LP, LS))
                for off, o, n in segs:
                    conv.inc(dve.tensor_scalar(to[:, o:o + n], raw[:, off:off + n], vec[:, col[1]:col[1] + 1],
                                               vec[:, V_CB + channel_tile:V_CB + channel_tile + 1], ALU.mult, ALU.add))
                for k, shift in ((0, -1), (2, 1)):
                    for m, (off, o, n) in enumerate(segs):
                        conv.wait()
                        ins = dve.scalar_tensor_tensor(to[:, o:o + n], raw[:, off + shift:off + shift + n], vec[:, col[k]:col[k] + 1],
                                                       to[:, o:o + n], ALU.mult, ALU.add)
                        (done if k == 2 and m == 1 else conv).inc(ins)
                done.wait()

            for b in range(2 * HG):
                g = b // 2
                if b % 2 == 0:
                    short_conv(b, RAW[0], CX, HG + g)
                else:
                    short_conv(b, RAW[1], CH, 2 * HG + g)
                    dve.tensor_tensor(Z[:, g, :], CX, CH, ALU.mult).then_inc(sem["z_ready"], 1)
                    dve.wait_ge(sem["z_ready"], g + 1)

            A0, A1, B0, B1 = (AB[:, m, :] for m in range(4))
            T0, T1 = TT[:, 0, :], TT[:, 1, :]
            for q in range(5, 10):
                butterflies(q, [A0, A1, B0, B1])
                P0, P1, Q0, Q1 = (KS[:, q - 5, m, :] for m in range(4))
                for out, l, r, op in ((T0, A0, P0, ALU.mult), (T1, B0, Q0, ALU.mult), (T0, T0, T1, ALU.subtract),
                                      (T1, A0, Q0, ALU.mult), (A0, B0, P0, ALU.mult), (T1, T1, A0, ALU.add),
                                      (A0, A1, P1, ALU.mult), (B0, B1, Q1, ALU.mult), (A0, A0, B0, ALU.subtract),
                                      (B0, A1, Q1, ALU.mult), (A1, B1, P1, ALU.mult), (B0, B0, A1, ALU.add),
                                      (P0, T0, A0, ALU.add), (P1, T1, B0, ALU.subtract),
                                      (Q0, T0, A0, ALU.subtract), (Q1, T1, B0, ALU.add)):
                    spec.wait()
                    spec.inc(dve.tensor_tensor(out, l, r, op))
                spec.wait()
            for c0, c1 in ((0, 1), (LP + 1, LP + 3), (LP + LS + 3, LP + LS + 4)):
                dve.memset(RAW0[:, c0:c1], 0.0).then_inc(sem["pad_zero"], 1)
            dve.memset(stat[:, :, :], 0.0).then_inc(sem["pad_zero"], 1)

            hz = step
            for g in range(HG):
                short_conv(2 * HG + g, RAW0, CX0, g)
                hz.inc(dve.tensor_scalar(Z[:, g, :], Z[:, g, :], vec[:, V_FB + g:V_FB + g + 1], None, ALU.mult))
                hz.wait()
                dve.wait_ge(sem["inv_mm"], 3 * g + 3)
                for odd in range(2):
                    for s, bank, c0, c1, o, n in ((0, 3 + odd, 0, 512, 0, LP), (1, 5, odd * P, (odd + 1) * P, LP, LS)):
                        dst = Z[:, g, o + odd:o + n:2]
                        ins = dve.scalar_tensor_tensor(dst, PS[:, bank, c0:c1], invn[:, s, g:g + 1], dst, ALU.mult, ALU.add)
                        if odd and s:
                            ins.then_inc(sem["inv_used"], 1)
                        else:
                            hz.inc(ins)
                dve.wait_ge(sem["inv_used"], g + 1)
                dve.tensor_tensor(Z[:, g, :], Z[:, g, :], CX0, ALU.mult).then_inc(sem["hz_ready"], 1)
                dve.wait_ge(sem["hz_ready"], g + 1)

            c = step
            dve.wait_ge(sem["lam_in"], 64)
            c.inc(dve.tensor_tensor(LAMV[:, 0, :], LAMV[:, 0, :], LAMV[:, 1, :], ALU.mult))
            c.inc(dve.tensor_tensor(LAMV[:, 2, :], LAMV[:, 2, :], LAMV[:, 3, :], ALU.mult))
            c.wait()
            dve.tensor_reduce(lam[:, 0:1], LAMV[:, 0, :], AX.X, ALU.add).then_inc(sem["lam_sum"], 1)
            dve.tensor_reduce(lam[:, 1:2], LAMV[:, 2, :], AX.X, ALU.add).then_inc(sem["lam_sum"], 1)
            dve.wait_ge(sem["lam_exp"], 1)
            c.inc(dve.tensor_tensor(lam[:, 0:1], lam[:, 3:4], lam[:, 2:3], ALU.subtract))
            c.wait()
            dve.tensor_scalar(lam[:, 0:1], lam[:, 0:1], -LAM_INIT, None, ALU.add).then_inc(sem["lam_ready"], 1)
            dve.wait_ge(sem["inv_mm"], 3 * HG)
            dve.memset(K0, 0.0).then_inc(sem["k_zero"], 1)
            dve.memset(K1, 0.0).then_inc(sem["k_zero"], 1)
            dve.wait_ge(sem["k_zero"], 2)
            dve.wait_ge(sem["lam_ready"], 1)
            dve.wait_ge(sem["rope_in"], 32)

            rope = smax = mix = step

            def head(h, first):
                for part, raw in enumerate((QRAW, KRAW)):
                    dve.wait_ge(sem["raw_qk"], h * 6 + (3 * part + 3))
                    for n, (c0, cn) in enumerate(CHUNKS):
                        dve.wait_ge(sem["pm_mm"], h * 6 + (3 * part + n + 1))
                        o = c0 % LP
                        to = QT if part == 0 else KRAW
                        if part == 1 and n == 0:
                            dve.wait_ge(sem["q_roped"], h + 1)
                        rope.inc(dve.tensor_tensor(RT[:, c0:c0 + cn], PS[:, 3 * part + n, 0:cn], SIN[:, o:o + cn], ALU.mult))
                        rope.inc(dve.tensor_tensor(to[:, c0:c0 + cn], raw[:, c0:c0 + cn], COS[:, o:o + cn], ALU.mult))
                    rope.wait()
                    if part == 0:
                        dve.tensor_tensor(QT, QT, RT, ALU.add).then_inc(sem["q_roped"], 1)
                    else:
                        dve.tensor_tensor(K0[0:DH, :], KRAW[0:DH, :], RT[0:DH, :], ALU.add).then_inc(sem["k_roped"], 1)
                        dve.tensor_tensor(K1[DH:P, :], KRAW[DH:P, :], RT[DH:P, :], ALU.add).then_inc(sem["k_roped"], 1)

                def maxima(i):
                    kn = keys(i)[1]
                    for c in range(2):
                        dve.wait_ge(sem["s_mm"], h * 20 + (2 * i + c + 1))
                        s = PS[:, 2 * c:2 * c + 2, :].rearrange("p b n -> p (b n)")[:, 0:kn]
                        smax.inc(dve.tensor_reduce(att[:, i % 2, 0, c:c + 1], s, AX.X, ALU.max))
                        smax.wait()
                        dve.tensor_scalar(att[:, i % 2, 1, c:c + 1], att[:, i % 2, 0, c:c + 1], -(DH ** -0.5), None,
                                          ALU.mult).then_inc(sem["smax_ready"], 1)

                def output(i):
                    dve.wait_ge(sem["pv_mm"], h * NT + (i + 1))
                    dve.tensor_scalar(AO[:, i, bass.ds(h * P, P)], PS[:, 6 + i % 2, 0:P], att[:, i % 2, 3, 0:1], None,
                                      ALU.mult).then_inc(sem["o_ready"], 1)

                def mixed(i):
                    kn = keys(i)[1]
                    dve.wait_ge(sem["exp_ready"], h * 20 + (2 * i + 2))
                    if i >= 2:
                        dve.wait_ge(sem["o_ready"], h * NT + (i - 1))
                    r = att[:, i % 2, :, :]
                    mix.inc(dve.reciprocal(r[:, 3, 0:2], r[:, 2, 0:2]))
                    mix.wait()
                    mix.inc(dve.tensor_scalar(r[:, 3, 2:3], r[:, 2, 0:1], r[:, 3, 1:2], lam[:, 0:1], ALU.mult, ALU.mult))
                    mix.wait()
                    dve.scalar_tensor_tensor(PP[i % 2][0][:, 0:kn], PP[i % 2][1][:, 0:kn], r[:, 3, 2:3], PP[i % 2][0][:, 0:kn],
                                             ALU.mult, ALU.add).then_inc(sem["w_ready"], 1)

                for i in range(NT):
                    maxima(i)
                    if i >= 2:
                        output(i - 2)
                    mixed(i)
                output(NT - 2)
                output(NT - 1)
                dve.wait_ge(sem["o_ready"], h * NT + NT)

            head(0, True)
            with dve.Fori(1, HEADS) as h:
                step.enter(h, 52)
                head(h, False)
            step.leave(HEADS - 1)

            c = step
            heads = AO.rearrange("p t (h v) -> p (t h) v", h=HEADS)
            c.inc(dve.tensor_tensor(SQ, AO, AO, ALU.mult))
            c.wait()
            dve.tensor_reduce(sub[:, 0, :], SQ.rearrange("p t (h v) -> p (t h) v", h=HEADS), AX.X, ALU.add).then_inc(sem["sub_sum"], 1)
            dve.wait_ge(sem["sub_root"], 1)
            c.inc(dve.reciprocal(sub[:, 2, :], sub[:, 1, :]))
            c.wait()
            dve.tensor_tensor(heads, heads, wide(sub[:, 2, :], DV), ALU.mult).then_inc(sem["sub_ready"], 1)
            for q in range(3 * HEADS):
                h, n = q // 3, q % 3
                c0, cn = CHUNKS[n]
                dve.wait_ge(sem["sub_tr"], q + 1)
                dve.tensor_scalar(AT[:, h, c0:c0 + cn], PS[:, q % 8, 0:cn], vec[:, V_SUB:V_SUB + 1], 1.0 - LAM_INIT,
                                  ALU.mult, ALU.mult).then_inc(sem["at_ready"], 1)

            mg = step

            def merged(B, b):
                for n, (c0, cn) in enumerate(CHUNKS):
                    s = (b + n) % 2
                    dve.wait_ge(sem["mg_sig"], B * 6 + (2 * n + 2))
                    for part in range(2):
                        mg.inc(dve.tensor_tensor(TM[:, s, part, 0:cn], SG[:, s, part, 0:cn], PS[:, 4 * s + 2 + part, 0:cn], ALU.mult))
                    mg.wait()
                    dve.tensor_tensor(MT[:, bass.ds(B, 1), c0:c0 + cn].rearrange("p a n -> p (a n)"), TM[:, s, 0, 0:cn], TM[:, s, 1, 0:cn],
                                      ALU.add).then_inc(sem["m_ready"], 1)

            merged(0, 0)
            merged(1, 1)
            with dve.Fori(1, KD // 2) as cc:
                mg.enter(cc, 12)
                for b in range(2):
                    merged(cc * 2 + b, b)
            mg.leave(KD // 2 - 1)

            dve.wait_ge(sem["xr_in"], 32)
            for q in range(2 * NT):
                t, n = q // 2, q % 2
                dve.wait_ge(sem["wo_mm"], q + 1)
                dst = X[:, t, n * 512:(n + 1) * 512]
                dve.tensor_tensor(dst, PS[:, q % 6, :], dst, ALU.add).then_inc(sem["x1_ready"], 1)
            norm_stage(N_X, NT, lambda t: X[:, t, :], U2T, V_X)
            norm_stage(N_MEM, 4, lambda m: MS[m % 2], MEMT, V_MEM)
            for q in range(8):
                m, n = q // 2, q % 2
                dve.wait_ge(sem["vm_mm"], q + 1)
                dve.tensor_copy(VM[:, m, n * 512:(n + 1) * 512], PS[:, q % 6, :]).then_inc(sem["vm_ready"], 1)

            def keys_out(B, b):
                dve.wait_ge(sem["xb_mm"], B * 4 + 4)
                dve.tensor_copy(KX[:, bass.ds(B, 1), :].rearrange("p a n -> p (a n)"), PS[:, 4 * b + 3, :]).then_inc(sem["xk_ready"], 1)

            keys_out(0, 0)
            keys_out(1, 1)
            with dve.Fori(1, KD // 2) as cc:
                for b in range(2):
                    keys_out(cc * 2 + b, b)

            xmax = xp = step

            def cross_out(i):
                for half in range(2):
                    dve.wait_ge(sem["xo_mm"], 2 * i + half + 1)
                    dve.tensor_copy(OT[:, 4 * half:4 * half + 4, tiles[i]], bank4(6 + half)).then_inc(sem["ot_ready"], 1)

            for i in range(NT):
                r = att[:, i % 2, :, :]
                dve.wait_ge(sem["xs_mm"], i + 1)
                if i >= 1:
                    dve.wait_ge(sem["xp_ready"], i)
                s = PS[:, 2 * (i % 2):2 * (i % 2) + 2, :].rearrange("p b (h m) -> p (b h) m", h=2)
                xmax.inc(dve.tensor_reduce(r[:, 0, :], s, AX.X, ALU.max))
                xmax.wait()
                dve.tensor_scalar(r[:, 1, :], r[:, 0, :], -(XD ** -0.5), None, ALU.mult).then_inc(sem["xmax_ready"], 1)
                dve.wait_ge(sem["xexp_ready"], 4 * i + 4)
                xp.inc(dve.reciprocal(r[:, 3, :], r[:, 2, :]))
                xp.wait()
                dve.tensor_tensor(XP[i % 2], XP[i % 2], wide(r[:, 3, :], NMEM), ALU.mult).then_inc(sem["xp_ready"], 1)
                if i >= 2:
                    cross_out(i - 2)
            cross_out(NT - 2)
            cross_out(NT - 1)

            for q in range(2 * NT):
                n, t = q // NT, q % NT
                dve.wait_ge(sem["xo2_mm"], q + 1)
                dst = X[:, t, n * 512:(n + 1) * 512]
                dve.tensor_tensor(dst, PS[:, q % 6, :], dst, ALU.add).then_inc(sem["x2_ready"], 1)
            norm_stage(N_FFN, NT, lambda t: X[:, t, :], HT, V_FFN, stored=True)
            c = step
            dve.wait_ge(sem["rt_mm"], NT)
            logits = PS[:, 0, 0:NT * NE].rearrange("p (t e) -> p t e", e=NE)
            c.inc(dve.tensor_reduce(RM[:, 0, 0:NT], logits, AX.X, ALU.max))
            c.wait()
            dve.tensor_tensor(LG, logits, wide(RM[:, 0, 0:NT], NE), ALU.subtract).then_inc(sem["rt_low"], 1)
            dve.wait_ge(sem["rt_exp"], 1)
            c.inc(dve.tensor_reduce(RM[:, 1, 0:NT], LG, AX.X, ALU.add))
            c.wait()
            c.inc(dve.reciprocal(RM[:, 0, 0:NT], RM[:, 1, 0:NT]))
            c.wait()
            dve.tensor_tensor(LG, LG, wide(RM[:, 0, 0:NT], NE), ALU.mult).then_inc(sem["aff_ready"], 1)
            c = step
            dve.wait_ge(sem["aff_tr"], 1)
            for n, (c0, cn) in enumerate(CHUNKS):
                c.inc(dve.tensor_copy(AF[:, c0:c0 + cn], PS[0:NE, 1 + n, 0:cn]))
            c.wait()
            for tok, rounds, s0 in ((AF[:, 0:LP], CP // 8, 0), (AF[:, LP:T], CS // 8, CP)):
                for r in range(rounds):
                    v = VAL[:, s0 + 8 * r:s0 + 8 * r + 8]
                    c.inc(dve.max(v, tok))
                    c.wait()
                    c.inc(dve.max_index(IDX[:, s0 + 8 * r:s0 + 8 * r + 8], v, tok))
                    if r + 1 < rounds:
                        c.wait()
                        c.inc(dve.match_replace(tok, v, tok, -1.0))
                        c.wait()
            c.wait()
            c.inc(dve.tensor_copy(SLOT_I[:, 0:CE], IDX))
            c.wait()
            c.inc(dve.tensor_scalar(SLOT_I[:, CP:CE], SLOT_I[:, CP:CE], float(LP), None, ALU.add))
            c.inc(dve.tensor_copy(SLOT_V[:, 0:CP], VAL[:, 0:CP]))
            c.wait()
            for j in range(4):
                o = CE + CS * j
                c.inc(dve.tensor_scalar(SLOT_I[:, o:o + CS], SLOT_I[:, CP:CE], 4.0, float(j), ALU.mult, ALU.add))
                c.inc(dve.tensor_copy(SLOT_V[:, o:o + CS], VAL[:, CP:CE]))
            c.wait()
            dve.memset(RM[:, :, :], 0.0).then_inc(sem["slots_ready"], 1)
            dve.wait_ge(sem["idx_tr"], 1)
            dve.tensor_copy(idx_p[:, :], PS[:, 4, 0:NE]).then_inc(sem["idx_ready"], 1)
            dve.tensor_copy(idx_s[:, :], PS[0:CS, 4, NE:2 * NE]).then_inc(sem["idx_ready"], 1)
            dve.tensor_copy(idx_q[:, :], PS[:, 4, 2 * NE:3 * NE]).then_inc(sem["idx_ready"], 1)
            for s in range(2):
                dve.tensor_copy(gates[:, s, :], PS[:, 4, (3 + s) * NE:(4 + s) * NE]).then_inc(sem["idx_ready"], 1)
            dve.wait_ge(sem["idx_ready"], 5)

            def slots_in(e):
                dve.wait_ge(sem["xe_tr"], e * 3 + 3)
                for half in range(2):
                    g = vec[:, V_FFN + 4 * half:V_FFN + 4 * half + 4]
                    dve.tensor_tensor(XET[:, 4 * half:4 * half + 4, 0:CP], bank4(3 + half), wide(g, P), ALU.mult).then_inc(sem["xet_ready"], 1)
                dve.tensor_tensor(XET[:, :, CP:CE], PS[:, 5, 0:KD * CS].rearrange("p (k s) -> p k s", k=KD),
                                  wide(vec[:, V_FFN:V_FFN + KD], CS), ALU.mult).then_inc(sem["xet_ready"], 1)

            def hidden(e):
                for f in range(FF // P):
                    dve.wait_ge(sem["silu_ready"], e * 8 + (f + 1))
                    dve.tensor_tensor(HE[:, f, :], SL[:, f % 2, :], PS[:, f % 3, CE:2 * CE], ALU.mult).then_inc(sem["he_ready"], 1)

            def results(e, first):
                if not first:
                    dve.wait_ge(sem["scatter_p"], e * 16)
                    dve.wait_ge(sem["scatter_s"], e * 16)
                for n in range(2):
                    dve.wait_ge(sem["dn_mm"], e * 3 + (n + 1))
                    dve.tensor_scalar(YP[:, n * 512:(n + 1) * 512], PS[:, 6 + n, :], gates[:, 0, bass.ds(e, 1)], None,
                                      ALU.mult).then_inc(sem["y_out"], 1)
                dve.wait_ge(sem["dn_mm"], e * 3 + 3)
                dve.tensor_scalar(YS, PS[:, 5, 0:256], gates[:, 1, bass.ds(e, 1)], None, ALU.mult).then_inc(sem["y_out"], 1)

            slots_in(0)
            hidden(0)
            slots_in(1)
            results(0, True)
            with dve.Fori(1, NE - 1) as e:
                hidden(e)
                slots_in(e + 1)
                results(e, False)
            hidden(NE - 1)
            results(NE - 1, False)
            dve.wait_ge(sem["gain_in"], 16)
            for t in range(NT):
                dve.wait_ge(sem["fin_act"], 2 * t + 2)
                dve.reciprocal(stat[:, 2, t:t + 1], stat[:, 1, t:t + 1]).then_inc(sem["fin_rec"], 1)
                dve.wait_ge(sem["fin_rec"], t + 1)
                dve.scalar_tensor_tensor(FIN[t], FIN[t], stat[:, 2, t:t + 1], GROW, ALU.mult, ALU.mult).then_inc(sem["fin_ready"], 1)


_INS = ["x_prompt", "x_sample", "mem_prompt", "mem_sample", "norm_mix", "w_in", "lambda_q1", "lambda_k1",
        "lambda_q2", "lambda_k2", "subln", "w_br_attn", "hy_conv_w", "hy_conv_b", "filt_w1", "filt_b1",
        "filt_w2", "filt_b2", "filt_w3", "filt_freq", "filt_bias", "w_br_hyena", "w_out", "norm_x", "norm_mem",
        "w_xq", "w_xkv", "w_xo", "norm_ffn", "w_router", "w_exp_gate", "w_exp_up", "w_exp_down", "norm_final"]
_OUTS = [(1, LP, D), (1, LS, D)]


def build(nc, arrays):
    a = {n: nc.dram_tensor(f"in_{n}", v.shape, F32, kind="ExternalInput").ap() for n, v in arrays.items()}
    outs = [nc.dram_tensor(f"out_{i}", s, F32, kind="ExternalOutput").ap() for i, s in enumerate(_OUTS)]
    encoder_kernel(nc, a, *outs)


def kernel(**inputs):
    import concourse.bacc as bacc
    from concourse.bass_utils import run_bass_kernel_spmd

    arrays = {n: np.ascontiguousarray(inputs[n]) for n in _INS} | shape_tables()
    nc = bacc.Bacc("TRN2", target_bir_lowering=False, num_devices=1)
    build(nc, arrays)
    r = run_bass_kernel_spmd(nc, [{f"in_{n}": v for n, v in arrays.items()}], core_ids=[0])
    return tuple(r.results[0][f"out_{i}"] for i in range(len(_OUTS)))
```

```python
from contextlib import ExitStack

import numpy as np

import concourse.bass as bass
from concourse import mybir

F32 = mybir.dt.float32
U32 = mybir.dt.uint32
BF16 = mybir.dt.bfloat16
ACT = mybir.ActivationFunctionType
ALU = mybir.AluOpType
AX = mybir.AxisListType

P = 128
D = 1024
KD = D // P
LP, LS = 1024, 256
T = LP + LS
NTP, NTS = LP // P, LS // P
NT = NTP + NTS
CHUNKS = [(0, 512), (512, 512), (1024, 256)]
HEADS, DH, DV = 4, 64, 128
ROT = DH // 4
HY = 512
HG = HY // P
EMB, FH = 33, 64
COL_K, COL_V, COL_HY = 512, 1024, 1536
COL_GA, COL_GB = 3072, 4096
NMEM = 256
XH, XD = 4, 256
NE, FF = 16, 1024
CP, CS = 2 * LP // NE, 2 * LS // NE
CE = CP + CS
EPS = 1e-6
LAM_INIT = 0.2
PI_LOW = 3.1415925
INV_2PI = float(np.float32(1 / (2 * np.pi)))
TWO_PI_A = 6.28125
TWO_PI_B = float(2 * np.pi - 6.28125)
ROUND = 12582912.0

V_MIX, V_X, V_MEM, V_FFN = 0, 8, 16, 24
V_CW, V_CB, V_FB, V_SUB, V_FREQ, V_B1, V_B2 = 32, 68, 80, 84, 85, 86, 87
NV = 88


def shape_tables():
    f = np.float32

    def order(n):
        return np.concatenate([np.arange(0, n, 2), np.arange(1, n, 2)])

    feats, decays = [], []
    bands = (EMB - 1) // 2
    lo, hi = np.log(1e-2) / 1.5, np.log(1e-2) / 0.3
    deltas = np.abs(np.linspace(lo, hi, HY).astype(f))
    for n in (LP, LS):
        t = np.linspace(0.0, 1.0, n).astype(f)
        w = (f(2.0 * np.pi) * np.arange(n).astype(f) / f(n)).astype(f)
        fr = np.linspace(1e-4, bands - 1, bands).astype(f)
        a = (fr[None, :] * w[:, None]).astype(f)
        z = np.concatenate([t[:, None], np.cos(a), -np.sin(a)], axis=1).astype(f)
        feats.append(z[order(n)])
        decays.append(np.exp(-t[:, None] * deltas[None, :]).astype(f)[order(n)])
    feat = np.ascontiguousarray(np.concatenate(feats).T)
    decay = np.ascontiguousarray(np.concatenate(decays).reshape(NT, P, HY).transpose(1, 0, 2))

    def transforms(n):
        k = 2 * np.arange(n // 2) + 1
        even, odd = np.arange(0, n, 2), np.arange(1, n, 2)
        return np.stack([
            g(np.pi * ((t[:, None] * k[None, :]) % (4 * n)) / (2 * n))
            for g, t in ((np.cos, even), (np.cos, odd), (np.sin, even), (np.sin, odd))
        ])

    def rows(m):
        kinds, n, w = m.shape
        return np.ascontiguousarray(m.reshape(kinds, n // P, P, w).transpose(2, 0, 1, 3).astype(f))

    tp, ts = transforms(LP), transforms(LS)
    back = [0, 2, 1, 3]
    inv = ROT // 2
    freq = (f(500000.0) ** (-np.arange(0, ROT, 2).astype(f) / f(ROT))).astype(f)
    ang = (np.arange(LP).astype(f)[None, :] * freq[:, None]).astype(f)
    cos, sin = np.ones((P, LP), f), np.zeros((P, LP), f)
    perm = np.zeros((P, P), f)
    for c in range(2):
        a = DH * c
        cos[a:a + inv], cos[a + inv:a + ROT] = np.cos(ang), np.cos(ang)
        sin[a:a + inv], sin[a + inv:a + ROT] = np.sin(ang), np.sin(ang)
        for d in range(inv):
            perm[a + inv + d, a + d] = -1.0
            perm[a + d, a + inv + d] = 1.0
    return {
        "feat": feat, "decay": decay,
        "fwd_p": rows(tp), "fwd_s": rows(ts),
        "inv_p": rows(tp.transpose(0, 2, 1)[back] / LP), "inv_s": rows(ts.transpose(0, 2, 1)[back] / LS),
        "rope_cos": cos, "rope_sin": sin, "perm": perm, "ident": np.eye(P, dtype=f),
    }


class Count:

    def __init__(self, eng, sem):
        self.eng, self.sem, self.base, self.n = eng, sem, 0, 0

    def inc(self, ins):
        ins.then_inc(self.sem, 1)
        self.n += 1

    def value(self):
        return self.base + self.n

    def wait(self):
        self.eng.wait_ge(self.sem, self.base + self.n)

    def enter(self, i, per):
        self.start, self.per = self.base + self.n, per
        self.base, self.n = i * per + (self.start - per), 0

    def leave(self, passes):
        assert self.n == self.per, (self.n, self.per)
        self.base, self.n = 0, self.start + passes * self.per


SEMS = """dve_step vec_zero vec_in vec_tr vec_ready const_in feat_in decay_in fwd_in inv_in
mlp_mm  arg_ready sin_ready h_mm h_dve tap_abs sums_ready h_pool norm_mm invn_ready
dft_mm dft_act dft_dve x_in_0 x_in_1 x_in_2 norm_act root_rec xn_ready xn_tr ut_ready
hy_in_0 hy_in_1 hy_in_2 hy_mm raw_ready pad_zero  conv_done z_ready z_tr zt_ready
inv_mm  inv_used hz_ready wv_in v_mm v_ready lam_in  lam_sum lam_exp lam_ready
wq_in wk_in rope_in qk_mm raw_qk pm_mm  q_roped k_roped k_zero
s_mm  smax_ready exp_ready  w_ready w_tr wt_ready pv_mm o_ready
 sub_sum sub_root sub_ready sub_tr at_ready
mg_in_0 mg_in_1 mg_mm mg_sig  m_ready wo_in xr_in wo_mm x1_ready
mem_in_0 mem_in_1 wxv_in vm_mm vm_ready xb_in_0 xb_in_1 xb_mm q_ready xk_ready
xs_mm  xmax_ready xexp_ready  xp_ready xp_tr pt_ready xo_mm ot_ready
wx_in_0 wx_in_1 xo2_mm x2_ready acc_out hn_out_0 hn_out_1 wr_in rt_mm  rt_low rt_exp aff_ready aff_tr
 slots_ready idx_tr idx_ready eg0 eu0 eg1 eu1 ed0 ed1 col_ready gather_p gather_s xe_tr xet_ready
gu_mm silu_ready he_ready scol_ready dn_mm y_out scatter_p scatter_s gain_in
fin_act fin_rec fin_ready fin_out""".split() + [f"fin_in_{t}" for t in range(NT // 2)]


def encoder_kernel(nc, a, out_p, out_s):
    def rows_of(p, s, t, n):
        return (p if t < n else s)[(t % n) * P:(t % n + 1) * P, :]

    x_rows = [rows_of(a["x_prompt"][0], a["x_sample"][0], t, NTP) for t in range(NT)]
    out_rows = [rows_of(out_p[0], out_s[0], t, NTP) for t in range(NT)]
    mem_rows = [rows_of(a["mem_prompt"][0], a["mem_sample"][0], t, 2) for t in range(4)]
    w_in = a["w_in"][0]
    acc = nc.dram_tensor("residual_rows", [T, D], F32, kind="Internal").ap()
    hn = nc.dram_tensor("normed_rows", [T, D], F32, kind="Internal").ap()
    acc_quarters = acc.rearrange("t (j n) -> (t j) n", j=4)

    with ExitStack() as ctx:
        sem = {n: ctx.enter_context(nc.semaphore(n)) for n in SEMS}
        arena = ctx.enter_context(nc.sbuf_tensor("arena", [P, 204 * 256], F32))
        PS = ctx.enter_context(nc.psum_tensor("banks", [P, 8, 512], F32))

        def at(kb, *dims):
            n = int(np.prod(dims))
            v = arena[:, int(kb * 256):int(kb * 256) + n]
            if len(dims) == 2:
                v = v.rearrange("p (a b) -> p a b", a=dims[0])
            if len(dims) == 3:
                v = v.rearrange("p (a b c) -> p a b c", a=dims[0], b=dims[1])
            return v

        def small(name, shape, dt=F32):
            return ctx.enter_context(nc.sbuf_tensor(name, shape, dt))

        vec, ident, perm = small("vec", [P, NV]), small("ident_sb", [P, P]), small("perm_sb", [P, P])
        ones, eps = small("ones", [P, 2]), small("eps", [P, 1])
        stat = small("stat", [P, 3, 16])
        invn = small("invn", [P, 2, HG])
        att = small("att", [P, 2, 4, 4])
        lam = small("lam", [P, 4])
        sub = small("sub", [P, 3, NT * HEADS])
        rw = small("rw", [P, KD, NE])
        idx_p, idx_s, idx_q = small("idx_p", [P, NE], U32), small("idx_s", [CS, NE], U32), small("idx_q", [P, NE], U32)
        gates = small("gates", [P, 2, NE])
        now_p, now_s = small("now_p", [P, 1], U32), small("now_s", [CS, 1], U32)
        turn = small("turn", [P, 1])
        out_p_idx, out_q_idx = small("out_p_idx", [P, 1], U32), small("out_q_idx", [P, 1], U32)

        UT = at(0, KD, T)
        SF, DF = at(0, NT, HY), at(20, NT, HY)
        DEC = at(60, NT, HY)
        KS = at(80, 5, 4, HY)
        TAP = at(80, 2, 2, HY)
        FWD, FWDS = at(120, 4, 4, 512), at(152, 4, P)
        FEAT, W3F, H1, H2 = at(154, T), at(159, 2 * HY), at(163, T), at(168, T)
        ARG, RND, W1F, W2F, VROW = at(173, T), at(178, T), at(183, P), at(183.5, P), at(184, P)
        HACC, HAB = at(186, 2, HY), at(192, 4, HY).rearrange("p (r s) c -> p r s c", r=2)
        XS = [at(182 + 4 * i, D) for i in range(3)]
        XN = [at(194 + 4 * i, D) for i in range(2)]
        SQJ = at(202, D // 2).bitcast(BF16)
        Z = at(40, HG, T)
        ZT = at(60, NT, HY)
        RAW, CX, CH = [at(166, LP + LS + 4), at(171.25, LP + LS + 4)], at(176.5, T), at(182, T)
        RAW0, CX0 = at(68, LP + LS + 4), at(73.25, T)
        HYW = [at(154 + 4 * i, KD, P) for i in range(3)] + [at(60, KD, P), at(64, KD, P)]
        TEF, TE, AB, TT = at(60, 2, HY), at(188, 2, HY), at(192, 4, HY), at(200, 2, HY)
        INV, INVS = at(154, 4, 4, 512), at(186, 4, P)
        V, AO, AT = at(80, NT, HY), at(60, NT, HY), at(100, HEADS, T)
        WV, COS, SIN = at(120, KD, HY), at(136, LP), at(140, LP)
        PP = [[at(120 + 8 * i + 4 * c, LP) for c in range(2)] for i in range(2)]
        WT = [at(144 + 4 * i, KD, P) for i in range(2)]
        WQ, WK = at(160, KD, P), at(164, KD, P)
        QKRAW, RT = [at(168, T), at(173, T)], at(178, T)
        QK = [[at(100 + 5 * i, T) for i in range(3)], [at(184 + 5 * i, T) for i in range(3)]]
        LAMV = at(152, 4, DH)
        SQ = at(120, NT, HY)
        MT = at(60, KD, T)
        MGW = [(at(160 + 12 * b, KD, P), at(164 + 12 * b, KD, P), at(168 + 12 * b, HG, P), at(170 + 12 * b, HG, P))
               for b in range(2)]
        SG, TM = at(144, 2, 2, HY), at(152, 2, 2, HY)
        WO = [at(120, KD, 512), at(184, KD, 512)]
        X = at(0, NT, D)
        U2T = at(100, KD, T)
        MEMT, MS = at(40, KD, 2 * NMEM), [at(56, D), at(96, D)]
        WXV, VM = at(60, KD, D), at(172, 4, D)
        XQW, XKW = [at(156 + 8 * b, KD, P) for b in range(2)], [at(160 + 8 * b, KD, P) for b in range(2)]
        QX, KX = at(60, KD, T), at(140, KD, 2 * NMEM)
        XP, PT = [at(156 + 4 * i, XH, NMEM) for i in range(2)], [at(164 + 4 * i, 2 * XH, P) for i in range(2)]
        OT = at(100, KD, T)
        WXO = [at(40, KD, 512), at(140, KD, 512)]
        HT = at(60, KD, T)
        LG, AF = at(156, NT, NE), at(157, T)[0:NE]
        VAL, IDX = at(162, CE)[0:NE], at(163, CE)[0:NE].bitcast(U32)
        SLOT_I, SLOT_V = at(164, P + CS + P)[0:NE], at(166, P + CS + P)[0:NE]
        RM = at(168, 2, 16)
        WG, WU, WD = [at(0, KD, 512), at(32, KD, 512)], [at(16, KD, 512), at(48, KD, 512)], [at(64, KD, 512), at(80, KD, 512)]
        XE, XES = at(100, D), at(104, D)[0:CS]
        XET, HE = at(112, KD, CE), at(117, KD, CE)
        SL = at(122, 2, CE)
        YP, YS = at(124, D), at(128, 256)
        GROW = at(130, D)
        FIN = [at(4 * t, D) for t in range(NT)]

        def blocked(dram, c0, n):
            return dram[:, bass.ds(c0, n)].rearrange("(k p) c -> p k c", p=P)

        def bank4(b):
            return PS[:, b, :].rearrange("p (a c) -> p a c", a=4)

        def wide(v, n):
            return v.unsqueeze(2).to_broadcast([v.shape[0], v.shape[1], n])

        def taps_at(r):
            before = 2 * r + (r > 0) + (r > NTP)
            return before + 2, before + 2 + (r in (0, NTP))

        def taps_summed(r):
            return 2 * (r + 1) - 1 - (r >= NTP)

        def dft_read(q):
            return (4 * q if q < 5 else 20 + 20 * (q - 5)) + 4

        DFT_ALL = 20 + 5 * 20
        N_X, N_MEM, N_FFN = NT, 2 * NT, 2 * NT + 4
        NORMED = N_FFN + NT
        tiles = [slice(t * P, (t + 1) * P) for t in range(NT)]

        def keys(i):
            return (0, LP) if i < NTP else (LP, LS)

        def w_blocks(i):
            return (2 * i if i < NTP else 2 * NTP + (i - NTP)), (2 if i < NTP else 1)

        W_HEAD = 2 * NTP + NTS
        SUB_BANKS = (2, 3, 6, 7)
        UNITS = HEADS * NT

        def turned(u):
            before, groups = w_blocks(u % NT)
            return W_HEAD * (u // NT) + before, groups

        RAW_JOBS = [[(0, 0)], [(1, 0)], [(0, 1)], [(1, 1)], [(0, 2), (1, 2)]]
        TURN_JOBS = [[(0, 0)], [(1, 0)], [(1, 1)], [(0, 1)], [(0, 2), (1, 2)]]

        def job_bank(h, j):
            return 7 if h else j % 5

        def roped(h, j):
            done = [part for job in TURN_JOBS[:j] for part, _ in job]
            return 3 * h + done.count(0), 6 * h + 2 * done.count(1)
        block = ctx.enter_context(nc.Block())

        @block.sync
        def _(sp):
            sp.wait_ge(sem["vec_zero"], 1)
            n_vec = 0
            for row, v, r in ((V_MIX, a["norm_mix"], 8), (V_X, a["norm_x"], 8), (V_MEM, a["norm_mem"], 8),
                              (V_FFN, a["norm_ffn"], 8), (V_CB, a["hy_conv_b"], 12), (V_FB, a["filt_bias"], 4),
                              (V_SUB, a["subln"], 1)):
                sp.dma_start(VROW[row:row + r, :], v[0].rearrange("(r c) -> r c", c=P)).then_inc(sem["vec_in"], 16)
            sp.dma_start(VROW[V_CW:V_CW + 36, :], a["hy_conv_w"][0].rearrange("k (r c) -> (k r) c", c=P)).then_inc(sem["vec_in"], 16)
            for row, v in ((V_FREQ, a["filt_freq"]), (V_B1, a["filt_b1"]), (V_B2, a["filt_b2"])):
                sp.dma_start(VROW[row:row + 1, 0:FH], v).then_inc(sem["vec_in"], 16)
            sp.dma_start(ident[:, :], a["ident"]).then_inc(sem["const_in"], 16)
            sp.dma_start(perm[:, :], a["perm"]).then_inc(sem["const_in"], 16)
            sp.dma_start(FEAT[0:EMB, :], a["feat"]).then_inc(sem["feat_in"], 16)
            sp.dma_start(W1F[0:EMB, 0:FH], a["filt_w1"][0]).then_inc(sem["feat_in"], 16)
            sp.dma_start(W2F[0:FH, 0:FH], a["filt_w2"][0]).then_inc(sem["feat_in"], 16)
            sp.dma_start(W3F[0:FH, :], a["filt_w3"][0]).then_inc(sem["feat_in"], 16)
            sp.dma_start(DEC, a["decay"]).then_inc(sem["decay_in"], 16)
            sp.dma_start(FWD, a["fwd_p"]).then_inc(sem["fwd_in"], 16)
            sp.dma_start(FWDS, a["fwd_s"].rearrange("p a b c -> p (a b) c")).then_inc(sem["fwd_in"], 16)
            sp.dma_start(rw[:, :, :], blocked(a["w_router"][0], 0, NE)).then_inc(sem["wr_in"], 16)
            sp.wait_ge(sem["norm_mm"], 1)
            for t in range(NT):
                if t >= 3:
                    sp.wait_ge(sem["xn_ready"], t - 2)
                sp.dma_start(XS[t % 3], x_rows[t]).then_inc(sem[f"x_in_{t % 3}"], 16)
            sp.wait_ge(sem["h_mm"], NT)
            for b in range(2 * HG):
                if b >= 3:
                    sp.wait_ge(sem["hy_mm"], 3 * (b - 2))
                c0 = COL_HY + HY * (1 + b % 2) + P * (b // 2)
                sp.dma_start(HYW[b % 3], blocked(w_in, c0, P)).then_inc(sem[f"hy_in_{b % 3}"], 16)
            sp.wait_ge(sem["z_ready"], HG)
            sp.dma_start(INV, a["inv_p"]).then_inc(sem["inv_in"], 16)
            sp.dma_start(INVS, a["inv_s"].rearrange("p a b c -> p (a b) c")).then_inc(sem["inv_in"], 16)
            sp.wait_ge(sem["dft_mm"], 40)
            for g in range(HG):
                if g == 2:
                    sp.dma_start(WV, blocked(w_in, COL_V, HY)).then_inc(sem["wv_in"], 16)
                    sp.dma_start(COS, a["rope_cos"]).then_inc(sem["rope_in"], 16)
                    sp.dma_start(SIN, a["rope_sin"]).then_inc(sem["rope_in"], 16)
                if g >= 2:
                    sp.wait_ge(sem["hy_mm"], 3 * (2 * HG + g - 1))
                sp.dma_start(HYW[3 + g % 2], blocked(w_in, COL_HY + P * g, P)).then_inc(sem[f"hy_in_{g % 2}"], 16)
            sp.wait_ge(sem["inv_mm"], 3 * HG)
            for h in range(HEADS):
                if h:
                    sp.wait_ge(sem["qk_mm"], 5 * h)
                sp.dma_start(WQ, blocked(w_in, h * P, P)).then_inc(sem["wq_in"], 16)
                sp.dma_start(WK, blocked(w_in, COL_K + h * P, P)).then_inc(sem["wk_in"], 16)

            def merge_load(B, b):
                ga, gb, wa, wh = MGW[b]
                s = sem[f"mg_in_{b}"]
                sp.dma_start(ga, blocked(w_in, B * P + COL_GA, P)).then_inc(s, 16)
                sp.dma_start(gb, blocked(w_in, B * P + COL_GB, P)).then_inc(s, 16)
                sp.dma_start(wa, blocked(a["w_br_attn"][0], B * P, P)).then_inc(s, 16)
                sp.dma_start(wh, blocked(a["w_br_hyena"][0], B * P, P)).then_inc(s, 16)

            sp.wait_ge(sem["q_roped"], 3 * HEADS)
            sp.wait_ge(sem["k_roped"], 6 * HEADS)
            merge_load(0, 0)
            merge_load(1, 1)
            sp.wait_ge(sem["s_mm"], 2 * UNITS)
            sp.dma_start(WO[1], blocked(a["w_out"][0], 512, 512)).then_inc(sem["wo_in"], 16)
            sp.wait_ge(sem["sub_ready"], 1)
            sp.dma_start(WO[0], blocked(a["w_out"][0], 0, 512)).then_inc(sem["wo_in"], 16)
            with sp.Fori(1, KD // 2) as c:
                for b in range(2):
                    sp.wait_ge(sem["mg_mm"], c * 6 + (3 * b - 3))
                    merge_load(c * 2 + b, b)
            sp.wait_ge(sem["mg_mm"], 3 * KD)
            sp.dma_start(X[:, 0:NTP, :], a["x_prompt"][0].rearrange("(t p) d -> p t d", p=P)).then_inc(sem["xr_in"], 16)
            sp.dma_start(X[:, NTP:NT, :], a["x_sample"][0].rearrange("(t p) d -> p t d", p=P)).then_inc(sem["xr_in"], 16)
            sp.wait_ge(sem["wo_mm"], 2 * NT)
            sp.dma_start(MS[0], mem_rows[0]).then_inc(sem["mem_in_0"], 16)
            sp.dma_start(MS[1], mem_rows[1]).then_inc(sem["mem_in_1"], 16)
            sp.dma_start(WXV, blocked(a["w_xkv"][0], D, D)).then_inc(sem["wxv_in"], 16)

            def xq_load(B, b):
                sp.dma_start(XQW[b], blocked(a["w_xq"][0], B * P, P)).then_inc(sem[f"xb_in_{b}"], 16)
                sp.dma_start(XKW[b], blocked(a["w_xkv"][0], B * P, P)).then_inc(sem[f"xb_in_{b}"], 16)

            xq_load(0, 0)
            xq_load(1, 1)
            for m in (2, 3):
                sp.wait_ge(sem["xn_ready"], N_MEM + m - 1)
                sp.dma_start(MS[m % 2], mem_rows[m]).then_inc(sem[f"mem_in_{m % 2}"], 16)
            with sp.Fori(1, KD // 2) as c:
                for b in range(2):
                    sp.wait_ge(sem["xb_mm"], c * 8 + (4 * b - 4))
                    xq_load(c * 2 + b, b)
            sp.wait_ge(sem["xb_mm"], 4 * KD)
            sp.dma_start(WXO[0], blocked(a["w_xo"][0], 0, 512)).then_inc(sem["wx_in_0"], 16)
            sp.wait_ge(sem["xs_mm"], NT)
            sp.dma_start(WXO[1], blocked(a["w_xo"][0], 512, 512)).then_inc(sem["wx_in_1"], 16)
            for t in range(NT):
                sp.wait_ge(sem["x2_ready"], NT + t + 1)
                sp.dma_start(acc[tiles[t], :], X[:, t, :]).then_inc(sem["acc_out"], 16)
                sp.wait_ge(sem["xn_ready"], N_FFN + t + 1)
                sp.dma_start(hn[tiles[t], :], XN[t % 2]).then_inc(sem[f"hn_out_{t % 2}"], 16)
            sp.wait_ge(sem["acc_out"], 16 * NT)
            sp.wait_ge(sem["rt_mm"], NT)

            def expert_load(e, first):
                halves = (("eg0", WG[0], "w_exp_gate", 0), ("eu0", WU[0], "w_exp_up", 0),
                          ("eg1", WG[1], "w_exp_gate", 512), ("eu1", WU[1], "w_exp_up", 512),
                          ("ed0", WD[0], "w_exp_down", 0), ("ed1", WD[1], "w_exp_down", 512))
                for n, (s, dst, w, c0) in enumerate(halves):
                    if not first and n in (0, 2):
                        sp.wait_ge(sem["gu_mm"], e * 8 + (2 * n - 4))
                    if not first and n == 4:
                        sp.wait_ge(sem["dn_mm"], e * 3)
                    src = a[w][0][bass.ds(e, 1), :, c0:c0 + 512].rearrange("e (k p) c -> p (e k) c", p=P)
                    sp.dma_start(dst, src).then_inc(sem[s], 16)

            expert_load(0, True)
            sp.dma_start(GROW, a["norm_final"].unsqueeze(0).to_broadcast([P, D])).then_inc(sem["gain_in"], 16)
            with sp.Fori(1, NE) as e:
                expert_load(e, False)
            sp.wait_ge(sem["gu_mm"], 8 * NE)
            sp.wait_ge(sem["scatter_p"], 16 * NE)
            sp.wait_ge(sem["scatter_s"], 16 * NE)
            for t in range(0, NT, 2):
                sp.dma_start(at(4 * t, 2, D), acc[t * P:(t + 2) * P, :].rearrange("(t p) d -> p t d", p=P)).then_inc(sem[f"fin_in_{t // 2}"], 16)
            for t in range(NT):
                sp.wait_ge(sem["fin_ready"], t + 1)
                sp.dma_start(out_rows[t], FIN[t]).then_inc(sem["fin_out"], 16)
            sp.wait_ge(sem["fin_out"], 16 * NT)

        @block.gpsimd
        def _(pool):
            taps = Count(pool, sem["h_pool"])
            for r in range(NT):
                pool.wait_ge(sem["h_dve"], taps_at(r)[1])
                taps.inc(pool.tensor_tensor(SF[:, r, :], TAP[:, r % 2, 0, :], TAP[:, r % 2, 1, :], ALU.add))
                taps.inc(pool.tensor_tensor(DF[:, r, :], TAP[:, r % 2, 0, :], TAP[:, r % 2, 1, :], ALU.subtract))

            pool.wait_ge(sem["dft_mm"], 40)
            for n, v in enumerate(("lambda_q1", "lambda_k1", "lambda_q2", "lambda_k2")):
                pool.dma_start(LAMV[:, n, :], a[v].to_broadcast([P, DH])).then_inc(sem["lam_in"], 16)

            def gather(e, first):
                if not first:
                    pool.wait_ge(sem["gather_p"], e * 16)
                    pool.wait_ge(sem["gather_s"], e * 16)
                pool.tensor_copy(now_p[:, :], idx_p[:, bass.ds(e, 1)]).then_inc(sem["col_ready"], 1)
                pool.tensor_copy(now_s[:, :], idx_s[:, bass.ds(e, 1)]).then_inc(sem["col_ready"], 1)
                if not first:
                    pool.wait_ge(sem["xe_tr"], e * 3)
                pool.wait_ge(sem["col_ready"], e * 2 + 2)
                pool.tensor_tensor(turn[:, :], ones[:, 0:1], ones[:, 0:1], ALU.mult)
                pool.indirect_dma_start(XE, None, hn, bass.IndirectOffsetOnAxis(ap=now_p[:, 0:1], axis=0)).then_inc(sem["gather_p"], 16)
                pool.indirect_dma_start(XES, None, hn, bass.IndirectOffsetOnAxis(ap=now_s[:, 0:1], axis=0)).then_inc(sem["gather_s"], 16)

            def scatter(e, first):
                if not first:
                    pool.wait_ge(sem["scatter_p"], e * 16)
                    pool.wait_ge(sem["scatter_s"], e * 16)
                pool.tensor_copy(out_p_idx[:, :], idx_p[:, bass.ds(e, 1)]).then_inc(sem["scol_ready"], 1)
                pool.tensor_copy(out_q_idx[:, :], idx_q[:, bass.ds(e, 1)]).then_inc(sem["scol_ready"], 1)
                pool.wait_ge(sem["scol_ready"], e * 2 + 2)
                pool.wait_ge(sem["y_out"], e * 3 + 3)
                pool.tensor_tensor(turn[:, :], ones[:, 0:1], ones[:, 0:1], ALU.mult)
                pool.indirect_dma_start(acc, bass.IndirectOffsetOnAxis(ap=out_p_idx[:, 0:1], axis=0), YP, None,
                                        compute_op=ALU.add).then_inc(sem["scatter_p"], 16)
                pool.indirect_dma_start(acc_quarters, bass.IndirectOffsetOnAxis(ap=out_q_idx[:, 0:1], axis=0), YS, None,
                                        compute_op=ALU.add).then_inc(sem["scatter_s"], 16)

            pool.wait_ge(sem["idx_ready"], 5)
            pool.wait_ge(sem["hn_out_0"], 16 * NT // 2)
            pool.wait_ge(sem["hn_out_1"], 16 * NT // 2)
            pool.wait_ge(sem["acc_out"], 16 * NT)
            gather(0, True)
            gather(1, False)
            scatter(0, True)
            with pool.Fori(1, NE - 1) as e:
                gather(e + 1, False)
                scatter(e, False)
            scatter(NE - 1, False)

        @block.tensor
        def _(pe):
            def product(out, pairs):
                for n, (l, r) in enumerate(pairs):
                    last = pe.matmul(out, l, r, start=(n == 0), stop=(n == len(pairs) - 1))
                return last

            def wait(name, v):
                pe.wait_ge(sem[name], v)

            wait("vec_in", 16 * 11)
            wait("const_in", 32)
            pe.transpose(PS[:, 0, 0:NV], VROW[0:NV, :], ident[0:NV, 0:NV]).then_inc(sem["vec_tr"], 1)
            wait("feat_in", 64)
            wait("vec_ready", 1)
            for layer, (w, h) in enumerate(((W1F, FEAT), (W2F, H1))):
                if layer:
                    wait("sin_ready", 1)
                for n, (c0, cn) in enumerate(CHUNKS):
                    product(PS[:, n, 0:cn], [(w, h[:, c0:c0 + cn])]).then_inc(sem["mlp_mm"], 1)
            wait("sin_ready", 2)
            for r in range(NT):
                if r >= 4:
                    wait("h_dve", taps_at(r - 4)[0])
                b = 2 * (r % 4)
                product(PS[:, b, :], [(H2[:, tiles[r]], W3F[:, 0:HY])])
                product(PS[:, b + 1, :], [(H2[:, tiles[r]], W3F[:, HY:2 * HY])]).then_inc(sem["h_mm"], 1)
            wait("sums_ready", 1)
            for s in range(2):
                for g in range(HG):
                    last = product(PS[:, 0, 4 * s + g:4 * s + g + 1], [(HACC[:, s, tiles[g]], ones[:, 0:1])])
            last.then_inc(sem["norm_mm"], 1)

            def dft(q, even, odd):
                j = q % 5
                b = 4 * (q % 2)
                if q >= 2:
                    wait("dft_dve", dft_read(q - 2))
                for kind in (0, 2, 1, 3):
                    src = (even, odd)[kind % 2][kind // 2]
                    if j < 4:
                        pairs = [(FWD[:, kind, m, tiles[j]], src[:, 4 * (kind % 2) + m, :]) for m in range(4)]
                    else:
                        pairs = [(FWDS[:, kind, :], src[:, NTP + kind % 2, :])]
                    product(PS[:, b + kind, :], pairs).then_inc(sem["dft_mm"], 1)

            wait("h_pool", 2 * NT)
            wait("fwd_in", 32)
            wait("invn_ready", 1)
            for q in range(5):
                dft(q, (SF, DF), (SF, DF))

            def turn_rows(q):
                wait("xn_ready", q + 1)
                for half in range(2):
                    if q >= 1:
                        wait("ut_ready", 2 * (q - 1) + half + 1)
                    for k in range(4):
                        last = pe.transpose(PS[:, 6 + half, k * P:(k + 1) * P], XN[q % 2][:, tiles[4 * half + k]], ident[:, :])
                    last.then_inc(sem["xn_tr"], 1)

            wait("dft_dve", dft_read(3))
            for t in range(NT):
                turn_rows(t)

            def hyena_project(b, slot, arrived, first_bank):
                wait(f"hy_in_{arrived[0]}", arrived[1])
                for n, (c0, cn) in enumerate(CHUNKS):
                    product(PS[:, first_bank + n, 0:cn], [(HYW[slot][:, k, :], UT[:, k, c0:c0 + cn]) for k in range(KD)]
                            ).then_inc(sem["hy_mm"], 1)

            def turn_z(g):
                wait("z_ready", g + 1)
                for part, (n0, n1) in enumerate(((0, 4), (4, 8), (8, 10))):
                    if part == 2:
                        wait("zt_ready", 3 * g + 1)
                    elif g >= 1:
                        wait("zt_ready", 3 * g if part == 0 else 3 * g - 1)
                    for r in range(n0, n1):
                        base, odd = (256 * (r % 4), r // 4) if r < NTP else (LP, r - NTP)
                        last = pe.transpose(PS[:, 6 + part % 2, (r - n0) * P:(r - n0 + 1) * P],
                                            Z[:, g, base + odd:base + 256:2], ident[:, :])
                    last.then_inc(sem["z_tr"], 1)

            wait("dft_dve", dft_read(4))
            wait("ut_ready", 2 * NT)
            for b in range(2 * HG):
                if b >= 2:
                    wait("raw_ready", b - 1)
                hyena_project(b, b % 3, (b % 3, 16 * (b // 3 + 1)), 3 * (b % 2))
                if b >= 2 and b % 2 == 0:
                    turn_z(b // 2 - 1)
            turn_z(HG - 1)
            wait("zt_ready", 3 * HG)
            wait("raw_ready", 2 * HG)
            for q in range(5, 10):
                dft(q, (ZT, ZT), (ZT, ZT))
            wait("dft_dve", dft_read(8))
            loads = [3, 3]
            for g in range(HG):
                loads[g % 2] += 1
                if g >= 1:
                    wait("raw_ready", 2 * HG + g)
                hyena_project(2 * HG + g, 3 + g % 2, (g % 2, 16 * loads[g % 2]), 0)
                if g == 0:
                    wait("dft_dve", DFT_ALL)
                    wait("inv_in", 32)
                else:
                    wait("inv_used", g)
                for odd in range(2):
                    product(PS[:, 3 + odd, :], [(KS[:, j, 2 * odd + s, tiles[g]], INV[:, 2 * odd + s, j, :])
                                                for s in range(2) for j in range(4)]).then_inc(sem["inv_mm"], 1)
                for odd in range(2):
                    last = product(PS[:, 5, odd * P:(odd + 1) * P],
                                   [(KS[:, 4, 2 * odd + s, tiles[g]], INVS[:, 2 * odd + s, :]) for s in range(2)])
                last.then_inc(sem["inv_mm"], 1)
            def project_job(h, j):
                if j == 0:
                    wait("wq_in", 16 * (h + 1))
                    wait("wk_in", 16 * (h + 1))
                    if h == 0:
                        wait("raw_ready", 3 * HG)
                        wait("inv_used", HG)
                if h and (h > 1 or j):
                    if j:
                        wait("raw_qk", 5 * h + j)
                    else:
                        wait("q_roped", 3 * h)
                        wait("k_roped", 6 * h)
                for n, (part, chunk) in enumerate(RAW_JOBS[j]):
                    c0, cn = CHUNKS[chunk]
                    last = product(PS[:, job_bank(h, j), n * cn:(n + 1) * cn],
                                   [((WQ, WK)[part][:, k, :], UT[:, k, c0:c0 + cn]) for k in range(KD)])
                last.then_inc(sem["qk_mm"], 1)

            def turn_job(h, j):
                wait("raw_qk", 5 * (h + 1))
                if h and j:
                    wait("q_roped", roped(h, j)[0])
                    wait("k_roped", roped(h, j)[1])
                for n, (part, chunk) in enumerate(TURN_JOBS[j]):
                    c0, cn = CHUNKS[chunk]
                    last = product(PS[:, job_bank(h, j), n * cn:(n + 1) * cn], [(perm[:, :], QKRAW[part][:, c0:c0 + cn])])
                last.then_inc(sem["pm_mm"], 1)

            def scores(u):
                h, i = u // NT, u % NT
                q, *both = QK[h % 2]
                k0, kn = keys(i)
                if i in (0, 4, NTP):
                    ready = roped(h, {0: 3, 4: 4, NTP: 5}[i])
                    wait("q_roped", ready[0])
                    wait("k_roped", ready[1])
                for c, kk in enumerate(both):
                    if u >= 1:
                        wait("exp_ready", 2 * (u - 1) + c + 1)
                    for n in range(0, kn, 512):
                        m = min(512, kn - n)
                        last = product(PS[:, 2 * c + n // 512, 0:m], [(q[:, tiles[i]], kk[:, k0 + n:k0 + n + m])])
                    last.then_inc(sem["s_mm"], 1)

            def turn_map(u):
                before, groups = turned(u)
                wait("w_ready", u + 1)
                for g in range(groups):
                    if u >= 1:
                        wait("wt_ready", turned(u - 1)[0] + min(g + 1, turned(u - 1)[1]))
                    for m in range(4 * g, min(4 * g + 4, keys(u % NT)[1] // P)):
                        last = pe.transpose(PS[:, 4 + g, (m % 4) * P:(m % 4 + 1) * P], PP[u % 2][0][:, tiles[m]], ident[:, :])
                    last.then_inc(sem["w_tr"], 1)

            def values(u):
                h, i = u // NT, u % NT
                k0, kn = keys(i)
                before, groups = turned(u)
                if u >= 1:
                    wait("o_ready", u)
                wait("wt_ready", before + groups)
                product(PS[:, 6, (u % 4) * P:(u % 4 + 1) * P],
                        [(WT[u % 2][:, m, :], V[:, k0 // P + m, tiles[h]]) for m in range(kn // P)]).then_inc(sem["pv_mm"], 1)

            for j in range(5):
                project_job(0, j)
            wait("wv_in", 16)
            for t in range(NT):
                if t >= 2:
                    wait("v_ready", t - 1)
                product(PS[:, 6 + t % 2, :], [(UT[:, k, tiles[t]], WV[:, k, :]) for k in range(KD)]).then_inc(sem["v_mm"], 1)
            for j in range(5):
                turn_job(0, j)
            wait("q_roped", 3)
            wait("k_roped", 6)
            wait("v_ready", NT)
            scores(0)
            for u in range(UNITS):
                if u + 1 < UNITS:
                    scores(u + 1)
                if u >= 1:
                    values(u - 1)
                turn_map(u)
                h, i = u // NT + 1, u % NT
                if h < HEADS:
                    project_job(h, i) if i < 5 else turn_job(h, i - 5)
            values(UNITS - 1)

            def merge_gates(b, n):
                s, (c0, cn) = 4 * ((b + n) % 2), CHUNKS[n]
                for part in range(2):
                    product(PS[:, s + part, 0:cn], [(MGW[b][part][:, k, :], UT[:, k, c0:c0 + cn]) for k in range(KD)])

            wait("mg_in_0", 64)
            wait("exp_ready", 2 * UNITS)
            merge_gates(0, 0)
            wait("wt_ready", W_HEAD * HEADS)
            merge_gates(0, 1)
            wait("o_ready", UNITS)
            wait("sub_ready", 1)
            for q in range(3 * HEADS):
                h, n = q // 3, q % 3
                if q >= 4:
                    wait("at_ready", q - 3)
                for t in range(4 * n, min(4 * n + 4, NT)):
                    last = pe.transpose(PS[:, SUB_BANKS[q % 4], (t % 4) * P:(t % 4 + 1) * P], AO[:, t, tiles[h]], ident[:, :])
                last.then_inc(sem["sub_tr"], 1)
            wait("at_ready", 3 * HEADS)

            def merge(B, b, first):
                wait(f"mg_in_{b}", (B - b) * 32 + 64)
                wa, wh = MGW[b][2:]
                for n, (c0, cn) in enumerate(CHUNKS):
                    s = 4 * ((b + n) % 2)
                    if not (first and 3 * b + n < 2):
                        wait("m_ready", B * 3 + (n - 1))
                    if not (first and 3 * b + n < 2):
                        merge_gates(b, n)
                    product(PS[:, s + 2, 0:cn], [(wa[:, k, :], AT[:, k, c0:c0 + cn]) for k in range(HG)])
                    product(PS[:, s + 3, 0:cn], [(wh[:, k, :], Z[:, k, c0:c0 + cn]) for k in range(HG)]).then_inc(sem["mg_mm"], 1)

            wait("hz_ready", HG)
            merge(0, 0, True)
            merge(1, 1, True)
            with pe.Fori(1, KD // 2) as c:
                for b in range(2):
                    merge(c * 2 + b, b, False)
            wait("m_ready", 3 * KD)
            wait("wo_in", 32)
            for q in range(2 * NT):
                t, n = q // 2, q % 2
                if q >= 6:
                    wait("x1_ready", q - 5)
                product(PS[:, q % 6, :], [(MT[:, k, tiles[t]], WO[n][:, k, :]) for k in range(KD)]
                        ).then_inc(sem["wo_mm"], 1)
            for t in range(NT):
                turn_rows(N_X + t)
            for m in range(4):
                turn_rows(N_MEM + m)
            wait("ut_ready", 2 * N_FFN)
            wait("x1_ready", 2 * NT)
            wait("wxv_in", 16)
            for q in range(8):
                m, n = q // 2, q % 2
                if q >= 6:
                    wait("vm_ready", q - 5)
                product(PS[:, q % 6, :], [(MEMT[:, k, tiles[m]], WXV[:, k, n * 512:(n + 1) * 512]) for k in range(KD)]
                        ).then_inc(sem["vm_mm"], 1)

            def cross_project(B, b, first):
                wait(f"xb_in_{b}", (B - b) * 16 + 32)
                if first:
                    wait("vm_ready", 8)
                else:
                    wait("q_ready", B * 3 - 3)
                    wait("xk_ready", B - 1)
                for n, (c0, cn) in enumerate(CHUNKS):
                    product(PS[:, 4 * b + n, 0:cn], [(XQW[b][:, k, :], U2T[:, k, c0:c0 + cn]) for k in range(KD)]
                            ).then_inc(sem["xb_mm"], 1)
                product(PS[:, 4 * b + 3, :], [(XKW[b][:, k, :], MEMT[:, k, :]) for k in range(KD)]).then_inc(sem["xb_mm"], 1)

            cross_project(0, 0, True)
            cross_project(1, 1, True)
            with pe.Fori(1, KD // 2) as c:
                for b in range(2):
                    cross_project(c * 2 + b, b, False)

            def cross_scores(i):
                m0 = 0 if i < NTP else NMEM
                if i >= 2:
                    wait("xexp_ready", 4 * (i - 1))
                for hx in range(XH):
                    last = product(PS[:, 2 * (i % 2) + hx // 2, (hx % 2) * NMEM:(hx % 2 + 1) * NMEM],
                                   [(QX[:, 2 * hx + j, tiles[i]], KX[:, 2 * hx + j, m0:m0 + NMEM]) for j in range(2)])
                last.then_inc(sem["xs_mm"], 1)

            def cross_turn(i):
                wait("xp_ready", i + 1)
                for half in range(2):
                    if i >= 1:
                        wait("pt_ready", 2 * (i - 1) + half + 1)
                    for o in range(4 * half, 4 * half + 4):
                        last = pe.transpose(PS[:, 4 + half, (o % 4) * P:(o % 4 + 1) * P],
                                            XP[i % 2][:, o // 2, (o % 2) * P:(o % 2 + 1) * P], ident[:, :])
                    last.then_inc(sem["xp_tr"], 1)

            def cross_values(i):
                m0 = 0 if i < NTP else 2
                wait("pt_ready", 2 * i + 2)
                for half in range(2):
                    if i >= 1:
                        wait("ot_ready", 2 * (i - 1) + half + 1)
                    for o in range(4 * half, 4 * half + 4):
                        hx = o // 2
                        last = product(PS[:, 6 + half, (o % 4) * P:(o % 4 + 1) * P],
                                       [(VM[:, m0 + j, tiles[o]], PT[i % 2][:, 2 * hx + j, :]) for j in range(2)])
                    last.then_inc(sem["xo_mm"], 1)

            wait("q_ready", 3 * KD)
            wait("xk_ready", KD)
            cross_scores(0)
            for i in range(NT):
                if i + 1 < NT:
                    cross_scores(i + 1)
                if i >= 1:
                    cross_values(i - 1)
                cross_turn(i)
            cross_values(NT - 1)
            wait("ot_ready", 2 * NT)
            for q in range(2 * NT):
                n, t = q // NT, q % NT
                if q % NT == 0:
                    wait(f"wx_in_{n}", 16)
                if q >= 6:
                    wait("x2_ready", q - 5)
                product(PS[:, q % 6, :], [(OT[:, k, tiles[t]], WXO[n][:, k, :]) for k in range(KD)]).then_inc(sem["xo2_mm"], 1)

            def route(t):
                wait("ut_ready", 2 * (N_FFN + t) + 2)
                product(PS[:, 0, t * NE:(t + 1) * NE], [(HT[:, k, tiles[t]], rw[:, k, :]) for k in range(KD)]).then_inc(sem["rt_mm"], 1)

            wait("x2_ready", 2 * NT)
            wait("wr_in", 16)
            for t in range(NT):
                turn_rows(N_FFN + t)
                if t >= 1:
                    route(t - 1)
            route(NT - 1)
            wait("aff_ready", 1)
            for t in range(NT):
                last = pe.transpose(PS[0:NE, 1 + t // 4, (t % 4) * P:(t % 4 + 1) * P], LG[:, t, :], ident[:, :])
            last.then_inc(sem["aff_tr"], 1)
            wait("slots_ready", 1)
            pe.transpose(PS[:, 4, 0:NE], SLOT_I[:, 0:P], ident[0:NE, 0:NE])
            pe.transpose(PS[0:CS, 4, NE:2 * NE], SLOT_I[:, P:P + CS], ident[0:NE, 0:NE])
            pe.transpose(PS[:, 4, 2 * NE:3 * NE], SLOT_I[:, P + CS:2 * P + CS], ident[0:NE, 0:NE])
            pe.transpose(PS[:, 4, 3 * NE:4 * NE], SLOT_V[:, 0:P], ident[0:NE, 0:NE])
            pe.transpose(PS[:, 4, 4 * NE:5 * NE], SLOT_V[:, P + CS:2 * P + CS], ident[0:NE, 0:NE]).then_inc(sem["idx_tr"], 1)

            def turn_slots(e, first):
                wait("gather_p", e * 16 + 16)
                wait("gather_s", e * 16 + 16)
                if not first:
                    wait("xet_ready", e * 3)
                for half in range(2):
                    for k in range(4 * half, 4 * half + 4):
                        last = pe.transpose(PS[:, 3 + half, (k % 4) * P:(k % 4 + 1) * P], XE[:, tiles[k]], ident[:, :])
                    last.then_inc(sem["xe_tr"], 1)
                for k in range(KD):
                    last = pe.transpose(PS[:, 5, k * CS:(k + 1) * CS], XES[:, tiles[k]], ident[0:CS, 0:CS])
                last.then_inc(sem["xe_tr"], 1)

            def gate_up(e, first):
                wait("xet_ready", e * 3 + 3)
                for f in range(FF // P):
                    if f % 4 == 0:
                        wait(f"eg{f // 4}", e * 16 + 16)
                        wait(f"eu{f // 4}", e * 16 + 16)
                    if not (first and f < 3):
                        wait("he_ready", e * 8 + (f - 2))
                    for part, w in enumerate((WG, WU)):
                        last = product(PS[:, f % 3, part * CE:(part + 1) * CE],
                                       [(w[f // 4][:, k, tiles[f % 4]], XET[:, k, :]) for k in range(KD)])
                    last.then_inc(sem["gu_mm"], 1)

            def down(e, first, last_one):
                wait("he_ready", e * 8 + 8)
                if not first:
                    wait("y_out", e * 3)
                for n in range(2):
                    wait(f"ed{n}", e * 16 + 16)
                    product(PS[:, 6 + n, :], [(HE[:, f, 0:CP], WD[n][:, f, :]) for f in range(FF // P)]).then_inc(sem["dn_mm"], 1)
                if not last_one:
                    wait("xet_ready", e * 3 + 6)
                for f in range(FF // P):
                    for j in range(4):
                        last = pe.matmul(PS[CS * j:CS * (j + 1), 5, 0:256], HE[:, f, CP:CE],
                                         WD[j // 2][:, f, (j % 2) * 256:(j % 2 + 1) * 256],
                                         start=(f == 0), stop=(f == FF // P - 1), tile_position=(0, CS * j))
                last.then_inc(sem["dn_mm"], 1)

            turn_slots(0, True)
            gate_up(0, True)
            turn_slots(1, False)
            down(0, True, False)
            with pe.Fori(1, NE - 1) as e:
                gate_up(e, False)
                wait("y_out", e * 3)
                turn_slots(e + 1, False)
                down(e, False, False)
            gate_up(NE - 1, False)
            down(NE - 1, False, True)

        @block.scalar
        def _(act):
            for layer, h in enumerate((H1, H2)):
                act.wait_ge(sem["arg_ready"], layer + 1)
                act.activation(h, ARG, ACT.Sin).then_inc(sem["sin_ready"], 1)

            for r in range(NT):
                act.wait_ge(sem["h_dve"], taps_at(r)[1])
                if r >= 2:
                    act.wait_ge(sem["dve_step"], 14 + taps_summed(r - 2))
                act.activation(HAB[:, r % 2, :, :], TAP[:, r % 2, :, :], ACT.Abs).then_inc(sem["tap_abs"], 1)

            def spectra(q):
                for n, kind in enumerate((0, 2)):
                    act.wait_ge(sem["dft_mm"], 4 * q + n + 1)
                    if q >= 1:
                        act.wait_ge(sem["dft_dve"], dft_read(q - 1))
                    act.copy((TEF if q < 5 else TE)[:, n, :], PS[:, 4 * (q % 2) + kind, :]).then_inc(sem["dft_act"], 1)

            for q in range(5):
                spectra(q)

            steps = Count(act, sem["norm_act"])

            def normed(q, src):
                col = q % 16
                if q:
                    steps.wait()
                steps.inc(act.activation(SQJ, src, ACT.Square, accum_out=stat[:, 0, col:col + 1]))
                steps.wait()
                steps.inc(act.activation(stat[:, 1, col:col + 1], stat[:, 0, col:col + 1], ACT.Sqrt, scale=1.0 / D, bias=eps[:, 0:1]))

            act.wait_ge(sem["pad_zero"], 7)
            for t in range(NT):
                act.wait_ge(sem[f"x_in_{t % 3}"], 16 * (t // 3 + 1))
                normed(t, XS[t % 3])

            def raw_out(b, raw, first_bank):
                for n, off in enumerate((1, 513, LP + 3)):
                    cn = CHUNKS[n][1]
                    act.wait_ge(sem["hy_mm"], 3 * b + n + 1)
                    last = act.copy(raw[:, off:off + cn], PS[:, first_bank + n, 0:cn])
                last.then_inc(sem["raw_ready"], 1)

            def z_out(g):
                for part, (n0, n1) in enumerate(((0, 4), (4, 8), (8, 10))):
                    act.wait_ge(sem["z_tr"], 3 * g + part + 1)
                    act.copy(ZT[:, n0:n1, tiles[g]], bank4(6 + part % 2)[:, 0:n1 - n0, :]).then_inc(sem["zt_ready"], 1)

            for b in range(2 * HG):
                if b >= 2:
                    act.wait_ge(sem["conv_done"], b - 1)
                raw_out(b, RAW[b % 2], 3 * (b % 2))
                if b >= 2 and b % 2 == 0:
                    z_out(b // 2 - 1)
            z_out(HG - 1)
            for q in range(5, 10):
                spectra(q)
            act.wait_ge(sem["pad_zero"], 11)
            for g in range(HG):
                if g >= 1:
                    act.wait_ge(sem["conv_done"], 2 * HG + g)
                raw_out(2 * HG + g, RAW0, 0)
            act.wait_ge(sem["lam_sum"], 2)
            act.activation(lam[:, 2:4], lam[:, 0:2], ACT.Exp).then_inc(sem["lam_exp"], 1)
            def raw_out_job(h, j):
                act.wait_ge(sem["qk_mm"], 5 * h + j + 1)
                if h and j == 0:
                    act.wait_ge(sem["q_roped"], 3 * h)
                    act.wait_ge(sem["k_roped"], 6 * h)
                for n, (part, chunk) in enumerate(RAW_JOBS[j]):
                    c0, cn = CHUNKS[chunk]
                    last = act.copy(QKRAW[part][:, c0:c0 + cn], PS[:, job_bank(h, j), n * cn:(n + 1) * cn])
                last.then_inc(sem["raw_qk"], 1)

            def exps(u):
                kn = keys(u % NT)[1]
                for c in range(2):
                    act.wait_ge(sem["smax_ready"], 2 * u + c + 1)
                    if u >= 2:
                        act.wait_ge(sem["w_tr"], sum(turned(u - 2)))
                    s = PS[:, 2 * c:2 * c + 2, :].rearrange("p b n -> p (b n)")[:, 0:kn]
                    act.activation(PP[u % 2][c][:, 0:kn], s, ACT.Exp, bias=att[:, u % 2, 1, c:c + 1], scale=DH ** -0.5,
                                   accum_out=att[:, u % 2, 2, c:c + 1]).then_inc(sem["exp_ready"], 1)

            def maps(u):
                before, groups = turned(u)
                for g in range(groups):
                    act.wait_ge(sem["w_tr"], before + g + 1)
                    if u >= 2:
                        act.wait_ge(sem["pv_mm"], u - 1)
                    m = min(4, keys(u % NT)[1] // P - 4 * g)
                    act.copy(WT[u % 2][:, 4 * g:4 * g + m, :], bank4(4 + g)[:, 0:m, :]).then_inc(sem["wt_ready"], 1)

            for j in range(5):
                raw_out_job(0, j)
            for t in range(NT):
                act.wait_ge(sem["v_mm"], t + 1)
                act.copy(V[:, t, :], PS[:, 6 + t % 2, :]).then_inc(sem["v_ready"], 1)
            exps(0)
            for u in range(UNITS):
                if u + 1 < UNITS:
                    exps(u + 1)
                maps(u)
                if u // NT + 1 < HEADS and u % NT < 5:
                    raw_out_job(u // NT + 1, u % NT)
            act.wait_ge(sem["sub_sum"], 1)
            act.activation(sub[:, 1, :], sub[:, 0, :], ACT.Sqrt, scale=1.0 / DV, bias=eps[:, 0:1]).then_inc(sem["sub_root"], 1)

            def gates_out(B, b, first):
                for n, (c0, cn) in enumerate(CHUNKS):
                    s = (b + n) % 2
                    act.wait_ge(sem["mg_mm"], B * 3 + (n + 1))
                    if not (first and 3 * b + n < 2):
                        act.wait_ge(sem["m_ready"], B * 3 + (n - 1))
                    for part in range(2):
                        act.activation(SG[:, s, part, 0:cn], PS[:, 4 * s + part, 0:cn], ACT.Sigmoid).then_inc(sem["mg_sig"], 1)

            gates_out(0, 0, True)
            gates_out(1, 1, True)
            with act.Fori(1, KD // 2) as c:
                for b in range(2):
                    gates_out(c * 2 + b, b, False)
            for t in range(NT):
                act.wait_ge(sem["x1_ready"], 2 * t + 2)
                normed(N_X + t, X[:, t, :])
            for m in range(4):
                act.wait_ge(sem[f"mem_in_{m % 2}"], 16 * (m // 2 + 1))
                normed(N_MEM + m, MS[m % 2])

            def queries_out(B, b):
                for n, (c0, cn) in enumerate(CHUNKS):
                    act.wait_ge(sem["xb_mm"], B * 4 + (n + 1))
                    act.copy(QX[:, bass.ds(B, 1), c0:c0 + cn].rearrange("p a n -> p (a n)"), PS[:, 4 * b + n, 0:cn]).then_inc(sem["q_ready"], 1)

            queries_out(0, 0)
            queries_out(1, 1)
            with act.Fori(1, KD // 2) as c:
                for b in range(2):
                    queries_out(c * 2 + b, b)

            def cross_exps(i):
                act.wait_ge(sem["xmax_ready"], i + 1)
                if i >= 2:
                    act.wait_ge(sem["xp_tr"], 2 * (i - 1))
                for hx in range(XH):
                    act.activation(XP[i % 2][:, hx, :], PS[:, 2 * (i % 2) + hx // 2, (hx % 2) * NMEM:(hx % 2 + 1) * NMEM],
                                   ACT.Exp, bias=att[:, i % 2, 1, hx:hx + 1], scale=XD ** -0.5,
                                   accum_out=att[:, i % 2, 2, hx:hx + 1]).then_inc(sem["xexp_ready"], 1)

            cross_exps(0)
            for i in range(NT):
                if i + 1 < NT:
                    cross_exps(i + 1)
                for half in range(2):
                    act.wait_ge(sem["xp_tr"], 2 * i + half + 1)
                    if i >= 2:
                        act.wait_ge(sem["xo_mm"], 2 * (i - 1))
                    act.copy(PT[i % 2][:, 4 * half:4 * half + 4, :], bank4(4 + half)).then_inc(sem["pt_ready"], 1)
            for t in range(NT):
                act.wait_ge(sem["x2_ready"], NT + t + 1)
                normed(N_FFN + t, X[:, t, :])
            act.wait_ge(sem["rt_low"], 1)
            act.activation(LG, LG, ACT.Exp).then_inc(sem["rt_exp"], 1)

            def silus(e, first):
                for f in range(FF // P):
                    act.wait_ge(sem["gu_mm"], e * 8 + (f + 1))
                    if not (first and f < 2):
                        act.wait_ge(sem["he_ready"], e * 8 + (f - 1))
                    act.activation(SL[:, f % 2, :], PS[:, f % 3, 0:CE], ACT.Silu).then_inc(sem["silu_ready"], 1)

            silus(0, True)
            with act.Fori(1, NE) as e:
                silus(e, False)
            fin = Count(act, sem["fin_act"])
            for t in range(NT):
                act.wait_ge(sem[f"fin_in_{t // 2}"], 16)
                if t:
                    fin.wait()
                fin.inc(act.activation(SQJ, FIN[t], ACT.Square, accum_out=stat[:, 0, t:t + 1]))
                fin.wait()
                fin.inc(act.activation(stat[:, 1, t:t + 1], stat[:, 0, t:t + 1], ACT.Sqrt, scale=1.0 / D, bias=eps[:, 0:1]))

        @block.vector
        def _(dve):
            dve.memset(VROW, 0.0)
            dve.memset(at(154, 30 * 256), 0.0)
            dve.memset(ones[:, :], 1.0)
            dve.memset(eps[:, :], EPS).then_inc(sem["vec_zero"], 1)
            dve.wait_ge(sem["vec_tr"], 1)
            dve.tensor_copy(vec[:, :], PS[:, 0, 0:NV]).then_inc(sem["vec_ready"], 1)
            dve.wait_ge(sem["vec_ready"], 1)

            c = step = Count(dve, sem["dve_step"])
            for layer, vb in enumerate((V_B1, V_B2)):
                if layer:
                    dve.wait_ge(sem["sin_ready"], 1)
                for n, (c0, cn) in enumerate(CHUNKS):
                    dve.wait_ge(sem["mlp_mm"], 3 * layer + n + 1)
                    c.inc(dve.tensor_scalar(ARG[:, c0:c0 + cn], PS[:, n, 0:cn], vec[:, vb:vb + 1], vec[:, V_FREQ:V_FREQ + 1],
                                            ALU.add, ALU.mult))
                c.wait()
                c.inc(dve.tensor_scalar(RND, ARG, INV_2PI, ROUND, ALU.mult, ALU.add))
                c.wait()
                c.inc(dve.tensor_scalar(RND, RND, ROUND, None, ALU.subtract))
                for part in (TWO_PI_A, TWO_PI_B):
                    c.wait()
                    c.inc(dve.scalar_tensor_tensor(ARG, RND, -part, ARG, ALU.mult, ALU.add))
                c.wait()
                dve.tensor_scalar(ARG, ARG, PI_LOW, -PI_LOW, ALU.min, ALU.max).then_inc(sem["arg_ready"], 1)

            c = Count(dve, sem["h_dve"])
            dve.wait_ge(sem["decay_in"], 16)
            for r in range(NT):
                dve.wait_ge(sem["h_mm"], r + 1)
                if r >= 2:
                    dve.wait_ge(sem["h_pool"], 2 * (r - 1))
                c.wait() if r else None
                for side in range(2):
                    c.inc(dve.tensor_tensor(TAP[:, r % 2, side, :], PS[:, 2 * (r % 4) + side, :], DEC[:, r, :], ALU.mult))
                assert c.value() == taps_at(r)[0]
                c.wait()
                if r in (0, NTP):
                    c.inc(dve.memset(TAP[0:1, r % 2, 1, :], 0.0))
                    c.wait()
                assert c.value() == taps_at(r)[1]
                into = HACC[:, r // NTP, :]
                dve.wait_ge(sem["tap_abs"], r + 1)
                if r in (0, NTP):
                    step.inc(dve.tensor_tensor(into, HAB[:, r % 2, 0, :], HAB[:, r % 2, 1, :], ALU.add))
                else:
                    for side in range(2):
                        step.wait()
                        step.inc(dve.tensor_tensor(into, HAB[:, r % 2, side, :], into, ALU.add))
            step.wait()
            dve.memset(lam[:, :], 0.0).then_inc(sem["sums_ready"], 1)
            dve.wait_ge(sem["norm_mm"], 1)
            dve.reciprocal(invn[:, :, :].rearrange("p a b -> p (a b)"), PS[:, 0, 0:2 * HG]).then_inc(sem["invn_ready"], 1)
            for raw in RAW:
                for c0, c1 in ((0, 1), (LP + 1, LP + 3), (LP + LS + 3, LP + LS + 4)):
                    dve.memset(raw[:, c0:c1], 0.0).then_inc(sem["pad_zero"], 1)
            dve.memset(att[:, :, :, :], 0.0).then_inc(sem["pad_zero"], 1)

            spec = Count(dve, sem["dft_dve"])

            def butterflies(q, to):
                b = 4 * (q % 2)
                dve.wait_ge(sem["dft_act"], 2 * q + 2)
                dve.wait_ge(sem["dft_mm"], 4 * q + 4)
                te = TEF if q < 5 else TE
                spec.inc(dve.tensor_tensor(to[0], te[:, 0, :], PS[:, b + 1, :], ALU.add))
                spec.inc(dve.tensor_tensor(to[1], te[:, 0, :], PS[:, b + 1, :], ALU.subtract))
                spec.inc(dve.tensor_tensor(to[2], PS[:, b + 3, :], te[:, 1, :], ALU.add))
                spec.inc(dve.tensor_tensor(to[3], PS[:, b + 3, :], te[:, 1, :], ALU.subtract))
                assert spec.value() == dft_read(q)

            for q in range(5):
                if q:
                    spec.wait()
                butterflies(q, [KS[:, q, m, :] for m in range(4)])

            def scaled(q, src, stored):
                dve.wait_ge(sem["norm_act"], 2 * q + 2)
                col = slice(q % 16, q % 16 + 1)
                dve.reciprocal(stat[:, 2, col], stat[:, 1, col]).then_inc(sem["root_rec"], 1)
                if q >= 2:
                    dve.wait_ge(sem["xn_tr"], 2 * (q - 1))
                if stored and q >= N_FFN + 2:
                    dve.wait_ge(sem[f"hn_out_{q % 2}"], 16 * ((q - N_FFN) // 2))
                dve.wait_ge(sem["root_rec"], q + 1)
                dve.tensor_scalar(XN[q % 2], src, stat[:, 2, col], None, ALU.mult).then_inc(sem["xn_ready"], 1)

            def rows_in(q, dst, t, gain):
                for half in range(2):
                    dve.wait_ge(sem["xn_tr"], 2 * q + half + 1)
                    g = vec[:, gain + 4 * half:gain + 4 * half + 4]
                    dve.tensor_tensor(dst[:, 4 * half:4 * half + 4, tiles[t]], bank4(6 + half), wide(g, P), ALU.mult).then_inc(sem["ut_ready"], 1)

            def norm_stage(q0, n, src, dst, gain, stored=False):
                scaled(q0, src(0), stored)
                for t in range(n):
                    if t + 1 < n:
                        scaled(q0 + t + 1, src(t + 1), stored)
                    rows_in(q0 + t, dst, t, gain)

            dve.wait_ge(sem["dft_mm"], 20)
            norm_stage(0, NT, lambda t: XS[t % 3], UT, V_MIX)

            conv, done = step, Count(dve, sem["conv_done"])

            def short_conv(b, raw, to, channel_tile):
                dve.wait_ge(sem["raw_ready"], b + 1)
                col = [V_CW + 12 * k + channel_tile for k in range(3)]
                segs = ((1, 0, LP), (LP + 3, LP, LS))
                for off, o, n in segs:
                    conv.inc(dve.tensor_scalar(to[:, o:o + n], raw[:, off:off + n], vec[:, col[1]:col[1] + 1],
                                               vec[:, V_CB + channel_tile:V_CB + channel_tile + 1], ALU.mult, ALU.add))
                for k, shift in ((0, -1), (2, 1)):
                    for m, (off, o, n) in enumerate(segs):
                        conv.wait()
                        ins = dve.scalar_tensor_tensor(to[:, o:o + n], raw[:, off + shift:off + shift + n], vec[:, col[k]:col[k] + 1],
                                                       to[:, o:o + n], ALU.mult, ALU.add)
                        (done if k == 2 and m == 1 else conv).inc(ins)
                done.wait()

            for b in range(2 * HG):
                g = b // 2
                if b % 2 == 0:
                    short_conv(b, RAW[0], CX, HG + g)
                else:
                    short_conv(b, RAW[1], CH, 2 * HG + g)
                    dve.tensor_tensor(Z[:, g, :], CX, CH, ALU.mult).then_inc(sem["z_ready"], 1)
                    dve.wait_ge(sem["z_ready"], g + 1)

            A0, A1, B0, B1 = (AB[:, m, :] for m in range(4))
            T0, T1 = TT[:, 0, :], TT[:, 1, :]
            for q in range(5, 10):
                butterflies(q, [A0, A1, B0, B1])
                P0, P1, Q0, Q1 = (KS[:, q - 5, m, :] for m in range(4))
                for out, l, r, op in ((T0, A0, P0, ALU.mult), (T1, B0, Q0, ALU.mult), (T0, T0, T1, ALU.subtract),
                                      (T1, A0, Q0, ALU.mult), (A0, B0, P0, ALU.mult), (T1, T1, A0, ALU.add),
                                      (A0, A1, P1, ALU.mult), (B0, B1, Q1, ALU.mult), (A0, A0, B0, ALU.subtract),
                                      (B0, A1, Q1, ALU.mult), (A1, B1, P1, ALU.mult), (B0, B0, A1, ALU.add),
                                      (P0, T0, A0, ALU.add), (P1, T1, B0, ALU.subtract),
                                      (Q0, T0, A0, ALU.subtract), (Q1, T1, B0, ALU.add)):
                    spec.wait()
                    spec.inc(dve.tensor_tensor(out, l, r, op))
                spec.wait()
            for c0, c1 in ((0, 1), (LP + 1, LP + 3), (LP + LS + 3, LP + LS + 4)):
                dve.memset(RAW0[:, c0:c1], 0.0).then_inc(sem["pad_zero"], 1)
            dve.memset(stat[:, :, :], 0.0).then_inc(sem["pad_zero"], 1)

            hz = step
            for g in range(HG):
                short_conv(2 * HG + g, RAW0, CX0, g)
                hz.inc(dve.tensor_scalar(Z[:, g, :], Z[:, g, :], vec[:, V_FB + g:V_FB + g + 1], None, ALU.mult))
                hz.wait()
                dve.wait_ge(sem["inv_mm"], 3 * g + 3)
                for odd in range(2):
                    for s, bank, c0, c1, o, n in ((0, 3 + odd, 0, 512, 0, LP), (1, 5, odd * P, (odd + 1) * P, LP, LS)):
                        dst = Z[:, g, o + odd:o + n:2]
                        ins = dve.scalar_tensor_tensor(dst, PS[:, bank, c0:c1], invn[:, s, g:g + 1], dst, ALU.mult, ALU.add)
                        if odd and s:
                            ins.then_inc(sem["inv_used"], 1)
                        else:
                            hz.inc(ins)
                dve.wait_ge(sem["inv_used"], g + 1)
                dve.tensor_tensor(Z[:, g, :], Z[:, g, :], CX0, ALU.mult).then_inc(sem["hz_ready"], 1)
                dve.wait_ge(sem["hz_ready"], g + 1)

            c = step
            dve.wait_ge(sem["lam_in"], 64)
            c.inc(dve.tensor_tensor(LAMV[:, 0, :], LAMV[:, 0, :], LAMV[:, 1, :], ALU.mult))
            c.inc(dve.tensor_tensor(LAMV[:, 2, :], LAMV[:, 2, :], LAMV[:, 3, :], ALU.mult))
            c.wait()
            dve.tensor_reduce(lam[:, 0:1], LAMV[:, 0, :], AX.X, ALU.add).then_inc(sem["lam_sum"], 1)
            dve.tensor_reduce(lam[:, 1:2], LAMV[:, 2, :], AX.X, ALU.add).then_inc(sem["lam_sum"], 1)
            dve.wait_ge(sem["lam_exp"], 1)
            c.inc(dve.tensor_tensor(lam[:, 0:1], lam[:, 3:4], lam[:, 2:3], ALU.subtract))
            c.wait()
            dve.tensor_scalar(lam[:, 0:1], lam[:, 0:1], -LAM_INIT, None, ALU.add).then_inc(sem["lam_ready"], 1)
            dve.wait_ge(sem["inv_mm"], 3 * HG)
            for _, k0, k1 in QK:
                dve.memset(k0, 0.0).then_inc(sem["k_zero"], 1)
                dve.memset(k1, 0.0).then_inc(sem["k_zero"], 1)
            dve.wait_ge(sem["k_zero"], 4)
            dve.wait_ge(sem["lam_ready"], 1)
            dve.wait_ge(sem["rope_in"], 32)

            def rotate(h, j):
                q, k0, k1 = QK[h % 2]
                dve.wait_ge(sem["pm_mm"], 5 * h + j + 1)
                for n, (part, chunk) in enumerate(TURN_JOBS[j]):
                    if h or j or n:
                        dve.wait_ge(sem["q_roped"], roped(h, j)[0] + n)
                        if h or j > 1 or n:
                            dve.wait_ge(sem["k_roped"], roped(h, j)[1])
                    c0, cn = CHUNKS[chunk]
                    cols, o = slice(c0, c0 + cn), c0 % LP
                    raw = QKRAW[part][:, cols]
                    step.inc(dve.tensor_tensor(RT[:, cols], PS[:, job_bank(h, j), n * cn:(n + 1) * cn], SIN[:, o:o + cn], ALU.mult))
                    step.inc(dve.tensor_tensor(raw, raw, COS[:, o:o + cn], ALU.mult))
                    step.wait()
                    if part == 0:
                        dve.tensor_tensor(q[:, cols], raw, RT[:, cols], ALU.add).then_inc(sem["q_roped"], 1)
                    else:
                        dve.tensor_tensor(k0[0:DH, cols], raw[0:DH, :], RT[0:DH, cols], ALU.add).then_inc(sem["k_roped"], 1)
                        dve.tensor_tensor(k1[DH:P, cols], raw[DH:P, :], RT[DH:P, cols], ALU.add).then_inc(sem["k_roped"], 1)

            def maxima(u):
                kn = keys(u % NT)[1]
                for c in range(2):
                    dve.wait_ge(sem["s_mm"], 2 * u + c + 1)
                    s = PS[:, 2 * c:2 * c + 2, :].rearrange("p b n -> p (b n)")[:, 0:kn]
                    step.inc(dve.tensor_reduce(att[:, u % 2, 0, c:c + 1], s, AX.X, ALU.max))
                    step.wait()
                    dve.tensor_scalar(att[:, u % 2, 1, c:c + 1], att[:, u % 2, 0, c:c + 1], -(DH ** -0.5), None,
                                      ALU.mult).then_inc(sem["smax_ready"], 1)

            def output(u):
                h, i = u // NT, u % NT
                dve.wait_ge(sem["pv_mm"], u + 1)
                dve.tensor_scalar(AO[:, i, tiles[h]], PS[:, 6, (u % 4) * P:(u % 4 + 1) * P], att[:, u % 2, 3, 0:1], None,
                                  ALU.mult).then_inc(sem["o_ready"], 1)

            def mixed(u):
                kn = keys(u % NT)[1]
                dve.wait_ge(sem["exp_ready"], 2 * u + 2)
                if u >= 2:
                    dve.wait_ge(sem["o_ready"], u - 1)
                r = att[:, u % 2, :, :]
                step.inc(dve.reciprocal(r[:, 3, 0:2], r[:, 2, 0:2]))
                step.wait()
                step.inc(dve.tensor_scalar(r[:, 3, 2:3], r[:, 2, 0:1], r[:, 3, 1:2], lam[:, 0:1], ALU.mult, ALU.mult))
                step.wait()
                dve.scalar_tensor_tensor(PP[u % 2][0][:, 0:kn], PP[u % 2][1][:, 0:kn], r[:, 3, 2:3], PP[u % 2][0][:, 0:kn],
                                         ALU.mult, ALU.add).then_inc(sem["w_ready"], 1)

            for j in range(5):
                rotate(0, j)
            for u in range(UNITS):
                maxima(u)
                if u >= 2:
                    output(u - 2)
                h, i = (u - 1) // NT + 1, (u - 1) % NT
                if u >= 1 and h < HEADS and i >= 5:
                    rotate(h, i - 5)
                mixed(u)
            output(UNITS - 2)
            output(UNITS - 1)
            dve.wait_ge(sem["o_ready"], UNITS)

            c = step
            heads = AO.rearrange("p t (h v) -> p (t h) v", h=HEADS)
            c.inc(dve.tensor_tensor(SQ, AO, AO, ALU.mult))
            c.wait()
            dve.tensor_reduce(sub[:, 0, :], SQ.rearrange("p t (h v) -> p (t h) v", h=HEADS), AX.X, ALU.add).then_inc(sem["sub_sum"], 1)
            dve.wait_ge(sem["sub_root"], 1)
            c.inc(dve.reciprocal(sub[:, 2, :], sub[:, 1, :]))
            c.wait()
            dve.tensor_tensor(heads, heads, wide(sub[:, 2, :], DV), ALU.mult).then_inc(sem["sub_ready"], 1)
            for q in range(3 * HEADS):
                h, n = q // 3, q % 3
                c0, cn = CHUNKS[n]
                dve.wait_ge(sem["sub_tr"], q + 1)
                dve.tensor_scalar(AT[:, h, c0:c0 + cn], PS[:, SUB_BANKS[q % 4], 0:cn], vec[:, V_SUB:V_SUB + 1], 1.0 - LAM_INIT,
                                  ALU.mult, ALU.mult).then_inc(sem["at_ready"], 1)

            mg = step

            def merged(B, b):
                for n, (c0, cn) in enumerate(CHUNKS):
                    s = (b + n) % 2
                    dve.wait_ge(sem["mg_sig"], B * 6 + (2 * n + 2))
                    for part in range(2):
                        mg.inc(dve.tensor_tensor(TM[:, s, part, 0:cn], SG[:, s, part, 0:cn], PS[:, 4 * s + 2 + part, 0:cn], ALU.mult))
                    mg.wait()
                    dve.tensor_tensor(MT[:, bass.ds(B, 1), c0:c0 + cn].rearrange("p a n -> p (a n)"), TM[:, s, 0, 0:cn], TM[:, s, 1, 0:cn],
                                      ALU.add).then_inc(sem["m_ready"], 1)

            merged(0, 0)
            merged(1, 1)
            with dve.Fori(1, KD // 2) as cc:
                mg.enter(cc, 12)
                for b in range(2):
                    merged(cc * 2 + b, b)
            mg.leave(KD // 2 - 1)

            dve.wait_ge(sem["xr_in"], 32)
            for q in range(2 * NT):
                t, n = q // 2, q % 2
                dve.wait_ge(sem["wo_mm"], q + 1)
                dst = X[:, t, n * 512:(n + 1) * 512]
                dve.tensor_tensor(dst, PS[:, q % 6, :], dst, ALU.add).then_inc(sem["x1_ready"], 1)
            norm_stage(N_X, NT, lambda t: X[:, t, :], U2T, V_X)
            norm_stage(N_MEM, 4, lambda m: MS[m % 2], MEMT, V_MEM)
            for q in range(8):
                m, n = q // 2, q % 2
                dve.wait_ge(sem["vm_mm"], q + 1)
                dve.tensor_copy(VM[:, m, n * 512:(n + 1) * 512], PS[:, q % 6, :]).then_inc(sem["vm_ready"], 1)

            def keys_out(B, b):
                dve.wait_ge(sem["xb_mm"], B * 4 + 4)
                dve.tensor_copy(KX[:, bass.ds(B, 1), :].rearrange("p a n -> p (a n)"), PS[:, 4 * b + 3, :]).then_inc(sem["xk_ready"], 1)

            keys_out(0, 0)
            keys_out(1, 1)
            with dve.Fori(1, KD // 2) as cc:
                for b in range(2):
                    keys_out(cc * 2 + b, b)

            xmax = xp = step

            def cross_out(i):
                for half in range(2):
                    dve.wait_ge(sem["xo_mm"], 2 * i + half + 1)
                    dve.tensor_copy(OT[:, 4 * half:4 * half + 4, tiles[i]], bank4(6 + half)).then_inc(sem["ot_ready"], 1)

            for i in range(NT):
                r = att[:, i % 2, :, :]
                dve.wait_ge(sem["xs_mm"], i + 1)
                if i >= 1:
                    dve.wait_ge(sem["xp_ready"], i)
                s = PS[:, 2 * (i % 2):2 * (i % 2) + 2, :].rearrange("p b (h m) -> p (b h) m", h=2)
                xmax.inc(dve.tensor_reduce(r[:, 0, :], s, AX.X, ALU.max))
                xmax.wait()
                dve.tensor_scalar(r[:, 1, :], r[:, 0, :], -(XD ** -0.5), None, ALU.mult).then_inc(sem["xmax_ready"], 1)
                dve.wait_ge(sem["xexp_ready"], 4 * i + 4)
                xp.inc(dve.reciprocal(r[:, 3, :], r[:, 2, :]))
                xp.wait()
                dve.tensor_tensor(XP[i % 2], XP[i % 2], wide(r[:, 3, :], NMEM), ALU.mult).then_inc(sem["xp_ready"], 1)
                if i >= 2:
                    cross_out(i - 2)
            cross_out(NT - 2)
            cross_out(NT - 1)

            for q in range(2 * NT):
                n, t = q // NT, q % NT
                dve.wait_ge(sem["xo2_mm"], q + 1)
                dst = X[:, t, n * 512:(n + 1) * 512]
                dve.tensor_tensor(dst, PS[:, q % 6, :], dst, ALU.add).then_inc(sem["x2_ready"], 1)
            norm_stage(N_FFN, NT, lambda t: X[:, t, :], HT, V_FFN, stored=True)
            c = step
            dve.wait_ge(sem["rt_mm"], NT)
            logits = PS[:, 0, 0:NT * NE].rearrange("p (t e) -> p t e", e=NE)
            c.inc(dve.tensor_reduce(RM[:, 0, 0:NT], logits, AX.X, ALU.max))
            c.wait()
            dve.tensor_tensor(LG, logits, wide(RM[:, 0, 0:NT], NE), ALU.subtract).then_inc(sem["rt_low"], 1)
            dve.wait_ge(sem["rt_exp"], 1)
            c.inc(dve.tensor_reduce(RM[:, 1, 0:NT], LG, AX.X, ALU.add))
            c.wait()
            c.inc(dve.reciprocal(RM[:, 0, 0:NT], RM[:, 1, 0:NT]))
            c.wait()
            dve.tensor_tensor(LG, LG, wide(RM[:, 0, 0:NT], NE), ALU.mult).then_inc(sem["aff_ready"], 1)
            c = step
            dve.wait_ge(sem["aff_tr"], 1)
            for n, (c0, cn) in enumerate(CHUNKS):
                c.inc(dve.tensor_copy(AF[:, c0:c0 + cn], PS[0:NE, 1 + n, 0:cn]))
            c.wait()
            for tok, rounds, s0 in ((AF[:, 0:LP], CP // 8, 0), (AF[:, LP:T], CS // 8, CP)):
                for r in range(rounds):
                    v = VAL[:, s0 + 8 * r:s0 + 8 * r + 8]
                    c.inc(dve.max(v, tok))
                    c.wait()
                    c.inc(dve.max_index(IDX[:, s0 + 8 * r:s0 + 8 * r + 8], v, tok))
                    if r + 1 < rounds:
                        c.wait()
                        c.inc(dve.match_replace(tok, v, tok, -1.0))
                        c.wait()
            c.wait()
            c.inc(dve.tensor_copy(SLOT_I[:, 0:CE], IDX))
            c.wait()
            c.inc(dve.tensor_scalar(SLOT_I[:, CP:CE], SLOT_I[:, CP:CE], float(LP), None, ALU.add))
            c.inc(dve.tensor_copy(SLOT_V[:, 0:CP], VAL[:, 0:CP]))
            c.wait()
            for j in range(4):
                o = CE + CS * j
                c.inc(dve.tensor_scalar(SLOT_I[:, o:o + CS], SLOT_I[:, CP:CE], 4.0, float(j), ALU.mult, ALU.add))
                c.inc(dve.tensor_copy(SLOT_V[:, o:o + CS], VAL[:, CP:CE]))
            c.wait()
            dve.memset(RM[:, :, :], 0.0).then_inc(sem["slots_ready"], 1)
            dve.wait_ge(sem["idx_tr"], 1)
            dve.tensor_copy(idx_p[:, :], PS[:, 4, 0:NE]).then_inc(sem["idx_ready"], 1)
            dve.tensor_copy(idx_s[:, :], PS[0:CS, 4, NE:2 * NE]).then_inc(sem["idx_ready"], 1)
            dve.tensor_copy(idx_q[:, :], PS[:, 4, 2 * NE:3 * NE]).then_inc(sem["idx_ready"], 1)
            for s in range(2):
                dve.tensor_copy(gates[:, s, :], PS[:, 4, (3 + s) * NE:(4 + s) * NE]).then_inc(sem["idx_ready"], 1)
            dve.wait_ge(sem["idx_ready"], 5)

            def slots_in(e):
                dve.wait_ge(sem["xe_tr"], e * 3 + 3)
                for half in range(2):
                    g = vec[:, V_FFN + 4 * half:V_FFN + 4 * half + 4]
                    dve.tensor_tensor(XET[:, 4 * half:4 * half + 4, 0:CP], bank4(3 + half), wide(g, P), ALU.mult).then_inc(sem["xet_ready"], 1)
                dve.tensor_tensor(XET[:, :, CP:CE], PS[:, 5, 0:KD * CS].rearrange("p (k s) -> p k s", k=KD),
                                  wide(vec[:, V_FFN:V_FFN + KD], CS), ALU.mult).then_inc(sem["xet_ready"], 1)

            def hidden(e):
                for f in range(FF // P):
                    dve.wait_ge(sem["silu_ready"], e * 8 + (f + 1))
                    dve.tensor_tensor(HE[:, f, :], SL[:, f % 2, :], PS[:, f % 3, CE:2 * CE], ALU.mult).then_inc(sem["he_ready"], 1)

            def results(e, first):
                if not first:
                    dve.wait_ge(sem["scatter_p"], e * 16)
                    dve.wait_ge(sem["scatter_s"], e * 16)
                for n in range(2):
                    dve.wait_ge(sem["dn_mm"], e * 3 + (n + 1))
                    dve.tensor_scalar(YP[:, n * 512:(n + 1) * 512], PS[:, 6 + n, :], gates[:, 0, bass.ds(e, 1)], None,
                                      ALU.mult).then_inc(sem["y_out"], 1)
                dve.wait_ge(sem["dn_mm"], e * 3 + 3)
                dve.tensor_scalar(YS, PS[:, 5, 0:256], gates[:, 1, bass.ds(e, 1)], None, ALU.mult).then_inc(sem["y_out"], 1)

            slots_in(0)
            hidden(0)
            slots_in(1)
            results(0, True)
            with dve.Fori(1, NE - 1) as e:
                hidden(e)
                slots_in(e + 1)
                results(e, False)
            hidden(NE - 1)
            results(NE - 1, False)
            dve.wait_ge(sem["gain_in"], 16)
            for t in range(NT):
                dve.wait_ge(sem["fin_act"], 2 * t + 2)
                dve.reciprocal(stat[:, 2, t:t + 1], stat[:, 1, t:t + 1]).then_inc(sem["fin_rec"], 1)
                dve.wait_ge(sem["fin_rec"], t + 1)
                dve.scalar_tensor_tensor(FIN[t], FIN[t], stat[:, 2, t:t + 1], GROW, ALU.mult, ALU.mult).then_inc(sem["fin_ready"], 1)


_INS = ["x_prompt", "x_sample", "mem_prompt", "mem_sample", "norm_mix", "w_in", "lambda_q1", "lambda_k1",
        "lambda_q2", "lambda_k2", "subln", "w_br_attn", "hy_conv_w", "hy_conv_b", "filt_w1", "filt_b1",
        "filt_w2", "filt_b2", "filt_w3", "filt_freq", "filt_bias", "w_br_hyena", "w_out", "norm_x", "norm_mem",
        "w_xq", "w_xkv", "w_xo", "norm_ffn", "w_router", "w_exp_gate", "w_exp_up", "w_exp_down", "norm_final"]
_OUTS = [(1, LP, D), (1, LS, D)]


def build(nc, arrays):
    a = {n: nc.dram_tensor(f"in_{n}", v.shape, F32, kind="ExternalInput").ap() for n, v in arrays.items()}
    outs = [nc.dram_tensor(f"out_{i}", s, F32, kind="ExternalOutput").ap() for i, s in enumerate(_OUTS)]
    encoder_kernel(nc, a, *outs)


def kernel(**inputs):
    import concourse.bacc as bacc
    from concourse.bass_utils import run_bass_kernel_spmd

    arrays = {n: np.ascontiguousarray(inputs[n]) for n in _INS} | shape_tables()
    nc = bacc.Bacc("TRN2", target_bir_lowering=False, num_devices=1)
    build(nc, arrays)
    r = run_bass_kernel_spmd(nc, [{f"in_{n}": v for n, v in arrays.items()}], core_ids=[0])
    return tuple(r.results[0][f"out_{i}"] for i in range(len(_OUTS)))
```

```python
from contextlib import ExitStack

import numpy as np

import concourse.bass as bass
from concourse import mybir

F32 = mybir.dt.float32
U32 = mybir.dt.uint32
BF16 = mybir.dt.bfloat16
ACT = mybir.ActivationFunctionType
ALU = mybir.AluOpType
AX = mybir.AxisListType

P = 128
D = 1024
KD = D // P
LP, LS = 1024, 256
T = LP + LS
NTP, NTS = LP // P, LS // P
NT = NTP + NTS
CHUNKS = [(0, 512), (512, 512), (1024, 256)]
HEADS, DH, DV = 4, 64, 128
ROT = DH // 4
HY = 512
HG = HY // P
EMB, FH = 33, 64
COL_K, COL_V, COL_HY = 512, 1024, 1536
COL_GA, COL_GB = 3072, 4096
NMEM = 256
XH, XD = 4, 256
NE, FF = 16, 1024
CP, CS = 2 * LP // NE, 2 * LS // NE
CE = CP + CS
EPS = 1e-6
LAM_INIT = 0.2
PI_LOW = 3.1415925
INV_2PI = float(np.float32(1 / (2 * np.pi)))
TWO_PI_A = 6.28125
TWO_PI_B = float(2 * np.pi - 6.28125)
ROUND = 12582912.0

V_MIX, V_X, V_MEM, V_FFN = 0, 8, 16, 24
V_CW, V_CB, V_FB, V_SUB, V_FREQ, V_B1, V_B2 = 32, 68, 80, 84, 85, 86, 87
NV = 88


def shape_tables():
    f = np.float32

    def order(n):
        even = np.arange(0, n, 2)
        return np.concatenate([even[0::2], even[1::2]] * (n == LP) + [even] * (n != LP) + [np.arange(1, n, 2)])

    feats, decays = [], []
    bands = (EMB - 1) // 2
    lo, hi = np.log(1e-2) / 1.5, np.log(1e-2) / 0.3
    deltas = np.abs(np.linspace(lo, hi, HY).astype(f))
    for n in (LP, LS):
        t = np.linspace(0.0, 1.0, n).astype(f)
        w = (f(2.0 * np.pi) * np.arange(n).astype(f) / f(n)).astype(f)
        fr = np.linspace(1e-4, bands - 1, bands).astype(f)
        a = (fr[None, :] * w[:, None]).astype(f)
        z = np.concatenate([t[:, None], np.cos(a), -np.sin(a)], axis=1).astype(f)
        feats.append(z[order(n)])
        decays.append(np.exp(-t[:, None] * deltas[None, :]).astype(f)[order(n)])
    feat = np.ascontiguousarray(np.concatenate(feats).T)
    decay = np.ascontiguousarray(np.concatenate(decays).reshape(NT, P, HY).transpose(1, 0, 2))

    def angles(n, k, t, fn):
        return fn(np.pi * ((t[:, None] * (2 * k + 1)[None, :]) % (4 * n)) / (2 * n))

    def rows(m):
        kinds, n, w = m.shape
        return np.ascontiguousarray(m.reshape(kinds, n // P, P, w).transpose(2, 0, 1, 3).astype(f))

    k = np.arange(LP // 4)
    both = np.concatenate([k, LP // 2 - 1 - k])
    te = np.stack([angles(LP, k, np.arange(c, LP, 4), g) for g in (np.cos, np.sin) for c in (0, 2)])
    to = np.stack([angles(LP, both, np.arange(1, LP, 2), g) for g in (np.cos, np.sin)])
    ts = np.stack([angles(LS, np.arange(LS // 2), np.arange(c, LS, 2), g) for g in (np.cos, np.sin) for c in (0, 1)])
    back = [0, 2, 1, 3]
    inv = ROT // 2
    freq = (f(500000.0) ** (-np.arange(0, ROT, 2).astype(f) / f(ROT))).astype(f)
    ang = (np.arange(LP).astype(f)[None, :] * freq[:, None]).astype(f)
    cos, sin = np.ones((P, LP), f), np.zeros((P, LP), f)
    perm = np.zeros((P, P), f)
    for c in range(2):
        a = DH * c
        cos[a:a + inv], cos[a + inv:a + ROT] = np.cos(ang), np.cos(ang)
        sin[a:a + inv], sin[a + inv:a + ROT] = np.sin(ang), np.sin(ang)
        for d in range(inv):
            perm[a + inv + d, a + d] = -1.0
            perm[a + d, a + inv + d] = 1.0
    return {
        "feat": feat, "decay": decay,
        "fwd_e": rows(te), "fwd_o": rows(to), "fwd_s": rows(ts),
        "inv_e": rows(te.transpose(0, 2, 1)[back] / LP), "inv_o": rows(to.transpose(0, 2, 1) / LP),
        "inv_s": rows(ts.transpose(0, 2, 1)[back] / LS),
        "rope_cos": cos, "rope_sin": sin, "perm": perm, "ident": np.eye(P, dtype=f), "reverse": np.eye(P, dtype=f)[::-1],
    }


class Count:

    def __init__(self, eng, sem):
        self.eng, self.sem, self.base, self.n = eng, sem, 0, 0

    def inc(self, ins):
        ins.then_inc(self.sem, 1)
        self.n += 1

    def value(self):
        return self.base + self.n

    def wait(self):
        self.eng.wait_ge(self.sem, self.base + self.n)

    def enter(self, i, per):
        self.start, self.per = self.base + self.n, per
        self.base, self.n = i * per + (self.start - per), 0

    def leave(self, passes):
        assert self.n == self.per, (self.n, self.per)
        self.base, self.n = 0, self.start + passes * self.per


SEMS = """dve_step vec_zero vec_in vec_tr vec_ready const_in perm_in rev_in feat_in decay_in fwd_in inv_in
mlp_mm mlp_used arg_ready sin_ready h_mm h_dve tap_abs taps_sum sums_ready h_pool norm_mm invn_ready
dft_mm dft_act dft_dve dft_kept dft_pool x_in_0 x_in_1 x_in_2 x_in_3 x_in_4 norm_act root_rec xn_ready xn_tr ut_ready
hy_in_0 hy_in_1 hy_in_2 hy_mm raw_ready pad_zero  conv_done z_ready z_tr zt_ready
inv_mm  inv_used hz_ready wv_in v_mm v_ready lam_in  lam_sum lam_exp lam_ready
wqk_in rope_in qk_mm raw_qk pm_mm  q_roped k_roped k_zero
s_mm  smax_ready exp_ready  w_ready w_tr wt_ready pv_mm o_ready
 sub_sum sub_root sub_ready sub_tr at_ready
mg_in_0 mg_in_1 mg_mm mg_sig  m_ready wo_in xr_in wo_mm x1_ready
mem_in_0 mem_in_1 wxv_in_0 wxv_in_1 vm_mm vm_ready xb_in_0 xb_in_1 xb_mm q_ready xk_ready
xs_mm  xmax_ready xexp_ready  xp_ready xp_tr pt_ready xo_mm ot_ready
wx_in_0 wx_in_1 xo2_mm x2_ready acc_out acc_out_s hn_out_0 hn_out_1 wr_in rt_mm  rt_low rt_exp aff_ready aff_tr
 slots_ready slots_tr sorted_ready reversed idx_tr idx_ready eg0 eu0 eg1 eu1 ed0 ed1 col_ready gather_p gather_s xe_tr xet_ready
gu_mm silu_ready he_ready scol_ready dn_mm y_out scatter_p scatter_s gain_in
fin_act fin_rec fin_ready fin_out""".split() + [f"fin_in_{t}" for t in range(NT // 2)]


def encoder_kernel(nc, a, out_p, out_s):
    def rows_of(p, s, t, n):
        return (p if t < n else s)[(t % n) * P:(t % n + 1) * P, :]

    out_rows = [rows_of(out_p[0], out_s[0], t, NTP) for t in range(NT)]
    w_in = a["w_in"][0]
    acc = nc.dram_tensor("residual_rows", [T, D], F32, kind="Internal").ap()
    hn = nc.dram_tensor("normed_rows", [T, D], F32, kind="Internal").ap()
    acc_quarters = acc.rearrange("t (j n) -> (t j) n", j=4)

    with ExitStack() as ctx:
        sem = {n: ctx.enter_context(nc.semaphore(n)) for n in SEMS}
        arena = ctx.enter_context(nc.sbuf_tensor("arena", [P, 204 * 256], F32))
        PS = ctx.enter_context(nc.psum_tensor("banks", [P, 8, 512], F32))

        def at(kb, *dims):
            n = int(np.prod(dims))
            v = arena[:, int(kb * 256):int(kb * 256) + n]
            if len(dims) == 2:
                v = v.rearrange("p (a b) -> p a b", a=dims[0])
            if len(dims) == 3:
                v = v.rearrange("p (a b c) -> p a b c", a=dims[0], b=dims[1])
            return v

        def small(name, shape, dt=F32):
            return ctx.enter_context(nc.sbuf_tensor(name, shape, dt))

        vec, ident, perm = small("vec", [P, NV]), small("ident_sb", [P, P]), small("perm_sb", [P, P])
        ones, eps = small("ones", [P, 2]), small("eps", [P, 1])
        stat = small("stat", [P, 3, 16])
        invn = small("invn", [P, 2, HG])
        att = small("att", [P, 2, 4, 4])
        lam = small("lam", [P, 4])
        sub = small("sub", [P, 3, NT * HEADS])
        rw = small("rw", [P, KD, NE])
        idx_p, idx_s, idx_q = small("idx_p", [P, NE], U32), small("idx_s", [CS, NE], U32), small("idx_q", [P, NE], U32)
        gates = small("gates", [P, 2, NE])
        now_p, now_s = small("now_p", [P, 1], U32), small("now_s", [CS, 1], U32)
        turn = small("turn", [P, 1])
        out_p_idx, out_q_idx = small("out_p_idx", [P, 1], U32), small("out_q_idx", [P, 1], U32)

        UT = at(0, KD, T)
        XS = at(80, NT, D)
        XN = [at(194 + 4 * i, D) for i in range(2)]
        SQJ = at(202, D // 2).bitcast(BF16)
        FEAT, H1, ARG, RND, H2 = at(60, T), at(65, T), at(70, T), at(75, T), at(140, T)
        W3F, W1F, W2F, VROW = at(145, 2 * HY), at(149, P), at(149.5, P), at(150, P)
        SF, DF = at(80, NT, HY), at(100, NT, HY)
        DEC = at(120, NT, HY)
        TAP, HAB, HACC = at(188, 2, 2, HY), at(196, 2, HY), at(200, 2, HY)
        Z = at(40, HG, T)
        ZT = at(60, NT, HY)
        HYW = [at(154 + 4 * i, KD, P) for i in range(3)] + [at(120, KD, P), at(124, KD, P)]
        RAW, CX, CH = [at(166, LP + LS + 4), at(171.25, LP + LS + 4)], at(176.5, T), at(182, T)
        RAW0, CX0 = at(68, LP + LS + 4), at(73.25, T)
        FWE, FWO, FWDS = at(120, 4, 2, 256), at(128, 2, 4, 512), at(144, 4, P)
        HALF = at(146, 4, HY)
        KSP, KSS = at(154, 4, 4 * HY), at(80, 4, HY)
        FOLD = at(186, 2, 2, HY)
        AB, T0, T1 = at(194, 4, HY), [at(182, HY), at(92, HY)], at(202, HY)
        TE = [at(194, 2, HY)] * 4 + [at(178, 2, HY)] * 2 + [at(88, 2, HY)] * 4
        INVE, INVO, INVS = at(94, 4, 2, 256), at(102, 2, 4, 512), at(118, 4, P)
        V, AO, AT = at(80, NT, HY), at(60, NT, HY), at(100, HEADS, T)
        WV, COS, SIN = at(120, KD, HY), at(136, LP), at(140, LP)
        PP = [[at(120 + 8 * i + 4 * c, LP) for c in range(2)] for i in range(2)]
        WT = [at(144 + 4 * i, KD, P) for i in range(2)]
        WQK = [(at(144, KD, P), at(148, KD, P))] + 3 * [(at(160, KD, P), at(164, KD, P))]
        QKRAW, RT = [at(168, T), at(173, T)], at(178, T)
        QK = [[at(100 + 5 * i, T) for i in range(3)], [at(184 + 5 * i, T) for i in range(3)]]
        LAMV = at(152, 4, DH)
        SQ = at(120, NT, HY)
        MT = at(60, KD, T)
        MGW = [(at(152 + 12 * b, KD, P), at(156 + 12 * b, KD, P), at(160 + 12 * b, HG, P), at(162 + 12 * b, HG, P))
               for b in range(2)]
        SG, TM = at(136, 2, 2, HY), at(144, 2, 2, HY)
        WO = [at(120, KD, 512), at(176, KD, 512)]
        X = at(0, NT, D)
        MEMT, MS = at(40, KD, 2 * NMEM), at(136, 4, D)
        U2T = at(136, KD, T)
        XQW, XKW = [at(100 + 8 * b, KD, P) for b in range(2)], [at(104 + 8 * b, KD, P) for b in range(2)]
        QX, KX = at(60, KD, T), at(120, KD, 2 * NMEM)
        WXV, VM = [at(176, KD, 512), at(136, KD, 512)], at(100, 4, D)
        XP, PT = [at(176 + 4 * i, XH, NMEM) for i in range(2)], [at(184 + 4 * i, 2 * XH, P) for i in range(2)]
        OT = at(136, KD, T)
        WXO = [at(40, KD, 512), at(120, KD, 512)]
        HT = at(60, KD, T)
        LG, AFP, AFS = at(176, NT, NE), at(177, LP // 2)[0:2 * NE], at(179, LS)[0:NE]
        VALP, IDXP = at(180, CP)[0:2 * NE], at(180.5, CP)[0:2 * NE].bitcast(U32)
        VALS, IDXS = at(181, CS)[0:NE], at(181.25, CS)[0:NE].bitcast(U32)
        SLOT_P = at(182, CP)[0:2 * NE]
        SLOT_I, SLOT_V = at(184, CS + P)[0:NE], at(186, CS + P)[0:NE]
        RM = at(188, 2, 16)
        SORTED = at(189, 2, 2 * NE)
        FIRST = at(190, 3, NE)
        WG, WU, WD = [at(0, KD, 512), at(32, KD, 512)], [at(16, KD, 512), at(48, KD, 512)], [at(64, KD, 512), at(80, KD, 512)]
        XE, XES = at(100, D), at(104, D)[0:CS]
        XET, HE = at(112, KD, CE), at(117, KD, CE)
        SL = at(122, 2, CE)
        YP, YS = at(124, D), at(128, 256)
        GROW = at(130, D)
        FIN = [at(4 * t, D) for t in range(NT)]

        def blocked(dram, c0, n):
            return dram[:, bass.ds(c0, n)].rearrange("(k p) c -> p k c", p=P)

        def bank4(b):
            return PS[:, b, :].rearrange("p (a c) -> p a c", a=4)

        def wide(v, n):
            return v.unsqueeze(2).to_broadcast([v.shape[0], v.shape[1], n])

        def taps_at(r):
            before = 2 * r + (r > 0) + (r > NTP)
            return before + 2, before + 2 + (r in (0, NTP))

        BESIDE = {(1, 0): [("layer", 0), ("layer", 1)], (1, 1): [("layer", 2)], (3, 0): [("turn", 0)],
                  (3, 1): [("taps", 0)], (3, 2): [("taps", 1)],
                  (4, 0): [("taps", 2)], (4, 1): [("taps", 3)], (4, 2): [("taps", 4)],
                  (5, 0): [("taps", 5)], (5, 1): [("taps", 6)], (5, 2): [("turn", 1)],
                  (6, 0): [("taps", 7)], (6, 1): [("taps", 8)], (6, 2): [("taps", 9)],
                  (7, 1): [("norms", 0)], (7, 2): [("turn", 2)]}

        def taps_summed(r):
            return 2 * (r + 1) - 1 - (r >= NTP)

        DFT_KIND, DFT_INPUT = [0, 1, 0, 1, 2, 3, 4, 4, 2, 3], [0, 0, 1, 1, 0, 0, 0, 1, 1, 1]
        DFT_STEPS = [4, 8, 4, 34, 4, 8, 4, 17, 4, 34]
        DFT_READ = [4, 8, 4, 4, 4, 8, 4, 4, 4, 4]
        DFT_ALL = sum(DFT_STEPS)
        DFT_COPIED = [0, 2, 4, 6, 7, 8]

        def dft_read(q):
            return sum(DFT_STEPS[:q]) + DFT_READ[q]

        DFT_PRODUCTS = [(q, j, sum(DFT_STEPS[:q]) + n) for q, j, n in ((3, 0, 4), (3, 2, 21), (7, 4, 4), (9, 1, 4), (9, 3, 21))]

        def spectrum(tile, kind):
            return KSP[:, tile, kind * HY:(kind + 1) * HY] if tile < 4 else KSS[:, kind, :]

        def product_done(tile):
            return {0: 3, 2: 6, 4: 13, 1: 16, 3: 19}[tile]

        N_MEM, N_X, N_FFN = NT, NT + 4, 2 * NT + 4
        tiles = [slice(t * P, (t + 1) * P) for t in range(NT)]

        def keys(i):
            return (0, LP) if i < NTP else (LP, LS)

        QUERY_TILES = [0, 1] + list(range(NTP, NT)) + list(range(2, NTP))

        def query_tile(u):
            return QUERY_TILES[u % NT]

        W_HEAD = 2 * NTP + NTS
        SUB_BANKS = (2, 3, 6, 7)
        UNITS = HEADS * NT
        XORDER = list(range(NTP, NT)) + list(range(NTP))
        XO_JOBS = [(t, n) for n in range(2) for t in range(4)] + [(t, n) for t in range(4, NT) for n in range(2)]
        X2_AT = [XO_JOBS.index((t, 1)) + 1 for t in range(NT)]
        XO_PROMPT = 2 * NTP

        def logit_slot(t):
            return 2 * (t % 4) + t // 4 if t < NTP else t

        def xo_bank(q):
            return q % 4 if q < XO_PROMPT else q % 2

        def turned(u):
            groups = [2 if t < NTP else 1 for t in QUERY_TILES]
            return W_HEAD * (u // NT) + sum(groups[:u % NT]), groups[u % NT]

        RAW_JOBS = [[(0, 0)], [(1, 0)], [(0, 1)], [(1, 1)], [(0, 2), (1, 2)]]
        TURN_JOBS = [[(0, 0)], [(1, 0)], [(1, 1)], [(0, 1)], [(0, 2), (1, 2)]]

        def job_bank(h, j):
            return 7 if h else j % 5

        def roped(h, j):
            done = [part for job in TURN_JOBS[:j] for part, _ in job]
            return 3 * h + done.count(0), 6 * h + 2 * done.count(1)

        block = ctx.enter_context(nc.Block())

        @block.sync
        def _(sp):
            sp.dma_start(ident[:, :], a["ident"]).then_inc(sem["const_in"], 16)

            def x_load(i):
                x = a["x_prompt"] if 2 * i < NTP else a["x_sample"]
                r = 2 * i * P - (0 if 2 * i < NTP else LP)
                sp.dma_start(XS[:, 2 * i:2 * i + 2, :], x[0][r:r + 2 * P, :].rearrange("(t p) d -> p t d", p=P)
                             ).then_inc(sem[f"x_in_{i}"], 16)

            x_load(0)
            sp.wait_ge(sem["vec_zero"], 1)
            for row, v, r in ((V_MIX, a["norm_mix"], 8), (V_X, a["norm_x"], 8), (V_MEM, a["norm_mem"], 8),
                              (V_FFN, a["norm_ffn"], 8), (V_CB, a["hy_conv_b"], 12), (V_FB, a["filt_bias"], 4),
                              (V_SUB, a["subln"], 1)):
                sp.dma_start(VROW[row:row + r, :], v[0].rearrange("(r c) -> r c", c=P)).then_inc(sem["vec_in"], 16)
            sp.dma_start(VROW[V_CW:V_CW + 36, :], a["hy_conv_w"][0].rearrange("k (r c) -> (k r) c", c=P)).then_inc(sem["vec_in"], 16)
            for row, v in ((V_FREQ, a["filt_freq"]), (V_B1, a["filt_b1"]), (V_B2, a["filt_b2"])):
                sp.dma_start(VROW[row:row + 1, 0:FH], v).then_inc(sem["vec_in"], 16)
            for i in range(1, NT // 2):
                x_load(i)

            def hyena_load(b):
                c0 = COL_HY + HY * (1 + b % 2) + P * (b // 2)
                sp.dma_start(HYW[b % 3], blocked(w_in, c0, P)).then_inc(sem[f"hy_in_{b % 3}"], 16)

            hyena_load(0)
            sp.dma_start(FEAT[0:EMB, :], a["feat"]).then_inc(sem["feat_in"], 16)
            sp.dma_start(W1F[0:EMB, 0:FH], a["filt_w1"][0]).then_inc(sem["feat_in"], 16)
            sp.dma_start(W2F[0:FH, 0:FH], a["filt_w2"][0]).then_inc(sem["feat_in"], 16)
            sp.dma_start(W3F[0:FH, :], a["filt_w3"][0]).then_inc(sem["feat_in"], 16)
            hyena_load(1)
            hyena_load(2)
            sp.dma_start(DEC, a["decay"]).then_inc(sem["decay_in"], 16)
            sp.dma_start(perm[:, :], a["perm"]).then_inc(sem["perm_in"], 16)
            sp.dma_start(rw[:, :, :], blocked(a["w_router"][0], 0, NE)).then_inc(sem["wr_in"], 16)
            for b in range(3, 2 * HG):
                sp.wait_ge(sem["hy_mm"], 3 * (b - 2))
                hyena_load(b)
            sp.wait_ge(sem["h_mm"], NT)
            sp.wait_ge(sem["h_dve"], taps_at(NT - 1)[1])
            sp.dma_start(FWE, a["fwd_e"]).then_inc(sem["fwd_in"], 16)
            sp.dma_start(FWO, a["fwd_o"]).then_inc(sem["fwd_in"], 16)
            sp.dma_start(FWDS, a["fwd_s"].rearrange("p a b c -> p (a b) c")).then_inc(sem["fwd_in"], 16)
            def factor_load(g):
                if g >= 2:
                    sp.wait_ge(sem["hy_mm"], 3 * (2 * HG + g - 1))
                sp.dma_start(HYW[3 + g % 2], blocked(w_in, COL_HY + P * g, P)).then_inc(sem[f"hy_in_{g % 2}"], 16)

            sp.wait_ge(sem["dft_mm"], 28)
            sp.dma_start(INVE, a["inv_e"]).then_inc(sem["inv_in"], 16)
            sp.dma_start(INVO, a["inv_o"]).then_inc(sem["inv_in"], 16)
            sp.dma_start(INVS, a["inv_s"].rearrange("p a b c -> p (a b) c")).then_inc(sem["inv_in"], 16)
            sp.wait_ge(sem["dft_mm"], 36)
            factor_load(0)
            factor_load(1)
            sp.wait_ge(sem["dft_mm"], 40)
            sp.dma_start(COS, a["rope_cos"]).then_inc(sem["rope_in"], 16)
            sp.dma_start(SIN, a["rope_sin"]).then_inc(sem["rope_in"], 16)
            factor_load(2)
            factor_load(3)
            sp.wait_ge(sem["hy_mm"], 9 * HG)
            sp.dma_start(WV, blocked(w_in, COL_V, HY)).then_inc(sem["wv_in"], 16)
            sp.wait_ge(sem["dft_dve"], DFT_ALL)
            for h in range(HEADS):
                if h == 1:
                    sp.wait_ge(sem["inv_mm"], 3 * HG)
                if h:
                    sp.wait_ge(sem["qk_mm"], 5 * h)
                sp.dma_start(WQK[h][0], blocked(w_in, h * P, P)).then_inc(sem["wqk_in"], 16)
                sp.dma_start(WQK[h][1], blocked(w_in, COL_K + h * P, P)).then_inc(sem["wqk_in"], 16)

            def merge_load(B, b):
                ga, gb, wa, wh = MGW[b]
                s = sem[f"mg_in_{b}"]
                sp.dma_start(ga, blocked(w_in, B * P + COL_GA, P)).then_inc(s, 16)
                sp.dma_start(gb, blocked(w_in, B * P + COL_GB, P)).then_inc(s, 16)
                sp.dma_start(wa, blocked(a["w_br_attn"][0], B * P, P)).then_inc(s, 16)
                sp.dma_start(wh, blocked(a["w_br_hyena"][0], B * P, P)).then_inc(s, 16)

            sp.wait_ge(sem["q_roped"], 3 * HEADS)
            sp.wait_ge(sem["k_roped"], 6 * HEADS)
            merge_load(0, 0)
            merge_load(1, 1)
            sp.wait_ge(sem["pm_mm"], 5 * HEADS)
            sp.dma_start(perm[:, :], a["reverse"]).then_inc(sem["rev_in"], 16)
            sp.wait_ge(sem["s_mm"], 2 * UNITS)
            sp.dma_start(WO[1], blocked(a["w_out"][0], 512, 512)).then_inc(sem["wo_in"], 16)
            sp.wait_ge(sem["sub_ready"], 1)
            sp.dma_start(WO[0], blocked(a["w_out"][0], 0, 512)).then_inc(sem["wo_in"], 16)
            with sp.Fori(1, KD // 2) as c:
                for b in range(2):
                    sp.wait_ge(sem["mg_mm"], c * 6 + (3 * b - 3))
                    merge_load(c * 2 + b, b)
            sp.wait_ge(sem["m_ready"], 3 * KD)
            for s, mem in enumerate((a["mem_prompt"], a["mem_sample"])):
                sp.dma_start(MS[:, 2 * s:2 * s + 2, :], mem[0].rearrange("(t p) d -> p t d", p=P)).then_inc(sem[f"mem_in_{s}"], 16)
            sp.dma_start(X[:, 0:NTP, :], a["x_prompt"][0].rearrange("(t p) d -> p t d", p=P)).then_inc(sem["xr_in"], 16)
            sp.dma_start(X[:, NTP:NT, :], a["x_sample"][0].rearrange("(t p) d -> p t d", p=P)).then_inc(sem["xr_in"], 16)

            def xq_load(B, b):
                sp.dma_start(XQW[b], blocked(a["w_xq"][0], B * P, P)).then_inc(sem[f"xb_in_{b}"], 16)
                sp.dma_start(XKW[b], blocked(a["w_xkv"][0], B * P, P)).then_inc(sem[f"xb_in_{b}"], 16)

            xq_load(0, 0)
            xq_load(1, 1)
            sp.wait_ge(sem["wo_mm"], 2 * NT)
            sp.dma_start(WXV[0], blocked(a["w_xkv"][0], D, 512)).then_inc(sem["wxv_in_0"], 16)
            with sp.Fori(1, KD // 2) as c:
                for b in range(2):
                    sp.wait_ge(sem["xb_mm"], c * 8 + (4 * b - 4))
                    xq_load(c * 2 + b, b)
            sp.wait_ge(sem["xb_mm"], 4 * KD)
            sp.dma_start(WXV[1], blocked(a["w_xkv"][0], D + 512, 512)).then_inc(sem["wxv_in_1"], 16)
            sp.wait_ge(sem["vm_mm"], 8)
            sp.dma_start(WXO[0], blocked(a["w_xo"][0], 0, 512)).then_inc(sem["wx_in_0"], 16)
            sp.wait_ge(sem["xs_mm"], NT)
            sp.dma_start(WXO[1], blocked(a["w_xo"][0], 512, 512)).then_inc(sem["wx_in_1"], 16)

            def expert_halves(e, first, which):
                halves = (("eg0", WG[0], "w_exp_gate", 0), ("eu0", WU[0], "w_exp_up", 0),
                          ("eg1", WG[1], "w_exp_gate", 512), ("eu1", WU[1], "w_exp_up", 512),
                          ("ed0", WD[0], "w_exp_down", 0), ("ed1", WD[1], "w_exp_down", 512))
                for n in which:
                    s, dst, w, c0 = halves[n]
                    if not first and n in (0, 2):
                        sp.wait_ge(sem["gu_mm"], e * 8 + (2 * n - 4))
                    if not first and n == 4:
                        sp.wait_ge(sem["dn_mm"], e * 3)
                    src = a[w][0][bass.ds(e, 1), :, c0:c0 + 512].rearrange("e (k p) c -> p (e k) c", p=P)
                    sp.dma_start(dst, src).then_inc(sem[s], 16)

            for t in range(NT):
                sp.wait_ge(sem["x2_ready"], X2_AT[t])
                s = "acc_out" if t < NTP else "acc_out_s"
                sp.dma_start(acc[tiles[t], :], X[:, t, :]).then_inc(sem[s], 16)
                sp.wait_ge(sem["xn_ready"], N_FFN + t + 1)
                sp.dma_start(hn[tiles[t], :], XN[t % 2]).then_inc(sem[f"hn_out_{t % 2}"], 16)
                if t == NTP - 1:
                    sp.wait_ge(sem["acc_out"], 16 * NTP)
                    expert_halves(0, True, (0, 1))
            sp.wait_ge(sem["acc_out_s"], 16 * NTS)
            sp.wait_ge(sem["xo2_mm"], 2 * NT)
            sp.wait_ge(sem["rt_mm"], NT)
            sp.wait_ge(sem["gather_p"], 16)
            sp.wait_ge(sem["gather_s"], 16)
            expert_halves(0, True, (2, 3, 4, 5))
            sp.dma_start(GROW, a["norm_final"].unsqueeze(0).to_broadcast([P, D])).then_inc(sem["gain_in"], 16)
            with sp.Fori(1, NE) as e:
                expert_halves(e, False, range(6))
            sp.wait_ge(sem["gu_mm"], 8 * NE)
            sp.wait_ge(sem["scatter_p"], 16 * NE)
            sp.wait_ge(sem["scatter_s"], 16 * NE)
            for t in range(0, NT, 2):
                sp.dma_start(at(4 * t, 2, D), acc[t * P:(t + 2) * P, :].rearrange("(t p) d -> p t d", p=P)).then_inc(sem[f"fin_in_{t // 2}"], 16)
            for t in range(NT):
                sp.wait_ge(sem["fin_ready"], t + 1)
                sp.dma_start(out_rows[t], FIN[t]).then_inc(sem["fin_out"], 16)
            sp.wait_ge(sem["fin_out"], 16 * NT)

        @block.gpsimd
        def _(pool):
            taps = Count(pool, sem["h_pool"])
            for r in range(NT):
                pool.wait_ge(sem["h_dve"], taps_at(r)[1])
                taps.inc(pool.tensor_tensor(SF[:, r, :], TAP[:, r % 2, 0, :], TAP[:, r % 2, 1, :], ALU.add))
                taps.inc(pool.tensor_tensor(DF[:, r, :], TAP[:, r % 2, 0, :], TAP[:, r % 2, 1, :], ALU.subtract))

            part = Count(pool, sem["dft_pool"])
            for q, tile, ready in DFT_PRODUCTS:
                P1, Q1 = spectrum(tile, 1), spectrum(tile, 3)
                pool.wait_ge(sem["dft_dve"], ready)
                part.inc(pool.tensor_tensor(HALF[:, 0, :], AB[:, 1, :], P1, ALU.mult))
                part.inc(pool.tensor_tensor(HALF[:, 2, :], AB[:, 3, :], Q1, ALU.mult))
                part.wait()
                part.inc(pool.tensor_tensor(HALF[:, 0, :], HALF[:, 0, :], HALF[:, 2, :], ALU.subtract))
                assert part.value() == product_done(tile)
                if tile in (2, 3):
                    pool.wait_ge(sem["dft_dve"], sum(DFT_STEPS[:q + 1]))
                    j = tile - 2
                    cos, cos2, sin, sin2 = spectrum(j, 0), spectrum(tile, 0), spectrum(j, 1), spectrum(tile, 1)
                    part.inc(pool.tensor_tensor(FOLD[:, j, 0, :], cos, cos2, ALU.add))
                    part.inc(pool.tensor_tensor(FOLD[:, j, 1, :], sin, sin2, ALU.subtract))
                    part.wait()
                    part.inc(pool.tensor_tensor(cos2, cos, cos2, ALU.subtract))
                    part.inc(pool.tensor_tensor(sin2, sin, sin2, ALU.add))

            pool.wait_ge(sem["dft_dve"], DFT_ALL)
            for n, v in enumerate(("lambda_q1", "lambda_k1", "lambda_q2", "lambda_k2")):
                pool.dma_start(LAMV[:, n, :], a[v].to_broadcast([P, DH])).then_inc(sem["lam_in"], 16)

            def gather(e, first):
                if not first:
                    pool.wait_ge(sem["gather_p"], e * 16)
                    pool.wait_ge(sem["gather_s"], e * 16)
                pool.tensor_copy(now_p[:, :], idx_p[:, bass.ds(e, 1)]).then_inc(sem["col_ready"], 1)
                if first:
                    pool.wait_ge(sem["col_ready"], 1)
                    pool.indirect_dma_start(XE, None, hn, bass.IndirectOffsetOnAxis(ap=now_p[:, 0:1], axis=0)).then_inc(sem["gather_p"], 16)
                    pool.wait_ge(sem["idx_ready"], 5)
                pool.tensor_copy(now_s[:, :], idx_s[:, bass.ds(e, 1)]).then_inc(sem["col_ready"], 1)
                if not first:
                    pool.wait_ge(sem["xe_tr"], e * 3)
                pool.wait_ge(sem["col_ready"], e * 2 + 2)
                pool.tensor_tensor(turn[:, :], ones[:, 0:1], ones[:, 0:1], ALU.mult)
                if not first:
                    pool.indirect_dma_start(XE, None, hn, bass.IndirectOffsetOnAxis(ap=now_p[:, 0:1], axis=0)).then_inc(sem["gather_p"], 16)
                pool.indirect_dma_start(XES, None, hn, bass.IndirectOffsetOnAxis(ap=now_s[:, 0:1], axis=0)).then_inc(sem["gather_s"], 16)

            def scatter(e, first):
                if not first:
                    pool.wait_ge(sem["scatter_p"], e * 16)
                    pool.wait_ge(sem["scatter_s"], e * 16)
                pool.tensor_copy(out_p_idx[:, :], idx_p[:, bass.ds(e, 1)]).then_inc(sem["scol_ready"], 1)
                pool.tensor_copy(out_q_idx[:, :], idx_q[:, bass.ds(e, 1)]).then_inc(sem["scol_ready"], 1)
                pool.wait_ge(sem["scol_ready"], e * 2 + 2)
                pool.wait_ge(sem["y_out"], e * 3 + 3)
                pool.tensor_tensor(turn[:, :], ones[:, 0:1], ones[:, 0:1], ALU.mult)
                pool.indirect_dma_start(acc, bass.IndirectOffsetOnAxis(ap=out_p_idx[:, 0:1], axis=0), YP, None,
                                        compute_op=ALU.add).then_inc(sem["scatter_p"], 16)
                pool.indirect_dma_start(acc_quarters, bass.IndirectOffsetOnAxis(ap=out_q_idx[:, 0:1], axis=0), YS, None,
                                        compute_op=ALU.add).then_inc(sem["scatter_s"], 16)

            pool.wait_ge(sem["idx_ready"], 2)
            pool.wait_ge(sem["hn_out_0"], 16 * NT // 2)
            pool.wait_ge(sem["hn_out_1"], 16 * NT // 2)
            pool.wait_ge(sem["acc_out"], 16 * NTP)
            pool.wait_ge(sem["acc_out_s"], 16 * NTS)
            gather(0, True)
            gather(1, False)
            scatter(0, True)
            with pool.Fori(1, NE - 1) as e:
                gather(e + 1, False)
                scatter(e, False)
            scatter(NE - 1, False)

        @block.tensor
        def _(pe):
            def product(out, pairs):
                for n, (l, r) in enumerate(pairs):
                    last = pe.matmul(out, l, r, start=(n == 0), stop=(n == len(pairs) - 1))
                return last

            def wait(name, v):
                pe.wait_ge(sem[name], v)

            wait("vec_in", 16 * 11)
            wait("const_in", 16)
            pe.transpose(PS[:, 0, 0:NV], VROW[0:NV, :], ident[0:NV, 0:NV]).then_inc(sem["vec_tr"], 1)

            def turn_rows(q):
                wait("xn_ready", q + 1)
                for half in range(2):
                    if q >= 1:
                        wait("ut_ready", 2 * (q - 1) + half + 1)
                    for k in range(4):
                        last = pe.transpose(PS[:, 6 + half, k * P:(k + 1) * P], XN[q % 2][:, tiles[4 * half + k]], ident[:, :])
                    last.then_inc(sem["xn_tr"], 1)

            for t in range(NT):
                turn_rows(t)

            def filter_layer(layer, n):
                c0, cn = CHUNKS[n]
                w, h = ((W1F, FEAT), (W2F, H1))[layer]
                if n == 2:
                    wait("mlp_used", 3 * layer + 1)
                product(PS[:, 6 + n % 2, 0:cn], [(w, h[:, c0:c0 + cn])]).then_inc(sem["mlp_mm"], 1)

            def filter_taps(r):
                if r == 0:
                    wait("sin_ready", 2)
                if r in (0, 7):
                    wait("zt_ready", 3 if r == 0 else 6)
                else:
                    wait("h_dve", taps_at(r - 1)[0])
                product(PS[:, 6, :], [(H2[:, tiles[r]], W3F[:, 0:HY])])
                product(PS[:, 7, :], [(H2[:, tiles[r]], W3F[:, HY:2 * HY])]).then_inc(sem["h_mm"], 1)

            def filter_norms():
                wait("sums_ready", 1)
                for s in range(2):
                    for g in range(HG):
                        last = product(PS[:, 6, 4 * s + g:4 * s + g + 1], [(HACC[:, s, tiles[g]], ones[:, 0:1])])
                last.then_inc(sem["norm_mm"], 1)

            def dft(q, c, s):
                b, kind_of_step = 4 * (q % 2), DFT_KIND[q]
                if q >= 2:
                    wait("dft_dve", dft_read(q - 2))
                if q == 5:
                    wait("dft_kept", 2)
                if kind_of_step == 4:
                    for kind in (0, 2, 1, 3):
                        product(PS[:, b + kind, :], [(FWDS[:, kind, :], (c, s)[kind // 2][:, NTP + kind % 2, :])]
                                ).then_inc(sem["dft_mm"], 1)
                elif kind_of_step % 2 == 0:
                    j = kind_of_step // 2
                    for kind in (0, 2, 1, 3):
                        product(PS[:, b + kind, :], [(FWE[:, kind, m, tiles[j]], (c, s)[kind // 2][:, 2 * (kind % 2) + m, :])
                                                     for m in range(2)]).then_inc(sem["dft_mm"], 1)
                else:
                    for n, j in enumerate((kind_of_step // 2, kind_of_step // 2 + 2)):
                        for kind in range(2):
                            product(PS[:, b + 2 * n + kind, :], [(FWO[:, kind, m, tiles[j]], (c, s)[kind][:, 4 + m, :])
                                                                 for m in range(4)]).then_inc(sem["dft_mm"], 1)

            def hyena_chunk(b, n, slot, first_bank):
                c0, cn = CHUNKS[n]
                product(PS[:, first_bank + n, 0:cn], [(HYW[slot][:, k, :], UT[:, k, c0:c0 + cn]) for k in range(KD)]
                        ).then_inc(sem["hy_mm"], 1)

            def turn_z(g):
                wait("z_ready", g + 1)
                for part, (n0, n1) in enumerate(((0, 4), (4, 8), (8, 10))):
                    if part == 2:
                        wait("zt_ready", 3 * g + 1)
                    for r in range(n0, n1):
                        if r < 4:
                            first, end, by = 512 * (r % 2) + 2 * (r // 2), 512 * (r % 2 + 1), 4
                        elif r < NTP:
                            first, end, by = 256 * (r % 4) + 1, 256 * (r % 4 + 1), 2
                        else:
                            first, end, by = LP + r - NTP, T, 2
                        last = pe.transpose(PS[:, 6 + part % 2, (r - n0) * P:(r - n0 + 1) * P],
                                            Z[:, g, first:end:by], ident[:, :])
                    last.then_inc(sem["z_tr"], 1)

            wait("feat_in", 64)
            wait("ut_ready", 2 * NT)
            for n in range(3):
                filter_layer(0, n)
            for b in range(2 * HG):
                wait(f"hy_in_{b % 3}", 16 * (b // 3 + 1))
                if b >= 2:
                    wait("raw_ready", b - 1)
                for n in range(3):
                    hyena_chunk(b, n, b % 3, 3 * (b % 2))
                    for kind, r in BESIDE.get((b, n), []):
                        if kind == "layer":
                            wait("sin_ready", 1)
                            filter_layer(1, r)
                        elif kind == "taps":
                            filter_taps(r)
                        elif kind == "norms":
                            filter_norms()
                        else:
                            if r == 1:
                                wait("h_dve", taps_at(6)[0])
                            if r == 2:
                                wait("invn_ready", 1)
                            turn_z(r)
            wait("h_pool", 2 * NT)
            wait("fwd_in", 48)
            wait("raw_ready", 2 * HG)
            wait("zt_ready", 9)
            dft(0, SF, DF)
            turn_z(HG - 1)
            wait("zt_ready", 3 * HG)
            for q in range(1, 10):
                if DFT_INPUT[q]:
                    dft(q, ZT, ZT)
                else:
                    dft(q, SF, DF)
            wait("dft_dve", dft_read(8))
            loads = [3, 3]

            def first_factor(g):
                if g >= 1:
                    wait("raw_ready", 2 * HG + g)
                loads[g % 2] += 1
                wait(f"hy_in_{g % 2}", 16 * loads[g % 2])
                for n in range(3):
                    hyena_chunk(2 * HG + g, n, 3 + g % 2, 0)

            first_factor(0)
            for g in range(HG):
                if g + 1 < HG:
                    first_factor(g + 1)
                if g == 0:
                    wait("dft_dve", DFT_ALL)
                    wait("inv_in", 48)
                else:
                    wait("inv_used", g)
                product(PS[:, 4, :], [(spectrum(j, 2 + k)[:, tiles[g]], INVO[:, k, j, :]) for k in range(2) for j in range(4)]
                        ).then_inc(sem["inv_mm"], 1)
                if g == 0:
                    wait("dft_pool", 23)
                product(PS[:, 3, 0:256], [(FOLD[:, j, k, tiles[g]], INVE[:, k, j, :]) for k in range(2) for j in range(2)])
                product(PS[:, 3, 256:512], [(spectrum(2 + j, k)[:, tiles[g]], INVE[:, 2 + k, j, :])
                                            for k in range(2) for j in range(2)]).then_inc(sem["inv_mm"], 1)
                for odd in range(2):
                    last = product(PS[:, 5, odd * P:(odd + 1) * P],
                                   [(KSS[:, 2 * odd + s, tiles[g]], INVS[:, 2 * odd + s, :]) for s in range(2)])
                last.then_inc(sem["inv_mm"], 1)

            def project_job(h, j):
                if j == 0:
                    wait("wqk_in", 32 * (h + 1))
                    if h == 0:
                        wait("raw_ready", 3 * HG)
                        wait("inv_used", HG)
                if h and (h > 1 or j):
                    if j:
                        wait("raw_qk", 5 * h + j)
                    else:
                        wait("q_roped", 3 * h)
                        wait("k_roped", 6 * h)
                for n, (part, chunk) in enumerate(RAW_JOBS[j]):
                    c0, cn = CHUNKS[chunk]
                    last = product(PS[:, job_bank(h, j), n * cn:(n + 1) * cn],
                                   [(WQK[h][part][:, k, :], UT[:, k, c0:c0 + cn]) for k in range(KD)])
                last.then_inc(sem["qk_mm"], 1)

            def turn_job(h, j):
                if h == 0 and j == 0:
                    wait("perm_in", 16)
                wait("raw_qk", 5 * (h + 1))
                if h and j:
                    wait("q_roped", roped(h, j)[0])
                    wait("k_roped", roped(h, j)[1])
                for n, (part, chunk) in enumerate(TURN_JOBS[j]):
                    c0, cn = CHUNKS[chunk]
                    last = product(PS[:, job_bank(h, j), n * cn:(n + 1) * cn], [(perm[:, :], QKRAW[part][:, c0:c0 + cn])])
                last.then_inc(sem["pm_mm"], 1)

            def scores(u):
                h, i = u // NT, query_tile(u)
                q, *both = QK[h % 2]
                k0, kn = keys(i)
                if u % NT in (0, 2):
                    ready = roped(h, 5 if u % NT else 3)
                    wait("q_roped", ready[0])
                    wait("k_roped", ready[1])
                for c, kk in enumerate(both):
                    if u >= 1:
                        wait("exp_ready", 2 * (u - 1) + c + 1)
                    for n in range(0, kn, 512):
                        m = min(512, kn - n)
                        last = product(PS[:, 2 * c + n // 512, 0:m], [(q[:, tiles[i]], kk[:, k0 + n:k0 + n + m])])
                    last.then_inc(sem["s_mm"], 1)

            def turn_map(u):
                before, groups = turned(u)
                wait("w_ready", u + 1)
                for g in range(groups):
                    if u >= 1:
                        wait("wt_ready", turned(u - 1)[0] + min(g + 1, turned(u - 1)[1]))
                    for m in range(4 * g, min(4 * g + 4, keys(query_tile(u))[1] // P)):
                        last = pe.transpose(PS[:, 4 + g, (m % 4) * P:(m % 4 + 1) * P], PP[u % 2][0][:, tiles[m]], ident[:, :])
                    last.then_inc(sem["w_tr"], 1)

            def values(u):
                h, i = u // NT, query_tile(u)
                k0, kn = keys(i)
                before, groups = turned(u)
                if u >= 1:
                    wait("o_ready", u)
                wait("wt_ready", before + groups)
                product(PS[:, 6, (u % 4) * P:(u % 4 + 1) * P],
                        [(WT[u % 2][:, m, :], V[:, k0 // P + m, tiles[h]]) for m in range(kn // P)]).then_inc(sem["pv_mm"], 1)

            for j in range(5):
                project_job(0, j)
            wait("wv_in", 16)
            for t in range(NT):
                if t >= 2:
                    wait("v_ready", t - 1)
                product(PS[:, 6 + t % 2, :], [(UT[:, k, tiles[t]], WV[:, k, :]) for k in range(KD)]).then_inc(sem["v_mm"], 1)
                if t == 1:
                    for j in range(5):
                        turn_job(0, j)
            wait("q_roped", 3)
            wait("k_roped", 6)
            wait("v_ready", NT)
            scores(0)
            for u in range(UNITS):
                if u + 1 < UNITS:
                    scores(u + 1)
                if u >= 1:
                    values(u - 1)
                turn_map(u)
                h, i = u // NT + 1, u % NT
                if h < HEADS:
                    project_job(h, i) if i < 5 else turn_job(h, i - 5)
            values(UNITS - 1)

            def merge_gates(b, n):
                s, (c0, cn) = 4 * ((b + n) % 2), CHUNKS[n]
                for part in range(2):
                    product(PS[:, s + part, 0:cn], [(MGW[b][part][:, k, :], UT[:, k, c0:c0 + cn]) for k in range(KD)])

            wait("mg_in_0", 64)
            wait("exp_ready", 2 * UNITS)
            merge_gates(0, 0)
            wait("wt_ready", W_HEAD * HEADS)
            merge_gates(0, 1)
            wait("o_ready", UNITS)
            wait("sub_ready", 1)
            for q in range(3 * HEADS):
                h, n = q // 3, q % 3
                if q >= 4:
                    wait("at_ready", q - 3)
                for t in range(4 * n, min(4 * n + 4, NT)):
                    last = pe.transpose(PS[:, SUB_BANKS[q % 4], (t % 4) * P:(t % 4 + 1) * P], AO[:, t, tiles[h]], ident[:, :])
                last.then_inc(sem["sub_tr"], 1)
            wait("at_ready", 3 * HEADS)

            def merge(B, b, first):
                wait(f"mg_in_{b}", (B - b) * 32 + 64)
                wa, wh = MGW[b][2:]
                for n, (c0, cn) in enumerate(CHUNKS):
                    s = 4 * ((b + n) % 2)
                    if not (first and 3 * b + n < 2):
                        wait("m_ready", B * 3 + (n - 1))
                    if not (first and 3 * b + n < 2):
                        merge_gates(b, n)
                    product(PS[:, s + 2, 0:cn], [(wa[:, k, :], AT[:, k, c0:c0 + cn]) for k in range(HG)])
                    product(PS[:, s + 3, 0:cn], [(wh[:, k, :], Z[:, k, c0:c0 + cn]) for k in range(HG)]).then_inc(sem["mg_mm"], 1)

            wait("hz_ready", HG)
            merge(0, 0, True)
            merge(1, 1, True)
            with pe.Fori(1, KD // 2) as c:
                for b in range(2):
                    merge(c * 2 + b, b, False)
            wait("m_ready", 3 * KD - 1)
            wait("wo_in", 32)
            for q in range(2 * NT):
                t, n = q // 2, q % 2
                if q == 4:
                    wait("m_ready", 3 * KD)
                if q >= 6:
                    wait("x1_ready", q - 5)
                product(PS[:, q % 6, :], [(MT[:, k, tiles[t]], WO[n][:, k, :]) for k in range(KD)]
                        ).then_inc(sem["wo_mm"], 1)
                if 1 <= q <= 4:
                    turn_rows(N_MEM + q - 1)
                if q in (5, 6):
                    turn_rows(N_X + q - 5)
                if q >= 7 and q % 2:
                    turn_rows(N_X + (q - 3) // 2)

            def cross_project(B, b, first):
                wait(f"xb_in_{b}", (B - b) * 16 + 32)
                if not first:
                    wait("q_ready", B * 3 - 3)
                    wait("xk_ready", B - 1)
                for n, (c0, cn) in enumerate(CHUNKS):
                    if first and b == 0:
                        wait("x1_ready", min(2 * NT - 1 + n, 2 * NT))
                        if n == 2:
                            turn_rows(N_X + NT - 1)
                            wait("ut_ready", 2 * N_FFN)
                        else:
                            wait("ut_ready", 2 * (N_X + 4 * n + 4))
                    product(PS[:, 4 * b + n, 0:cn], [(XQW[b][:, k, :], U2T[:, k, c0:c0 + cn]) for k in range(KD)]
                            ).then_inc(sem["xb_mm"], 1)
                product(PS[:, 4 * b + 3, :], [(XKW[b][:, k, :], MEMT[:, k, :]) for k in range(KD)]).then_inc(sem["xb_mm"], 1)

            cross_project(0, 0, True)
            cross_project(1, 1, True)
            with pe.Fori(1, KD // 2) as c:
                for b in range(2):
                    cross_project(c * 2 + b, b, False)

            wait("q_ready", 3 * KD - 3)
            wait("xk_ready", KD - 1)
            for q in range(8):
                m, n = q % 4, q // 4
                wait(f"wxv_in_{n}", 16)
                if q >= 4:
                    wait("vm_ready", q - 3)
                product(PS[:, q % 4, :], [(MEMT[:, k, tiles[m]], WXV[n][:, k, :]) for k in range(KD)]).then_inc(sem["vm_mm"], 1)

            def cross_scores(i):
                t = XORDER[i]
                m0 = 0 if t < NTP else NMEM
                if i >= 2:
                    wait("xexp_ready", 4 * (i - 1))
                for hx in range(XH):
                    last = product(PS[:, 2 * (i % 2) + hx // 2, (hx % 2) * NMEM:(hx % 2 + 1) * NMEM],
                                   [(QX[:, 2 * hx + j, tiles[t]], KX[:, 2 * hx + j, m0:m0 + NMEM]) for j in range(2)])
                last.then_inc(sem["xs_mm"], 1)

            def cross_turn(i):
                wait("xp_ready", i + 1)
                for half in range(2):
                    if i >= 1:
                        wait("pt_ready", 2 * (i - 1) + half + 1)
                    for o in range(4 * half, 4 * half + 4):
                        last = pe.transpose(PS[:, 4 + half, (o % 4) * P:(o % 4 + 1) * P],
                                            XP[i % 2][:, o // 2, (o % 2) * P:(o % 2 + 1) * P], ident[:, :])
                    last.then_inc(sem["xp_tr"], 1)

            def cross_values(i):
                m0 = 0 if XORDER[i] < NTP else 2
                wait("pt_ready", 2 * i + 2)
                for half in range(2):
                    if i >= 1:
                        wait("ot_ready", 2 * (i - 1) + half + 1)
                    for o in range(4 * half, 4 * half + 4):
                        hx = o // 2
                        last = product(PS[:, 6 + half, (o % 4) * P:(o % 4 + 1) * P],
                                       [(VM[:, m0 + j, tiles[o]], PT[i % 2][:, 2 * hx + j, :]) for j in range(2)])
                    last.then_inc(sem["xo_mm"], 1)

            def cross_project_out(q):
                t, n = XO_JOBS[q]
                wait(f"wx_in_{n}", 16)
                wait("ot_ready", 2 * XORDER.index(t) + 2)
                if q >= 4:
                    wait("x2_ready", q - 3 if q < XO_PROMPT + 2 else q - 1)
                product(PS[:, xo_bank(q), :], [(OT[:, k, tiles[t]], WXO[n][:, k, :]) for k in range(KD)]).then_inc(sem["xo2_mm"], 1)

            wait("q_ready", 3 * KD)
            wait("xk_ready", KD)
            wait("vm_ready", 8)
            cross_scores(0)
            for i in range(NT):
                if i + 1 < NT:
                    cross_scores(i + 1)
                if i >= 1:
                    cross_values(i - 1)
                if i == NT - 1:
                    cross_project_out(0)
                cross_turn(i)
            cross_project_out(1)
            cross_values(NT - 1)

            def route(t):
                wait("ut_ready", 2 * (N_FFN + t) + 2)
                s = logit_slot(t)
                product(PS[:, 4, s * NE:(s + 1) * NE], [(HT[:, k, tiles[t]], rw[:, k, :]) for k in range(KD)]).then_inc(sem["rt_mm"], 1)

            wait("wr_in", 16)
            for q in range(2, XO_PROMPT):
                cross_project_out(q)
                if q in X2_AT:
                    turn_rows(N_FFN + X2_AT.index(q))
                if q - 1 in X2_AT:
                    route(X2_AT.index(q - 1))
            turn_rows(N_FFN + NTP - 1)
            route(NTP - 1)
            wait("aff_ready", 1)
            for m in range(NTP // 2):
                last = pe.transpose(PS[0:2 * NE, 2, m * P:(m + 1) * P],
                                    LG[:, 2 * m:2 * m + 2, :].rearrange("p h e -> p (h e)"), ident[:, :])
            last.then_inc(sem["aff_tr"], 1)
            for q in range(XO_PROMPT, 2 * NT):
                cross_project_out(q)
                if q == X2_AT[NTP]:
                    turn_rows(N_FFN + NTP)
            route(NTP)
            turn_rows(N_FFN + NT - 1)
            route(NT - 1)
            wait("slots_ready", 1)
            pe.transpose(PS[:, 3, 0:2 * NE], SLOT_P, ident[0:2 * NE, 0:2 * NE])
            pe.transpose(PS[:, 3, 2 * NE:4 * NE], VALP, ident[0:2 * NE, 0:2 * NE]).then_inc(sem["slots_tr"], 1)
            wait("aff_ready", 2)
            for m in range(NTS):
                last = pe.transpose(PS[0:NE, 5, m * P:(m + 1) * P], LG[:, NTP + m, :], ident[:, :])
            last.then_inc(sem["aff_tr"], 1)
            wait("rev_in", 16)
            wait("sorted_ready", 1)
            product(PS[:, 2, 0:4 * NE], [(perm[:, :], SORTED.rearrange("p k h -> p (k h)"))]).then_inc(sem["reversed"], 1)
            wait("slots_ready", 2)
            pe.transpose(PS[0:CS, 4, 0:NE], SLOT_I[:, 0:CS], ident[0:NE, 0:NE])
            pe.transpose(PS[:, 4, NE:2 * NE], SLOT_I[:, CS:CS + P], ident[0:NE, 0:NE])
            pe.transpose(PS[:, 4, 2 * NE:3 * NE], SLOT_V[:, CS:CS + P], ident[0:NE, 0:NE]).then_inc(sem["idx_tr"], 1)

            def turn_slots(e, first):
                if first:
                    wait("idx_ready", 5)
                wait("gather_p", e * 16 + 16)
                wait("gather_s", e * 16 + 16)
                if not first:
                    wait("xet_ready", e * 3)
                for half in range(2):
                    for k in range(4 * half, 4 * half + 4):
                        last = pe.transpose(PS[:, 3 + half, (k % 4) * P:(k % 4 + 1) * P], XE[:, tiles[k]], ident[:, :])
                    last.then_inc(sem["xe_tr"], 1)
                for k in range(KD):
                    last = pe.transpose(PS[:, 5, k * CS:(k + 1) * CS], XES[:, tiles[k]], ident[0:CS, 0:CS])
                last.then_inc(sem["xe_tr"], 1)

            def gate_up(e, first):
                wait("xet_ready", e * 3 + 3)
                for f in range(FF // P):
                    if f % 4 == 0:
                        wait(f"eg{f // 4}", e * 16 + 16)
                        wait(f"eu{f // 4}", e * 16 + 16)
                    if not (first and f < 3):
                        wait("he_ready", e * 8 + (f - 2))
                    for part, w in enumerate((WG, WU)):
                        last = product(PS[:, f % 3, part * CE:(part + 1) * CE],
                                       [(w[f // 4][:, k, tiles[f % 4]], XET[:, k, :]) for k in range(KD)])
                    last.then_inc(sem["gu_mm"], 1)

            def down(e, first, last_one):
                wait("he_ready", e * 8 + 8)
                if not first:
                    wait("y_out", e * 3)
                for n in range(2):
                    wait(f"ed{n}", e * 16 + 16)
                    product(PS[:, 6 + n, :], [(HE[:, f, 0:CP], WD[n][:, f, :]) for f in range(FF // P)]).then_inc(sem["dn_mm"], 1)
                if not last_one:
                    wait("xet_ready", e * 3 + 6)
                for f in range(FF // P):
                    for j in range(4):
                        last = pe.matmul(PS[CS * j:CS * (j + 1), 5, 0:256], HE[:, f, CP:CE],
                                         WD[j // 2][:, f, (j % 2) * 256:(j % 2 + 1) * 256],
                                         start=(f == 0), stop=(f == FF // P - 1), tile_position=(0, CS * j))
                last.then_inc(sem["dn_mm"], 1)

            turn_slots(0, True)
            gate_up(0, True)
            turn_slots(1, False)
            down(0, True, False)
            with pe.Fori(1, NE - 1) as e:
                gate_up(e, False)
                wait("y_out", e * 3)
                turn_slots(e + 1, False)
                down(e, False, False)
            gate_up(NE - 1, False)
            down(NE - 1, False, True)

        @block.scalar
        def _(act):
            steps = Count(act, sem["norm_act"])

            def normed(q, src):
                col = q % 16
                if q:
                    steps.wait()
                steps.inc(act.activation(SQJ, src, ACT.Square, accum_out=stat[:, 0, col:col + 1]))
                steps.wait()
                steps.inc(act.activation(stat[:, 1, col:col + 1], stat[:, 0, col:col + 1], ACT.Sqrt, scale=1.0 / D, bias=eps[:, 0:1]))

            act.wait_ge(sem["vec_zero"], 1)
            for t in range(NT):
                act.wait_ge(sem[f"x_in_{t // 2}"], 16)
                normed(t, XS[:, t, :])

            def sines(layer):
                act.wait_ge(sem["arg_ready"], layer + 1)
                act.activation((H1, H2)[layer], ARG, ACT.Sin).then_inc(sem["sin_ready"], 1)

            def magnitudes(r):
                act.wait_ge(sem["h_dve"], taps_at(r)[1])
                if r >= 1:
                    act.wait_ge(sem["taps_sum"], taps_summed(r - 1))
                act.activation(HAB, TAP[:, r % 2, :, :], ACT.Abs).then_inc(sem["tap_abs"], 1)

            def spectra(q):
                e = DFT_COPIED.index(q)
                for n, kind in enumerate((0, 2)):
                    act.wait_ge(sem["dft_mm"], 4 * q + n + 1)
                    if e:
                        act.wait_ge(sem["dft_dve"], dft_read(DFT_COPIED[e - 1]))
                    act.copy(TE[q][:, n, :], PS[:, 4 * (q % 2) + kind, :]).then_inc(sem["dft_act"], 1)

            def raw_chunk(b, n, raw, first_bank):
                off, cn = (1, 513, LP + 3)[n], CHUNKS[n][1]
                act.wait_ge(sem["hy_mm"], 3 * b + n + 1)
                ins = act.copy(raw[:, off:off + cn], PS[:, first_bank + n, 0:cn])
                if n == 2:
                    ins.then_inc(sem["raw_ready"], 1)

            def z_out(g):
                for part, (n0, n1) in enumerate(((0, 4), (4, 8), (8, 10))):
                    act.wait_ge(sem["z_tr"], 3 * g + part + 1)
                    act.copy(ZT[:, n0:n1, tiles[g]], bank4(6 + part % 2)[:, 0:n1 - n0, :]).then_inc(sem["zt_ready"], 1)

            sines(0)
            act.wait_ge(sem["pad_zero"], 7)
            for b in range(2 * HG):
                if b >= 2:
                    act.wait_ge(sem["conv_done"], b - 1)
                for n in range(3):
                    raw_chunk(b, n, RAW[b % 2], 3 * (b % 2))
                    for kind, r in BESIDE.get((b, n), []):
                        if kind == "taps":
                            magnitudes(r)
                        elif kind == "turn":
                            z_out(r)
                        elif (kind, r) == ("layer", 2):
                            sines(1)
            spectra(0)
            z_out(HG - 1)
            for q in range(1, 10):
                if q in DFT_COPIED:
                    spectra(q)
                elif DFT_INPUT[q]:
                    for n in range(2):
                        act.wait_ge(sem["dft_mm"], 4 * q + 3 + n)
                        if q == 9:
                            act.wait_ge(sem["dft_dve"], DFT_PRODUCTS[1][2])
                        act.copy(FOLD[:, 1, n, :], PS[:, 4 * (q % 2) + 2 + n, :]).then_inc(sem["dft_kept"], 1)
            act.wait_ge(sem["pad_zero"], 11)
            for g in range(HG):
                if g >= 1:
                    act.wait_ge(sem["conv_done"], 2 * HG + g)
                for n in range(3):
                    raw_chunk(2 * HG + g, n, RAW0, 0)
            act.wait_ge(sem["lam_sum"], 2)
            act.activation(lam[:, 2:4], lam[:, 0:2], ACT.Exp).then_inc(sem["lam_exp"], 1)

            def raw_out_job(h, j):
                act.wait_ge(sem["qk_mm"], 5 * h + j + 1)
                if h and j == 0:
                    act.wait_ge(sem["q_roped"], 3 * h)
                    act.wait_ge(sem["k_roped"], 6 * h)
                for n, (part, chunk) in enumerate(RAW_JOBS[j]):
                    c0, cn = CHUNKS[chunk]
                    last = act.copy(QKRAW[part][:, c0:c0 + cn], PS[:, job_bank(h, j), n * cn:(n + 1) * cn])
                last.then_inc(sem["raw_qk"], 1)

            def exps(u):
                kn = keys(query_tile(u))[1]
                for c in range(2):
                    act.wait_ge(sem["smax_ready"], 2 * u + c + 1)
                    if u >= 2:
                        act.wait_ge(sem["w_tr"], sum(turned(u - 2)))
                    s = PS[:, 2 * c:2 * c + 2, :].rearrange("p b n -> p (b n)")[:, 0:kn]
                    act.activation(PP[u % 2][c][:, 0:kn], s, ACT.Exp, bias=att[:, u % 2, 1, c:c + 1], scale=DH ** -0.5,
                                   accum_out=att[:, u % 2, 2, c:c + 1]).then_inc(sem["exp_ready"], 1)

            def maps(u):
                before, groups = turned(u)
                for g in range(groups):
                    act.wait_ge(sem["w_tr"], before + g + 1)
                    if u >= 2:
                        act.wait_ge(sem["pv_mm"], u - 1)
                    m = min(4, keys(query_tile(u))[1] // P - 4 * g)
                    act.copy(WT[u % 2][:, 4 * g:4 * g + m, :], bank4(4 + g)[:, 0:m, :]).then_inc(sem["wt_ready"], 1)

            for j in range(5):
                raw_out_job(0, j)
            for t in range(NT):
                act.wait_ge(sem["v_mm"], t + 1)
                act.copy(V[:, t, :], PS[:, 6 + t % 2, :]).then_inc(sem["v_ready"], 1)
            exps(0)
            for u in range(UNITS):
                if u + 1 < UNITS:
                    exps(u + 1)
                maps(u)
                if u // NT + 1 < HEADS and u % NT < 5:
                    raw_out_job(u // NT + 1, u % NT)
            act.wait_ge(sem["sub_sum"], 1)
            act.activation(sub[:, 1, :], sub[:, 0, :], ACT.Sqrt, scale=1.0 / DV, bias=eps[:, 0:1]).then_inc(sem["sub_root"], 1)

            def gates_out(B, b, first):
                for n, (c0, cn) in enumerate(CHUNKS):
                    s = (b + n) % 2
                    act.wait_ge(sem["mg_mm"], B * 3 + (n + 1))
                    if not (first and 3 * b + n < 2):
                        act.wait_ge(sem["m_ready"], B * 3 + (n - 1))
                    for part in range(2):
                        act.activation(SG[:, s, part, 0:cn], PS[:, 4 * s + part, 0:cn], ACT.Sigmoid).then_inc(sem["mg_sig"], 1)

            gates_out(0, 0, True)
            gates_out(1, 1, True)
            with act.Fori(1, KD // 2) as c:
                for b in range(2):
                    gates_out(c * 2 + b, b, False)
            for m in range(4):
                act.wait_ge(sem[f"mem_in_{m // 2}"], 16)
                normed(N_MEM + m, MS[:, m, :])
            for t in range(NT):
                act.wait_ge(sem["x1_ready"], 2 * t + 2)
                normed(N_X + t, X[:, t, :])

            def queries_out(B, b):
                for n, (c0, cn) in enumerate(CHUNKS):
                    act.wait_ge(sem["xb_mm"], B * 4 + (n + 1))
                    act.copy(QX[:, bass.ds(B, 1), c0:c0 + cn].rearrange("p a n -> p (a n)"), PS[:, 4 * b + n, 0:cn]).then_inc(sem["q_ready"], 1)

            queries_out(0, 0)
            queries_out(1, 1)
            with act.Fori(1, KD // 2) as c:
                for b in range(2):
                    queries_out(c * 2 + b, b)

            def cross_exps(i):
                act.wait_ge(sem["xmax_ready"], i + 1)
                if i >= 2:
                    act.wait_ge(sem["xp_tr"], 2 * (i - 1))
                for hx in range(XH):
                    act.activation(XP[i % 2][:, hx, :], PS[:, 2 * (i % 2) + hx // 2, (hx % 2) * NMEM:(hx % 2 + 1) * NMEM],
                                   ACT.Exp, bias=att[:, i % 2, 1, hx:hx + 1], scale=XD ** -0.5,
                                   accum_out=att[:, i % 2, 2, hx:hx + 1]).then_inc(sem["xexp_ready"], 1)

            cross_exps(0)
            for i in range(NT):
                if i + 1 < NT:
                    cross_exps(i + 1)
                for half in range(2):
                    act.wait_ge(sem["xp_tr"], 2 * i + half + 1)
                    if i >= 2:
                        act.wait_ge(sem["xo_mm"], 2 * (i - 1))
                    act.copy(PT[i % 2][:, 4 * half:4 * half + 4, :], bank4(4 + half)).then_inc(sem["pt_ready"], 1)
            for t in range(NT):
                act.wait_ge(sem["x2_ready"], X2_AT[t])
                normed(N_FFN + t, X[:, t, :])
                if t == NTP - 1:
                    act.wait_ge(sem["rt_low"], 1)
                    act.activation(LG[:, 0:NTP, :], LG[:, 0:NTP, :], ACT.Exp).then_inc(sem["rt_exp"], 1)
            act.wait_ge(sem["rt_low"], 2)
            act.activation(LG[:, NTP:NT, :], LG[:, NTP:NT, :], ACT.Exp).then_inc(sem["rt_exp"], 1)

            def silus(e, first):
                for f in range(FF // P):
                    act.wait_ge(sem["gu_mm"], e * 8 + (f + 1))
                    if not (first and f < 2):
                        act.wait_ge(sem["he_ready"], e * 8 + (f - 1))
                    act.activation(SL[:, f % 2, :], PS[:, f % 3, 0:CE], ACT.Silu).then_inc(sem["silu_ready"], 1)

            silus(0, True)
            with act.Fori(1, NE) as e:
                silus(e, False)
            fin = Count(act, sem["fin_act"])
            for t in range(NT):
                act.wait_ge(sem[f"fin_in_{t // 2}"], 16)
                if t:
                    fin.wait()
                fin.inc(act.activation(SQJ, FIN[t], ACT.Square, accum_out=stat[:, 0, t:t + 1]))
                fin.wait()
                fin.inc(act.activation(stat[:, 1, t:t + 1], stat[:, 0, t:t + 1], ACT.Sqrt, scale=1.0 / D, bias=eps[:, 0:1]))

        @block.vector
        def _(dve):
            dve.memset(VROW, 0.0)
            dve.memset(eps[:, :], EPS)
            dve.memset(FEAT, 0.0)
            dve.memset(at(145, 5 * 256), 0.0)
            dve.memset(ones[:, :], 1.0).then_inc(sem["vec_zero"], 1)
            for raw in RAW:
                for c0, c1 in ((0, 1), (LP + 1, LP + 3), (LP + LS + 3, LP + LS + 4)):
                    dve.memset(raw[:, c0:c1], 0.0).then_inc(sem["pad_zero"], 1)
            dve.memset(att[:, :, :, :], 0.0).then_inc(sem["pad_zero"], 1)
            dve.wait_ge(sem["vec_tr"], 1)
            dve.tensor_copy(vec[:, :], PS[:, 0, 0:NV]).then_inc(sem["vec_ready"], 1)
            dve.wait_ge(sem["vec_ready"], 1)

            step = Count(dve, sem["dve_step"])

            def scaled(q, src, stored):
                dve.wait_ge(sem["norm_act"], 2 * q + 2)
                col = slice(q % 16, q % 16 + 1)
                dve.reciprocal(stat[:, 2, col], stat[:, 1, col]).then_inc(sem["root_rec"], 1)
                if q >= 2:
                    dve.wait_ge(sem["xn_tr"], 2 * (q - 1))
                if stored and q >= N_FFN + 2:
                    dve.wait_ge(sem[f"hn_out_{q % 2}"], 16 * ((q - N_FFN) // 2))
                dve.wait_ge(sem["root_rec"], q + 1)
                dve.tensor_scalar(XN[q % 2], src, stat[:, 2, col], None, ALU.mult).then_inc(sem["xn_ready"], 1)

            def rows_in(q, dst, t, gain):
                for half in range(2):
                    dve.wait_ge(sem["xn_tr"], 2 * q + half + 1)
                    g = vec[:, gain + 4 * half:gain + 4 * half + 4]
                    dve.tensor_tensor(dst[:, 4 * half:4 * half + 4, tiles[t]], bank4(6 + half), wide(g, P), ALU.mult).then_inc(sem["ut_ready"], 1)

            def norm_stage(q0, n, src, dst, gain, stored=False):
                scaled(q0, src(0), stored)
                for t in range(n):
                    if t + 1 < n:
                        scaled(q0 + t + 1, src(t + 1), stored)
                    rows_in(q0 + t, dst, t, gain)

            norm_stage(0, NT, lambda t: XS[:, t, :], UT, V_MIX)

            def angles(layer):
                c, vb = step, (V_B1, V_B2)[layer]
                if layer:
                    dve.wait_ge(sem["sin_ready"], 1)
                for n, (c0, cn) in enumerate(CHUNKS):
                    dve.wait_ge(sem["mlp_mm"], 3 * layer + n + 1)
                    dve.tensor_scalar(ARG[:, c0:c0 + cn], PS[:, 6 + n % 2, 0:cn], vec[:, vb:vb + 1], vec[:, V_FREQ:V_FREQ + 1],
                                      ALU.add, ALU.mult).then_inc(sem["mlp_used"], 1)
                dve.wait_ge(sem["mlp_used"], 3 * layer + 3)
                c.inc(dve.tensor_scalar(RND, ARG, INV_2PI, ROUND, ALU.mult, ALU.add))
                c.wait()
                c.inc(dve.tensor_scalar(RND, RND, ROUND, None, ALU.subtract))
                for part in (TWO_PI_A, TWO_PI_B):
                    c.wait()
                    c.inc(dve.scalar_tensor_tensor(ARG, RND, -part, ARG, ALU.mult, ALU.add))
                c.wait()
                dve.tensor_scalar(ARG, ARG, PI_LOW, -PI_LOW, ALU.min, ALU.max).then_inc(sem["arg_ready"], 1)

            taps, sums = Count(dve, sem["h_dve"]), Count(dve, sem["taps_sum"])

            def decayed(r):
                if r == 0:
                    dve.wait_ge(sem["decay_in"], 16)
                else:
                    taps.wait()
                dve.wait_ge(sem["h_mm"], r + 1)
                if r >= 2:
                    dve.wait_ge(sem["h_pool"], 2 * (r - 1))
                for side in range(2):
                    taps.inc(dve.tensor_tensor(TAP[:, r % 2, side, :], PS[:, 6 + side, :], DEC[:, r, :], ALU.mult))
                assert taps.value() == taps_at(r)[0]
                taps.wait()
                if r in (0, NTP):
                    taps.inc(dve.memset(TAP[0:1, r % 2, 1, :], 0.0))
                    taps.wait()
                assert taps.value() == taps_at(r)[1]
                into = HACC[:, r // NTP, :]
                dve.wait_ge(sem["tap_abs"], r + 1)
                if r in (0, NTP):
                    sums.inc(dve.tensor_tensor(into, HAB[:, 0, :], HAB[:, 1, :], ALU.add))
                else:
                    for side in range(2):
                        sums.wait()
                        sums.inc(dve.tensor_tensor(into, HAB[:, side, :], into, ALU.add))
                assert sums.value() == taps_summed(r)

            conv, done = step, Count(dve, sem["conv_done"])

            def short_conv(b, raw, to, channel_tile):
                dve.wait_ge(sem["raw_ready"], b + 1)
                col = [V_CW + 12 * k + channel_tile for k in range(3)]
                segs = ((1, 0, LP), (LP + 3, LP, LS))
                for off, o, n in segs:
                    conv.inc(dve.tensor_scalar(to[:, o:o + n], raw[:, off:off + n], vec[:, col[1]:col[1] + 1],
                                               vec[:, V_CB + channel_tile:V_CB + channel_tile + 1], ALU.mult, ALU.add))
                for k, shift in ((0, -1), (2, 1)):
                    for m, (off, o, n) in enumerate(segs):
                        conv.wait()
                        ins = dve.scalar_tensor_tensor(to[:, o:o + n], raw[:, off + shift:off + shift + n], vec[:, col[k]:col[k] + 1],
                                                       to[:, o:o + n], ALU.mult, ALU.add)
                        (done if k == 2 and m == 1 else conv).inc(ins)
                done.wait()

            def hyena_input(b):
                g = b // 2
                if b % 2 == 0:
                    short_conv(b, RAW[0], CX, HG + g)
                else:
                    short_conv(b, RAW[1], CH, 2 * HG + g)
                    dve.tensor_tensor(Z[:, g, :], CX, CH, ALU.mult).then_inc(sem["z_ready"], 1)
                    dve.wait_ge(sem["z_ready"], g + 1)

            angles(0)
            hyena_input(0)
            angles(1)
            hyena_input(1)
            hyena_input(2)
            for b, tiles_before in ((3, (0, 1)), (4, (2, 3, 4)), (5, (5, 6)), (6, (7, 8))):
                for r in tiles_before:
                    decayed(r)
                hyena_input(b)
            decayed(9)
            sums.wait()
            dve.memset(lam[:, :], 0.0).then_inc(sem["sums_ready"], 1)
            dve.wait_ge(sem["norm_mm"], 1)
            dve.reciprocal(invn[:, :, :].rearrange("p a b -> p (a b)"), PS[:, 6, 0:2 * HG]).then_inc(sem["invn_ready"], 1)
            hyena_input(7)

            spec = Count(dve, sem["dft_dve"])

            def butterflies(cos, cos2, sin, sin2, to):
                if spec.value():
                    spec.wait()
                spec.inc(dve.tensor_tensor(to[0], cos, cos2, ALU.add))
                spec.inc(dve.tensor_tensor(to[1], cos, cos2, ALU.subtract))
                spec.inc(dve.tensor_tensor(to[2], sin2, sin, ALU.add))
                spec.inc(dve.tensor_tensor(to[3], sin2, sin, ALU.subtract))

            def copied(q, to):
                b, te = 4 * (q % 2), TE[q]
                dve.wait_ge(sem["dft_act"], 2 * DFT_COPIED.index(q) + 2)
                dve.wait_ge(sem["dft_mm"], 4 * q + 4)
                butterflies(te[:, 0, :], PS[:, b + 1, :], te[:, 1, :], PS[:, b + 3, :], to)

            def odd_added(q, n, to):
                b = 4 * (q % 2) + 2 * n
                cos2, sin2 = PS[:, b, :], PS[:, b + 1, :]
                dve.wait_ge(sem["dft_mm"], 4 * q + 2 * n + 2)
                if DFT_INPUT[q] and n:
                    dve.wait_ge(sem["dft_kept"], 2 if q == 3 else 4)
                    cos2, sin2 = FOLD[:, 1, 0, :], FOLD[:, 1, 1, :]
                butterflies(HALF[:, n, :], cos2, HALF[:, 2 + n, :], sin2, to)

            half = [HALF[:, m, :] for m in range(4)]
            A0, A1, B0, B1 = (AB[:, m, :] for m in range(4))

            def multiplied(tile, T0):
                P0, P1, Q0, Q1 = (spectrum(tile, m) for m in range(4))
                for out, l, r, op in ((T0, A0, P0, ALU.mult), (T1, B0, Q0, ALU.mult), (T0, T0, T1, ALU.subtract),
                                      (T1, A0, Q0, ALU.mult), (A0, B0, P0, ALU.mult), (T1, T1, A0, ALU.add),
                                      (B0, A1, Q1, ALU.mult), (A0, B1, P1, ALU.mult), (B0, B0, A0, ALU.add)):
                    spec.wait()
                    spec.inc(dve.tensor_tensor(out, l, r, op))
                dve.wait_ge(sem["dft_pool"], product_done(tile))
                spec.wait()
                spec.inc(dve.tensor_tensor(P0, T0, half[0], ALU.add))
                spec.inc(dve.tensor_tensor(P1, T1, B0, ALU.subtract))
                spec.inc(dve.tensor_tensor(Q0, T0, half[0], ALU.subtract))
                spec.inc(dve.tensor_tensor(Q1, T1, B0, ALU.add))

            for q in range(10):
                j, odd = DFT_KIND[q] // 2, DFT_KIND[q] % 2
                if j == 2 and DFT_INPUT[q]:
                    copied(q, [A0, A1, B0, B1])
                    multiplied(4, T0[1])
                elif j == 2:
                    copied(q, [spectrum(4, m) for m in range(4)])
                elif not odd:
                    copied(q, half)
                elif not DFT_INPUT[q]:
                    for n in range(2):
                        odd_added(q, n, [spectrum(j + 2 * n, m) for m in range(4)])
                else:
                    for n in range(2):
                        odd_added(q, n, [A0, A1, B0, B1])
                        multiplied(j + 2 * n, T0[q // 6])
                assert spec.value() == sum(DFT_STEPS[:q + 1])
            for c0, c1 in ((0, 1), (LP + 1, LP + 3), (LP + LS + 3, LP + LS + 4)):
                dve.memset(RAW0[:, c0:c1], 0.0).then_inc(sem["pad_zero"], 1)
            dve.memset(stat[:, :, :], 0.0).then_inc(sem["pad_zero"], 1)

            hz = step
            for g in range(HG):
                short_conv(2 * HG + g, RAW0, CX0, g)
                hz.inc(dve.tensor_scalar(Z[:, g, :], Z[:, g, :], vec[:, V_FB + g:V_FB + g + 1], None, ALU.mult))
                hz.wait()
                dve.wait_ge(sem["inv_mm"], 3 * g + 3)
                for odd in range(2):
                    for s, bank, c0, c1, o, n in ((0, 3 + odd, 0, 512, 0, LP), (1, 5, odd * P, (odd + 1) * P, LP, LS)):
                        dst, src = Z[:, g, o + odd:o + n:2], PS[:, bank, c0:c1]
                        if not odd and not s:
                            dst, src = dst.rearrange("p (i r) -> p r i", r=2), src.rearrange("p (r i) -> p r i", r=2)
                        ins = dve.scalar_tensor_tensor(dst, src, invn[:, s, g:g + 1], dst, ALU.mult, ALU.add)
                        if odd and s:
                            ins.then_inc(sem["inv_used"], 1)
                        else:
                            hz.inc(ins)
                dve.wait_ge(sem["inv_used"], g + 1)
                dve.tensor_tensor(Z[:, g, :], Z[:, g, :], CX0, ALU.mult).then_inc(sem["hz_ready"], 1)
                dve.wait_ge(sem["hz_ready"], g + 1)

            c = step
            dve.wait_ge(sem["lam_in"], 64)
            c.inc(dve.tensor_tensor(LAMV[:, 0, :], LAMV[:, 0, :], LAMV[:, 1, :], ALU.mult))
            c.inc(dve.tensor_tensor(LAMV[:, 2, :], LAMV[:, 2, :], LAMV[:, 3, :], ALU.mult))
            c.wait()
            dve.tensor_reduce(lam[:, 0:1], LAMV[:, 0, :], AX.X, ALU.add).then_inc(sem["lam_sum"], 1)
            dve.tensor_reduce(lam[:, 1:2], LAMV[:, 2, :], AX.X, ALU.add).then_inc(sem["lam_sum"], 1)
            dve.wait_ge(sem["lam_exp"], 1)
            c.inc(dve.tensor_tensor(lam[:, 0:1], lam[:, 3:4], lam[:, 2:3], ALU.subtract))
            c.wait()
            dve.tensor_scalar(lam[:, 0:1], lam[:, 0:1], -LAM_INIT, None, ALU.add).then_inc(sem["lam_ready"], 1)
            dve.wait_ge(sem["inv_mm"], 3 * HG)
            for _, k0, k1 in QK:
                dve.memset(k0, 0.0).then_inc(sem["k_zero"], 1)
                dve.memset(k1, 0.0).then_inc(sem["k_zero"], 1)
            dve.wait_ge(sem["k_zero"], 4)
            dve.wait_ge(sem["lam_ready"], 1)
            dve.wait_ge(sem["rope_in"], 32)

            def rotate(h, j):
                q, k0, k1 = QK[h % 2]
                dve.wait_ge(sem["pm_mm"], 5 * h + j + 1)
                for n, (part, chunk) in enumerate(TURN_JOBS[j]):
                    if h or j or n:
                        dve.wait_ge(sem["q_roped"], roped(h, j)[0] + n)
                        if h or j > 1 or n:
                            dve.wait_ge(sem["k_roped"], roped(h, j)[1])
                    c0, cn = CHUNKS[chunk]
                    cols, o = slice(c0, c0 + cn), c0 % LP
                    raw = QKRAW[part][:, cols]
                    step.inc(dve.tensor_tensor(RT[:, cols], PS[:, job_bank(h, j), n * cn:(n + 1) * cn], SIN[:, o:o + cn], ALU.mult))
                    step.inc(dve.tensor_tensor(raw, raw, COS[:, o:o + cn], ALU.mult))
                    step.wait()
                    if part == 0:
                        dve.tensor_tensor(q[:, cols], raw, RT[:, cols], ALU.add).then_inc(sem["q_roped"], 1)
                    else:
                        dve.tensor_tensor(k0[0:DH, cols], raw[0:DH, :], RT[0:DH, cols], ALU.add).then_inc(sem["k_roped"], 1)
                        dve.tensor_tensor(k1[DH:P, cols], raw[DH:P, :], RT[DH:P, cols], ALU.add).then_inc(sem["k_roped"], 1)

            def maxima(u):
                kn = keys(query_tile(u))[1]
                for c in range(2):
                    dve.wait_ge(sem["s_mm"], 2 * u + c + 1)
                    s = PS[:, 2 * c:2 * c + 2, :].rearrange("p b n -> p (b n)")[:, 0:kn]
                    step.inc(dve.tensor_reduce(att[:, u % 2, 0, c:c + 1], s, AX.X, ALU.max))
                    step.wait()
                    dve.tensor_scalar(att[:, u % 2, 1, c:c + 1], att[:, u % 2, 0, c:c + 1], -(DH ** -0.5), None,
                                      ALU.mult).then_inc(sem["smax_ready"], 1)

            def output(u):
                h, i = u // NT, query_tile(u)
                dve.wait_ge(sem["pv_mm"], u + 1)
                dve.tensor_scalar(AO[:, i, tiles[h]], PS[:, 6, (u % 4) * P:(u % 4 + 1) * P], att[:, u % 2, 3, 0:1], None,
                                  ALU.mult).then_inc(sem["o_ready"], 1)

            def mixed(u):
                kn = keys(query_tile(u))[1]
                dve.wait_ge(sem["exp_ready"], 2 * u + 2)
                if u >= 2:
                    dve.wait_ge(sem["o_ready"], u - 1)
                r = att[:, u % 2, :, :]
                step.inc(dve.reciprocal(r[:, 3, 0:2], r[:, 2, 0:2]))
                step.wait()
                step.inc(dve.tensor_scalar(r[:, 3, 2:3], r[:, 2, 0:1], r[:, 3, 1:2], lam[:, 0:1], ALU.mult, ALU.mult))
                step.wait()
                dve.scalar_tensor_tensor(PP[u % 2][0][:, 0:kn], PP[u % 2][1][:, 0:kn], r[:, 3, 2:3], PP[u % 2][0][:, 0:kn],
                                         ALU.mult, ALU.add).then_inc(sem["w_ready"], 1)

            for j in range(5):
                rotate(0, j)
            for u in range(UNITS):
                maxima(u)
                if u >= 2:
                    output(u - 2)
                h, i = (u - 1) // NT + 1, (u - 1) % NT
                if u >= 1 and h < HEADS and i >= 5:
                    rotate(h, i - 5)
                mixed(u)
            output(UNITS - 2)
            output(UNITS - 1)
            dve.wait_ge(sem["o_ready"], UNITS)

            c = step
            heads = AO.rearrange("p t (h v) -> p (t h) v", h=HEADS)
            c.inc(dve.tensor_tensor(SQ, AO, AO, ALU.mult))
            c.wait()
            dve.tensor_reduce(sub[:, 0, :], SQ.rearrange("p t (h v) -> p (t h) v", h=HEADS), AX.X, ALU.add).then_inc(sem["sub_sum"], 1)
            dve.wait_ge(sem["sub_root"], 1)
            c.inc(dve.reciprocal(sub[:, 2, :], sub[:, 1, :]))
            c.wait()
            dve.tensor_tensor(heads, heads, wide(sub[:, 2, :], DV), ALU.mult).then_inc(sem["sub_ready"], 1)
            for q in range(3 * HEADS):
                h, n = q // 3, q % 3
                c0, cn = CHUNKS[n]
                dve.wait_ge(sem["sub_tr"], q + 1)
                dve.tensor_scalar(AT[:, h, c0:c0 + cn], PS[:, SUB_BANKS[q % 4], 0:cn], vec[:, V_SUB:V_SUB + 1], 1.0 - LAM_INIT,
                                  ALU.mult, ALU.mult).then_inc(sem["at_ready"], 1)

            mg = step

            def merged(B, b):
                for n, (c0, cn) in enumerate(CHUNKS):
                    s = (b + n) % 2
                    dve.wait_ge(sem["mg_sig"], B * 6 + (2 * n + 2))
                    for part in range(2):
                        mg.inc(dve.tensor_tensor(TM[:, s, part, 0:cn], SG[:, s, part, 0:cn], PS[:, 4 * s + 2 + part, 0:cn], ALU.mult))
                    mg.wait()
                    dve.tensor_tensor(MT[:, bass.ds(B, 1), c0:c0 + cn].rearrange("p a n -> p (a n)"), TM[:, s, 0, 0:cn], TM[:, s, 1, 0:cn],
                                      ALU.add).then_inc(sem["m_ready"], 1)

            merged(0, 0)
            merged(1, 1)
            with dve.Fori(1, KD // 2) as cc:
                mg.enter(cc, 12)
                for b in range(2):
                    merged(cc * 2 + b, b)
            mg.leave(KD // 2 - 1)

            norm_stage(N_MEM, 4, lambda m: MS[:, m, :], MEMT, V_MEM)
            dve.wait_ge(sem["xr_in"], 32)
            for q in range(2 * NT):
                t, n = q // 2, q % 2
                dve.wait_ge(sem["wo_mm"], q + 1)
                dst = X[:, t, n * 512:(n + 1) * 512]
                dve.tensor_tensor(dst, PS[:, q % 6, :], dst, ALU.add).then_inc(sem["x1_ready"], 1)
                if n:
                    scaled(N_X + t, X[:, t, :], False)
                    rows_in(N_X + t, U2T, t, V_X)

            def keys_out(B, b):
                dve.wait_ge(sem["xb_mm"], B * 4 + 4)
                dve.tensor_copy(KX[:, bass.ds(B, 1), :].rearrange("p a n -> p (a n)"), PS[:, 4 * b + 3, :]).then_inc(sem["xk_ready"], 1)

            keys_out(0, 0)
            keys_out(1, 1)
            with dve.Fori(1, KD // 2) as cc:
                for b in range(2):
                    keys_out(cc * 2 + b, b)
            for q in range(8):
                m, n = q % 4, q // 4
                dve.wait_ge(sem["vm_mm"], q + 1)
                dve.tensor_copy(VM[:, m, n * 512:(n + 1) * 512], PS[:, q % 4, :]).then_inc(sem["vm_ready"], 1)

            xmax = xp = step

            def cross_out(i):
                for half in range(2):
                    dve.wait_ge(sem["xo_mm"], 2 * i + half + 1)
                    dve.tensor_copy(OT[:, 4 * half:4 * half + 4, tiles[XORDER[i]]], bank4(6 + half)).then_inc(sem["ot_ready"], 1)

            for i in range(NT):
                r = att[:, i % 2, :, :]
                dve.wait_ge(sem["xs_mm"], i + 1)
                if i >= 1:
                    dve.wait_ge(sem["xp_ready"], i)
                s = PS[:, 2 * (i % 2):2 * (i % 2) + 2, :].rearrange("p b (h m) -> p (b h) m", h=2)
                xmax.inc(dve.tensor_reduce(r[:, 0, :], s, AX.X, ALU.max))
                xmax.wait()
                dve.tensor_scalar(r[:, 1, :], r[:, 0, :], -(XD ** -0.5), None, ALU.mult).then_inc(sem["xmax_ready"], 1)
                dve.wait_ge(sem["xexp_ready"], 4 * i + 4)
                xp.inc(dve.reciprocal(r[:, 3, :], r[:, 2, :]))
                xp.wait()
                dve.tensor_tensor(XP[i % 2], XP[i % 2], wide(r[:, 3, :], NMEM), ALU.mult).then_inc(sem["xp_ready"], 1)
                if i >= 2:
                    cross_out(i - 2)
            cross_out(NT - 2)
            cross_out(NT - 1)

            def second_residual(q):
                t, n = XO_JOBS[q]
                dve.wait_ge(sem["xo2_mm"], q + 1)
                dst = X[:, t, n * 512:(n + 1) * 512]
                dve.tensor_tensor(dst, PS[:, xo_bank(q), :], dst, ALU.add).then_inc(sem["x2_ready"], 1)

            def normed_tile(t):
                scaled(N_FFN + t, X[:, t, :], True)
                rows_in(N_FFN + t, HT, t, V_FFN)

            c = step

            def affinities(turn_no, t0, n, bank, into):
                dve.wait_ge(sem["rt_mm"], t0 + n)
                logits = PS[:, 4, t0 * NE:(t0 + n) * NE].rearrange("p (t e) -> p t e", e=NE)
                lg = LG[:, t0:t0 + n, :]
                c.inc(dve.tensor_reduce(RM[:, 0, t0:t0 + n], logits, AX.X, ALU.max))
                c.wait()
                dve.tensor_tensor(lg, logits, wide(RM[:, 0, t0:t0 + n], NE), ALU.subtract).then_inc(sem["rt_low"], 1)
                dve.wait_ge(sem["rt_exp"], turn_no)
                c.inc(dve.tensor_reduce(RM[:, 1, t0:t0 + n], lg, AX.X, ALU.add))
                c.wait()
                c.inc(dve.reciprocal(RM[:, 0, t0:t0 + n], RM[:, 1, t0:t0 + n]))
                c.wait()
                dve.tensor_tensor(lg, lg, wide(RM[:, 0, t0:t0 + n], NE), ALU.mult).then_inc(sem["aff_ready"], 1)
                dve.wait_ge(sem["aff_tr"], turn_no)
                c.inc(dve.tensor_copy(into, PS[0:into.shape[0], bank, 0:into.shape[1]]))

            def largest(tok, val, idx, r, rounds):
                v = val[:, 8 * r:8 * r + 8]
                c.wait()
                c.inc(dve.max(v, tok))
                c.wait()
                c.inc(dve.max_index(idx[:, 8 * r:8 * r + 8], v, tok))
                if r + 1 < rounds:
                    c.wait()
                    c.inc(dve.match_replace(tok, v, tok, -1.0))

            for q in range(XO_PROMPT):
                second_residual(q)
                if q + 1 in X2_AT:
                    normed_tile(X2_AT.index(q + 1))
            affinities(1, 0, NTP, 2, AFP)
            for r in range(CP // 8):
                largest(AFP, VALP, IDXP, r, CP // 8)
                if r in (3, 6, 9, 12):
                    second_residual(XO_PROMPT + r // 3 - 1)
                if r in (7, 13):
                    t = NTP + r // 13
                    scaled(N_FFN + t, X[:, t, :], True)
                if r in (10, 15):
                    t = NTP + r // 15
                    rows_in(N_FFN + t, HT, t, V_FFN)
            c.wait()
            dve.tensor_copy(SLOT_P, IDXP).then_inc(sem["slots_ready"], 1)
            dve.wait_ge(sem["slots_tr"], 1)
            dve.tensor_copy(SORTED.rearrange("p k h -> p (k h)"), PS[:, 3, 0:4 * NE]).then_inc(sem["sorted_ready"], 1)
            affinities(2, NTP, NTS, 5, AFS)
            dve.wait_ge(sem["reversed"], 1)
            dve.wait_ge(sem["sorted_ready"], 1)
            back = PS[:, 2, 0:4 * NE].rearrange("p (k h) -> p k h", k=2)
            c.inc(dve.tensor_tensor(FIRST[:, 0, :], SORTED[:, 1, 0:NE], back[:, 1, NE:2 * NE], ALU.is_ge))
            c.inc(dve.tensor_scalar(FIRST[:, 1, :], back[:, 0, NE:2 * NE], float(LP // 2), None, ALU.add))
            dve.tensor_tensor(gates[:, 0, :], SORTED[:, 1, 0:NE], back[:, 1, NE:2 * NE], ALU.max).then_inc(sem["idx_ready"], 1)
            c.wait()
            c.inc(dve.tensor_tensor(FIRST[:, 2, :], SORTED[:, 0, 0:NE], FIRST[:, 1, :], ALU.subtract))
            c.wait()
            c.inc(dve.tensor_tensor(FIRST[:, 2, :], FIRST[:, 2, :], FIRST[:, 0, :], ALU.mult))
            c.wait()
            dve.tensor_tensor(idx_p[:, :], FIRST[:, 2, :], FIRST[:, 1, :], ALU.add).then_inc(sem["idx_ready"], 1)
            for r in range(CS // 8):
                largest(AFS, VALS, IDXS, r, CS // 8)
            c.wait()
            c.inc(dve.tensor_copy(SLOT_I[:, 0:CS], IDXS))
            c.wait()
            c.inc(dve.tensor_scalar(SLOT_I[:, 0:CS], SLOT_I[:, 0:CS], float(LP), None, ALU.add))
            c.wait()
            for j in range(4):
                o = CS * (j + 1)
                c.inc(dve.tensor_scalar(SLOT_I[:, o:o + CS], SLOT_I[:, 0:CS], 4.0, float(j), ALU.mult, ALU.add))
                c.inc(dve.tensor_copy(SLOT_V[:, o:o + CS], VALS))
            c.wait()
            dve.memset(RM[:, 0, 0:1], 0.0).then_inc(sem["slots_ready"], 1)
            dve.wait_ge(sem["idx_tr"], 1)
            dve.tensor_copy(idx_s[:, :], PS[0:CS, 4, 0:NE]).then_inc(sem["idx_ready"], 1)
            dve.tensor_copy(idx_q[:, :], PS[:, 4, NE:2 * NE]).then_inc(sem["idx_ready"], 1)
            dve.tensor_copy(gates[:, 1, :], PS[:, 4, 2 * NE:3 * NE]).then_inc(sem["idx_ready"], 1)
            dve.wait_ge(sem["idx_ready"], 5)

            def slots_in(e):
                dve.wait_ge(sem["xe_tr"], e * 3 + 3)
                for half in range(2):
                    g = vec[:, V_FFN + 4 * half:V_FFN + 4 * half + 4]
                    dve.tensor_tensor(XET[:, 4 * half:4 * half + 4, 0:CP], bank4(3 + half), wide(g, P), ALU.mult).then_inc(sem["xet_ready"], 1)
                dve.tensor_tensor(XET[:, :, CP:CE], PS[:, 5, 0:KD * CS].rearrange("p (k s) -> p k s", k=KD),
                                  wide(vec[:, V_FFN:V_FFN + KD], CS), ALU.mult).then_inc(sem["xet_ready"], 1)

            def hidden(e):
                for f in range(FF // P):
                    dve.wait_ge(sem["silu_ready"], e * 8 + (f + 1))
                    dve.tensor_tensor(HE[:, f, :], SL[:, f % 2, :], PS[:, f % 3, CE:2 * CE], ALU.mult).then_inc(sem["he_ready"], 1)

            def results(e, first):
                if not first:
                    dve.wait_ge(sem["scatter_p"], e * 16)
                    dve.wait_ge(sem["scatter_s"], e * 16)
                for n in range(2):
                    dve.wait_ge(sem["dn_mm"], e * 3 + (n + 1))
                    dve.tensor_scalar(YP[:, n * 512:(n + 1) * 512], PS[:, 6 + n, :], gates[:, 0, bass.ds(e, 1)], None,
                                      ALU.mult).then_inc(sem["y_out"], 1)
                dve.wait_ge(sem["dn_mm"], e * 3 + 3)
                dve.tensor_scalar(YS, PS[:, 5, 0:256], gates[:, 1, bass.ds(e, 1)], None, ALU.mult).then_inc(sem["y_out"], 1)

            slots_in(0)
            hidden(0)
            slots_in(1)
            results(0, True)
            with dve.Fori(1, NE - 1) as e:
                hidden(e)
                slots_in(e + 1)
                results(e, False)
            hidden(NE - 1)
            results(NE - 1, False)
            dve.wait_ge(sem["gain_in"], 16)
            for t in range(NT):
                dve.wait_ge(sem["fin_act"], 2 * t + 2)
                dve.reciprocal(stat[:, 2, t:t + 1], stat[:, 1, t:t + 1]).then_inc(sem["fin_rec"], 1)
                dve.wait_ge(sem["fin_rec"], t + 1)
                dve.scalar_tensor_tensor(FIN[t], FIN[t], stat[:, 2, t:t + 1], GROW, ALU.mult, ALU.mult).then_inc(sem["fin_ready"], 1)


_INS = ["x_prompt", "x_sample", "mem_prompt", "mem_sample", "norm_mix", "w_in", "lambda_q1", "lambda_k1",
        "lambda_q2", "lambda_k2", "subln", "w_br_attn", "hy_conv_w", "hy_conv_b", "filt_w1", "filt_b1",
        "filt_w2", "filt_b2", "filt_w3", "filt_freq", "filt_bias", "w_br_hyena", "w_out", "norm_x", "norm_mem",
        "w_xq", "w_xkv", "w_xo", "norm_ffn", "w_router", "w_exp_gate", "w_exp_up", "w_exp_down", "norm_final"]
_OUTS = [(1, LP, D), (1, LS, D)]


def build(nc, arrays):
    a = {n: nc.dram_tensor(f"in_{n}", v.shape, F32, kind="ExternalInput").ap() for n, v in arrays.items()}
    outs = [nc.dram_tensor(f"out_{i}", s, F32, kind="ExternalOutput").ap() for i, s in enumerate(_OUTS)]
    encoder_kernel(nc, a, *outs)


def kernel(**inputs):
    import concourse.bacc as bacc
    from concourse.bass_utils import run_bass_kernel_spmd

    arrays = {n: np.ascontiguousarray(inputs[n]) for n in _INS} | shape_tables()
    nc = bacc.Bacc("TRN2", target_bir_lowering=False, num_devices=1)
    build(nc, arrays)
    r = run_bass_kernel_spmd(nc, [{f"in_{n}": v for n, v in arrays.items()}], core_ids=[0])
    return tuple(r.results[0][f"out_{i}"] for i in range(len(_OUTS)))
```
